# Optimizing a Trainium2 kernel written in Bass

```python
import math
import jax, jax.numpy as jnp
from jax import lax
import numpy as np

D_MODEL = 1024
BATCH = 1
SEQ = 512
DEPTH = 1

MEM_LEN = 256
EPS = 1e-6
HY_WIDTH = 768
HY_ORDER = 2
HY_SHORT = 3
HY_EMB = 33
HY_BANDS = (HY_EMB - 1) // 2
HY_FFN = 64
HY_FAST_PCT = 0.3
HY_SLOW_PCT = 1.5
HY_TARGET = 1e-2
FILTER_SCALE = 0.03
HEAD_DIM = 64
HEADS_PER_GROUP = 4
DIL_PAIRS = ((128, 1), (512, 4), (2048, 16))
N_GROUPS = len(DIL_PAIRS)
ATTN_HEADS = N_GROUPS * HEADS_PER_GROUP
ATTN_WIDTH = ATTN_HEADS * HEAD_DIM
ATTN_OUT = HEADS_PER_GROUP * HEAD_DIM
ROPE_THETA = 10000.0
IN_COLS = 3 * HY_WIDTH + 3 * ATTN_WIDTH
X_HEADS = 4
X_HEAD_DIM = 128
N_EXPERTS = 16
EC_FACTOR = 2
EXPERT_FF = 2048

kernel_name = "hybrid_hyena_dilated_attn_ec_moe_encoder"

def rmsnorm(x, g):
    xf = x.astype(jnp.float32)
    y = xf * lax.rsqrt(jnp.mean(xf * xf, axis=-1, keepdims=True) + EPS)
    return (y * g.astype(jnp.float32)).astype(x.dtype)

def rope(x, pos):
    dh = x.shape[-1]
    inv = ROPE_THETA ** (-jnp.arange(0, dh, 2, dtype=jnp.float32) / dh)
    ang = pos.astype(jnp.float32)[:, None] * inv[None, :]
    cos = jnp.cos(ang)[None, :, None, :]
    sin = jnp.sin(ang)[None, :, None, :]
    xf = x.astype(jnp.float32)
    x1, x2 = xf[..., : dh // 2], xf[..., dh // 2:]
    return jnp.concatenate([x1 * cos - x2 * sin, x2 * cos + x1 * sin], axis=-1).astype(x.dtype)

def short_conv_centred(u, w, b):
    up = jnp.pad(u, ((0, 0), (1, 1), (0, 0)))
    return up[:, :-2] * w[0] + up[:, 1:-1] * w[1] + up[:, 2:] * w[2] + b

def hyena_filters(L, w1, b1, f1, w2, b2, f2, w3):
    f32 = jnp.float32
    t = jnp.linspace(0.0, 1.0, L, dtype=f32)[:, None]
    grid = 2.0 * math.pi * jnp.arange(L, dtype=f32)[:, None] / L
    bands = jnp.linspace(1e-4, HY_BANDS - 1, HY_BANDS, dtype=f32)[None, :]
    emb = jnp.concatenate([t, jnp.cos(bands * grid), -jnp.sin(bands * grid)], axis=-1)
    h = jnp.sin(f1.astype(f32) * (emb @ w1.astype(f32) + b1.astype(f32)))
    h = jnp.sin(f2.astype(f32) * (h @ w2.astype(f32) + b2.astype(f32)))
    h = h @ w3.astype(f32)
    max_decay = math.log(HY_TARGET) / HY_FAST_PCT
    min_decay = math.log(HY_TARGET) / HY_SLOW_PCT
    deltas = jnp.linspace(min_decay, max_decay, HY_WIDTH, dtype=f32)
    decay = jnp.exp(-t * jnp.abs(deltas)[None, :])
    return h.reshape(L, HY_ORDER, 2, HY_WIDTH) * decay[:, None, None, :]

def bidir_fftconv(z, h_fwd, h_bwd, skip):
    L = z.shape[1]
    k = jnp.concatenate([h_fwd, jnp.zeros_like(h_fwd[:1]), h_bwd[:0:-1]], axis=0)
    zf = z.astype(jnp.float32)
    Z = jnp.fft.rfft(zf, n=2 * L, axis=1)
    K = jnp.fft.rfft(k, n=2 * L, axis=0)
    y = jnp.fft.irfft(Z * K[None], n=2 * L, axis=1)[:, :L]
    return (y + zf * skip.astype(jnp.float32)).astype(z.dtype)

def dilated_band_attention(q, k, v, dilation, n_side):
    B, S, H, dh = q.shape
    Lr = S // dilation
    blk = n_side
    nb = -(-Lr // blk)
    Lp = nb * blk

    def to_res(t):
        t = t.reshape(B, Lr, dilation, H, dh).transpose(0, 2, 3, 1, 4)
        return jnp.pad(t, ((0, 0), (0, 0), (0, 0), (0, Lp - Lr), (0, 0)))

    def windows(t):
        tp = jnp.pad(t, ((0, 0), (0, 0), (0, 0), (blk, blk), (0, 0))).reshape(B, dilation, H, nb + 2, blk, dh)
        return jnp.concatenate([tp[:, :, :, :-2], tp[:, :, :, 1:-1], tp[:, :, :, 2:]], axis=4)

    qb = to_res(q).reshape(B, dilation, H, nb, blk, dh)
    kw = windows(to_res(k))
    vw = windows(to_res(v))
    qi = jnp.arange(nb)[:, None] * blk + jnp.arange(blk)[None, :]
    ki = (jnp.arange(nb)[:, None] - 1) * blk + jnp.arange(3 * blk)[None, :]
    rel = ki[:, None, :] - qi[:, :, None]
    valid = (jnp.abs(rel) <= n_side) & (ki[:, None, :] >= 0) & (ki[:, None, :] < Lr)
    s = jnp.einsum('bdhnqc,bdhnkc->bdhnqk', qb, kw, preferred_element_type=jnp.float32) * (dh ** -0.5)
    s = jnp.where(valid, s, -1e30)
    lse = jax.nn.logsumexp(s, axis=-1, keepdims=True)
    p = jnp.exp(s - lse).astype(v.dtype)
    o = jnp.einsum('bdhnqk,bdhnkc->bdhnqc', p, vw)
    o = o.reshape(B, dilation, H, Lp, dh)[:, :, :, :Lr].transpose(0, 3, 1, 2, 4).reshape(B, S, H, dh)
    lse = lse[..., 0].reshape(B, dilation, H, Lp)[..., :Lr].transpose(0, 3, 1, 2).reshape(B, S, H)
    return o, lse

def setup_inputs(seed: int = 0) -> dict:
    key = jax.random.key(seed)
    ks = jax.random.split(key, 36)
    f32 = jnp.float32
    D, W, F, E = D_MODEL, HY_WIDTH, EXPERT_FF, N_EXPERTS

    def nrm(k, shape, scale):
        return jax.random.normal(k, shape, f32) * scale

    return {
        "x": nrm(ks[0], (BATCH, SEQ, D), 1.0),
        "mem": nrm(ks[1], (BATCH, MEM_LEN, D), 1.0),
        "ln_mix_g": 1.0 + nrm(ks[2], (D,), 0.01),
        "w_in": nrm(ks[3], (D, IN_COLS), D ** -0.5),
        "hy_conv_w": nrm(ks[4], (HY_SHORT, 3 * W), HY_SHORT ** -0.5),
        "hy_conv_b": nrm(ks[5], (3 * W,), 0.02),
        "filt_w1": nrm(ks[6], (HY_EMB, HY_FFN), HY_EMB ** -0.5),
        "filt_b1": nrm(ks[7], (HY_FFN,), 0.02),
        "filt_freq1": 1.0 + nrm(ks[8], (HY_FFN,), 0.01),
        "filt_w2": nrm(ks[9], (HY_FFN, HY_FFN), HY_FFN ** -0.5),
        "filt_b2": nrm(ks[10], (HY_FFN,), 0.02),
        "filt_freq2": 1.0 + nrm(ks[11], (HY_FFN,), 0.01),
        "filt_w3": nrm(ks[12], (HY_FFN, 2 * HY_ORDER * W), FILTER_SCALE * HY_FFN ** -0.5),
        "hy_skip": nrm(ks[13], (HY_ORDER, W), 1.0),
        "w_up_hy": nrm(ks[14], (W, D), W ** -0.5),
        "w_up_attn": nrm(ks[15], (ATTN_OUT, D), ATTN_OUT ** -0.5),
        "w_gate": nrm(ks[16], (D, 2 * D), D ** -0.5),
        "b_gate": nrm(ks[17], (2 * D,), 0.01),
        "w_out": nrm(ks[18], (D, D), D ** -0.5),
        "ln_x_g": 1.0 + nrm(ks[19], (D,), 0.01),
        "ln_mem_g": 1.0 + nrm(ks[20], (D,), 0.01),
        "w_q_x": nrm(ks[21], (D, X_HEADS * X_HEAD_DIM), D ** -0.5),
        "w_kv_mem": nrm(ks[22], (D, 2 * X_HEADS * X_HEAD_DIM), D ** -0.5),
        "w_o_x": nrm(ks[23], (X_HEADS * X_HEAD_DIM, D), (X_HEADS * X_HEAD_DIM) ** -0.5),
        "ln_moe_g": 1.0 + nrm(ks[24], (D,), 0.01),
        "w_router": nrm(ks[25], (D, E), D ** -0.5),
        "w_e_gate": nrm(ks[26], (E, D, F), D ** -0.5),
        "w_e_up": nrm(ks[27], (E, D, F), D ** -0.5),
        "w_e_down": nrm(ks[28], (E, F, D), F ** -0.5),
        "ln_f_g": 1.0 + nrm(ks[29], (D,), 0.01),
    }

def reference(x, mem, ln_mix_g, w_in, hy_conv_w, hy_conv_b, filt_w1, filt_b1, filt_freq1,
              filt_w2, filt_b2, filt_freq2, filt_w3, hy_skip, w_up_hy, w_up_attn, w_gate, b_gate,
              w_out, ln_x_g, ln_mem_g, w_q_x, w_kv_mem, w_o_x, ln_moe_g, w_router, w_e_gate,
              w_e_up, w_e_down, ln_f_g):
    B, S, D = x.shape
    M = mem.shape[1]
    W = HY_WIDTH
    pos = jnp.arange(S)
    for _ in range(DEPTH):
        h = rmsnorm(x, ln_mix_g)
        proj = h @ w_in
        p_hy = proj[..., : 3 * W]
        p_q, p_k, p_v = jnp.split(proj[..., 3 * W:], 3, axis=-1)

        u = short_conv_centred(p_hy, hy_conv_w, hy_conv_b)
        z, g1, g2 = jnp.split(u, 3, axis=-1)
        filt = hyena_filters(S, filt_w1, filt_b1, filt_freq1, filt_w2, filt_b2, filt_freq2, filt_w3)
        for o, gate in enumerate((g1, g2)):
            z = gate * bidir_fftconv(z, filt[:, o, 0], filt[:, o, 1], hy_skip[o])
        y_hy = z @ w_up_hy

        q = rope(p_q.reshape(B, S, ATTN_HEADS, HEAD_DIM), pos).reshape(B, S, N_GROUPS, HEADS_PER_GROUP, HEAD_DIM)
        k = rope(p_k.reshape(B, S, ATTN_HEADS, HEAD_DIM), pos).reshape(B, S, N_GROUPS, HEADS_PER_GROUP, HEAD_DIM)
        v = p_v.reshape(B, S, N_GROUPS, HEADS_PER_GROUP, HEAD_DIM)
        outs, lses = [], []
        for g, (window, dil) in enumerate(DIL_PAIRS):
            o_g, l_g = dilated_band_attention(q[:, :, g], k[:, :, g], v[:, :, g], dil, window // (2 * dil))
            outs.append(o_g)
            lses.append(l_g)
        wts = jax.nn.softmax(jnp.stack(lses, axis=0), axis=0).astype(x.dtype)
        attn = jnp.einsum('gbsh,gbshc->bshc', wts, jnp.stack(outs, axis=0)).reshape(B, S, ATTN_OUT)
        y_at = attn @ w_up_attn

        gates = jax.nn.sigmoid((h @ w_gate + b_gate).astype(jnp.float32)).astype(x.dtype)
        g_hy, g_at = jnp.split(gates, 2, axis=-1)
        x = x + (g_hy * y_hy + g_at * y_at) @ w_out

        hx = rmsnorm(x, ln_x_g)
        mn = rmsnorm(mem, ln_mem_g)
        qx = (hx @ w_q_x).reshape(B, S, X_HEADS, X_HEAD_DIM)
        kx, vx = jnp.split((mn @ w_kv_mem).reshape(B, M, 2 * X_HEADS, X_HEAD_DIM), 2, axis=2)
        sx = jnp.einsum('bqhc,bkhc->bhqk', qx, kx, preferred_element_type=jnp.float32) * (X_HEAD_DIM ** -0.5)
        px = jax.nn.softmax(sx, axis=-1).astype(x.dtype)
        ox = jnp.einsum('bhqk,bkhc->bqhc', px, vx).reshape(B, S, X_HEADS * X_HEAD_DIM)
        x = x + ox @ w_o_x

        hm = rmsnorm(x, ln_moe_g)
        aff = jax.nn.softmax((hm @ w_router).astype(jnp.float32), axis=-1)
        cap = max(1, EC_FACTOR * S // N_EXPERTS)
        gate_v, idx = lax.top_k(aff.transpose(0, 2, 1), cap)
        flat = (jnp.arange(B)[:, None, None] * S + idx).reshape(-1)
        hflat = hm.reshape(B * S, D)
        xe = hflat[flat].reshape(B, N_EXPERTS, cap, D)
        a = jnp.einsum('becd,edf->becf', xe, w_e_gate)
        b_ = jnp.einsum('becd,edf->becf', xe, w_e_up)
        ye = jnp.einsum('becf,efd->becd', jax.nn.silu(a) * b_, w_e_down) * gate_v[..., None].astype(x.dtype)
        y_moe = jnp.zeros((B * S, D), x.dtype).at[flat].add(ye.reshape(-1, D))
        x = x + y_moe.reshape(B, S, D)
    return rmsnorm(x, ln_f_g)


_drawn_inputs = setup_inputs


def setup_inputs(seed=0):
    import zlib

    import numpy as np

    out = dict(_drawn_inputs(seed))
    spreads = {}
    factors = {'ln_mix_g': 4.685,
     'filt_b1': 8.0,
     'filt_freq1': 8.0,
     'filt_b2': 8.0,
     'filt_freq2': 8.0,
     'b_gate': 8.0,
     'ln_x_g': 33.165,
     'ln_mem_g': 40.266,
     'ln_moe_g': 37.68,
     'ln_f_g': 34.326,
     'hy_conv_b': 4.111}
    for name, (base, spread) in spreads.items():
        noise = np.random.default_rng([zlib.crc32(name.encode()), seed]).standard_normal(out[name].shape)
        drawn = base * np.exp(spread * noise) if base else spread * noise
        out[name] = __import__('jax').numpy.asarray(drawn.astype(out[name].dtype))
    for name, factor in factors.items():
        out[name] = (out[name] * factor).astype(out[name].dtype)
    return out
```

```python
from contextlib import ExitStack

import concourse.bass as bass
from concourse import mybir

F32 = mybir.dt.float32
U32 = mybir.dt.uint32
ALU = mybir.AluOpType
ACT = mybir.ActivationFunctionType
AX = mybir.AxisListType

P = 128
SEQ = 512
NT = SEQ // P
D = 1024
KD = D // P
MEM = 256
MT = MEM // P
EPS = 1e-6
HW = 768
HC = HW // P
HYT = 3 * HC
FFN = 64
EMB = 33
SLOTS_PER_HEAD = 4
GROUPS = 3
AW = GROUPS * SLOTS_PER_HEAD * 64
NKEY = SEQ + P + P
XH = 4
NE = 16
CAP = 2 * SEQ // NE
FF = 2048
CW = 256
RING = 8
CH = 256
NU = HW // CH
FB = FF // CW
TWO_PI = 6.283185307179586
MAGIC = 12582912.0
PI_A, PI_B = 6.28125, 0.0019350051879882812
PI_C = TWO_PI - PI_A - PI_B

V_MIX, V_X, V_MEM, V_MOE, V_BG, V_CB, V_SKIP = 0, 8, 16, 24, 32, 48, 66
V_ROWS = 78
V_CW = 78
V_COLS = V_CW + 54


def encoder_block(nc, x, mem, ln_mix_g, w_in, hy_conv_w, hy_conv_b, filt_w1, filt_b1, filt_freq1,
                  filt_w2, filt_b2, filt_freq2, filt_w3, hy_skip, w_up_hy, w_up_attn, w_gate, b_gate,
                  w_out, ln_x_g, ln_mem_g, w_q_x, w_kv_mem, w_o_x, ln_moe_g, w_router, w_e_gate,
                  w_e_up, w_e_down, ln_f_g,
                  c_ident, c_embT, c_decay, c_dftc, c_dfts, c_dftsk, c_idftc, c_idfts,
                  c_rcos, c_rsin, c_mask, c_tval, c_iota, out):
    ctx = ExitStack()
    with ctx:
        def sb(name, shape, dt=F32):
            return ctx.enter_context(nc.sbuf_tensor(name, shape, dt))

        def sem(name):
            return ctx.enter_context(nc.semaphore(name))

        ring = sb("ring", [P, RING, 2048])
        xs = sb("xs", [P, NT, D])
        hT = sb("hT", [P, KD, SEQ])
        UT = sb("UT", [P, 9216])
        W = sb("W", [P, 16896])
        attnT = sb("attnT", [P, 2, SEQ])
        ident = sb("ident", [P, P])
        vrow = W[:, 16384:16640].rearrange("p (a d) -> p a d", a=2)
        vcol = sb("vcol", [P, V_COLS])
        st = sb("st", [P, 64])
        fcol = sb("fcol", [FFN, 4])
        h2T = sb("h2T", [FFN, SEQ])

        uT = UT[:, :].rearrange("p (m t) -> p m t", t=SEQ)
        embT = UT[0:EMB, 0:512]
        fw1 = UT[0:EMB, 512:576]
        fw2 = UT[0:FFN, 576:640]
        farg = UT[0:FFN, 1024:1536]
        fk = UT[0:FFN, 1536:2048]
        h1T = UT[0:FFN, 2048:2560]

        hn = W[:, 0:4096].rearrange("p (a d) -> p a d", a=NT)
        vnat = W[:, 0:3072].rearrange("p (a c) -> p a c", a=NT)
        qT = W[:, 3072:6144].rearrange("p (g r t) -> p g r t", g=GROUPS, r=2)
        kT = W[:, 6144:9216].rearrange("p (g r t) -> p g r t", g=GROUPS, r=2)
        masks = W[:, 9216:12288].rearrange("p (a k) -> p a k", a=NT)
        Sb = W[:, 12288:13824].rearrange("p (b k) -> p b k", b=2)
        PTb = W[:, 13824:15360].rearrange("p (b k) -> p b k", b=2)
        anat = W[:, 15360:15872].rearrange("p (b k) -> p b k", b=2)
        rcos = W[:, 15872:16128].rearrange("p (a k) -> p a k", a=NT)
        rsin = W[:, 16128:16384].rearrange("p (a k) -> p a k", a=NT)
        ropeA = W[:, 12288:12544]
        ropeB = W[:, 12544:12800]
        rope_out = W[:, 12800:13312].rearrange("p (b k) -> p b k", b=2)
        dftc = W[:, 0:1024].rearrange("p (a f) -> p a f", a=NT)
        dfts = W[:, 1024:2048].rearrange("p (a f) -> p a f", a=NT)
        idftc = W[:, 2048:3072].rearrange("p (j t) -> p j t", j=2)
        idfts = W[:, 3072:4096].rearrange("p (j t) -> p j t", j=2)
        dftsk = W[:, 4096:4352].rearrange("p (a f) -> p a f", a=2)
        Kb = [[W[:, 4352 + 2048 * b + 512 * i:4864 + 2048 * b + 512 * i].rearrange("p (j c) -> p j c", j=2)
               for i in range(4)] for b in range(2)]
        Zb = [W[:, 8448 + 512 * i:8960 + 512 * i].rearrange("p (j c) -> p j c", j=2) for i in range(4)]
        ff = W[:, 10496:11520].rearrange("p (a c) -> p a c", a=NT)
        fb = W[:, 11520:12544].rearrange("p (a c) -> p a c", a=NT)
        fs = W[:, 12544:13568].rearrange("p (a c) -> p a c", a=NT)
        znat = W[:, 13568:14592].rearrange("p (a c) -> p a c", a=NT)
        t1 = W[:, 13568:14080].rearrange("p (j c) -> p j c", j=2)
        t2 = W[:, 14080:14592].rearrange("p (j c) -> p j c", j=2)
        t3 = W[:, 14592:15104].rearrange("p (j c) -> p j c", j=2)
        dec = W[:, 15104:16128].rearrange("p (a c) -> p a c", a=NT)
        w3u = W[0:FFN, 16128:16640].rearrange("p (d c) -> p d c", d=2)
        ZP = Zb
        EV = lambda B: (B[2], B[1])
        mixT = W[:, 0:4096].rearrange("p (m t) -> p m t", m=KD)
        gs = W[:, 4096:6144].rearrange("p (b s t) -> p b s t", b=2, s=2)
        mt = W[:, 6144:7168].rearrange("p (s t) -> p s t", s=2)
        mems = W[:, 7168:9216].rearrange("p (a d) -> p a d", a=MT)
        mnT = W[:, 9216:11264].rearrange("p (k t) -> p k t", k=KD)
        mhn = W[:, 11264:13312].rearrange("p (a d) -> p a d", a=MT)
        kxT = W[:, 13312:14336].rearrange("p (h t) -> p h t", h=XH)
        vx = W[:, 14336:15360].rearrange("p (b c) -> p b c", b=MT)
        qxT = UT[:, 0:2048].rearrange("p (h t) -> p h t", h=XH)
        oxT = UT[:, 2048:4096].rearrange("p (h t) -> p h t", h=XH)
        Px = UT[:, 4096:6144].rearrange("p (b a t) -> p b a t", b=2, a=NT)
        PTx = UT[:, 6144:8192].rearrange("p (b s t) -> p b s t", b=2, s=2)
        wua = UT[:, 3072:5120].rearrange("p (k c) -> p k c", k=2)
        hT_out = lambda a: hT[:, :, :].rearrange("p k t -> p (k t)")[:, a * D:(a + 1) * D]
        Psel = W[:, 4096:8192].rearrange("p (a s) -> p a s", a=NT)
        iota = W[:, 8192:8704]
        PTe = W[:, 8704:9216]
        xeT = W[:, 9216:9728].rearrange("p (k s) -> p k s", k=KD)
        sil = W[0:CAP, 9728:10240].rearrange("p (b f) -> p b f", b=2)
        hh = W[0:CAP, 10240:10752].rearrange("p (b f) -> p b f", b=2)
        hhT = W[:, 10752:11008].rearrange("p (b i s) -> p b i s", b=2, i=2)
        ye = W[:, 11008:11520]
        gf = W[:, 11520:12544]
        wr = sb("wr", [P, KD, NE])
        aff = W[:, 12544:12608].rearrange("p (a e) -> p a e", a=NT)
        lg = W[:, 12608:12672].rearrange("p (a e) -> p a e", a=NT)
        affT = W[0:NE, 12672:13184]
        topv = W[0:NE, 13184:13312].rearrange("p (r s) -> p r s", r=2)
        topi = W[0:NE, 13312:13376].bitcast(U32)
        topf = W[0:NE, 13376:13504].rearrange("p (r s) -> p r s", r=2)
        bdiag = W[0:NE, 13504:14528].rearrange("p (e s) -> p e s", e=NE)
        ones16 = W[0:NE, 14528:14656]
        gcol = W[:, 14656:14672]
        icol = W[:, 14672:14688]
        tval = W[:, 14688:14692]

        ps = ctx.enter_context(nc.psum_tensor("ps", [P, 8, 512], F32))

        def psc(b0, b1, n):
            return ps[:, b0:b1, :].rearrange("p b c -> p (b c)")[:, 0:n]

        ld_ident, ld_x, ld_vec, ld_filt, ld_rope, ld_mask = (sem(n) for n in (
            "ld_ident", "ld_x", "ld_vec", "ld_filt", "ld_rope", "ld_mask"))
        ld_dft, ld_dec, ld_w3, ld_mem, ld_wr, ld_moe, ld_gf, ld_wua = (sem(n) for n in (
            "ld_dft", "ld_dec", "ld_w3", "ld_mem", "ld_wr", "ld_moe", "ld_gf", "ld_wua"))
        slot_loaded = [sem(f"slot{i}_loaded") for i in range(RING)]
        vec_turned, vec_ready = sem("vec_turned"), sem("vec_ready")
        mlp_mm, mlp_arg, mlp_sin = sem("mlp_mm"), sem("mlp_arg"), sem("mlp_sin")
        chain = sem("dve_chain")
        pchain = sem("pool_chain")
        norms = {}
        for tag in ("mix", "mem", "xa", "moe", "fin"):
            norms[tag] = {n: sem(f"{tag}_{n}") for n in ("sq", "var", "sqrt", "scaled", "turned", "evA", "evV")}
        qkv_full, v_copied, roped, qk_turned, qk_copied = (sem(n) for n in (
            "qkv_full", "v_copied", "roped", "qk_turned", "qk_copied"))
        s_full, s_masked, s_negmax, s_exp, p_turned, p_copied, o_full, o_scaled, at_turned, at_copied = (sem(n) for n in (
            "s_full", "s_masked", "s_negmax", "s_exp", "p_turned", "p_copied", "o_full", "o_scaled",
            "at_turned", "at_copied"))
        hy_full, hy_centre, hy_conv = sem("hy_full"), sem("hy_centre"), sem("hy_conv")
        f_full, f_copied, f_sumdif, k_full, k_even, k_ready = (sem(n) for n in (
            "f_full", "f_copied", "f_sumdif", "k_full", "k_even", "k_ready"))
        z_turned, z_copied, z_full, z_even, z_ready, prod, y_full, z_new = (sem(n) for n in (
            "z_turned", "z_copied", "z_full", "z_even", "z_ready", "prod", "y_full", "z_new"))
        mix_full, mix_gate, mix_done = sem("mix_full"), sem("mix_gate"), sem("mix_done")
        out_full, out_added = sem("out_full"), sem("out_added")
        kv_full, kv_copied, qx_full, qx_copied = (sem(n) for n in ("kv_full", "kv_copied", "qx_full", "qx_copied"))
        sx_full, sx_negmax, sx_exp, sx_norm, px_turned, px_copied, ox_full, ox_copied, xo_full, xo_added = (sem(n) for n in (
            "sx_full", "sx_negmax", "sx_exp", "sx_norm", "px_turned", "px_copied", "ox_full", "ox_copied",
            "xo_full", "xo_added"))
        r_full, r_negmax, r_exp, r_aff, r_turned, r_affT, top_done, sel_turned, sel_cols, sel_bcast, sel_ready = (sem(n) for n in (
            "r_full", "r_negmax", "r_exp", "r_aff", "r_turned", "r_affT", "top_done", "sel_turned", "sel_cols",
            "sel_bcast", "sel_ready"))
        xe_full, xe_ready, ab_full, silu_done, hh_ready, hh_turned, hhT_ready, y_step, ye_ready, pt_ready, sc_full, sc_added = (sem(n) for n in (
            "xe_full", "xe_ready", "ab_full", "silu_done", "hh_ready", "hh_turned", "hhT_ready", "y_step",
            "ye_ready", "pt_ready", "sc_full", "sc_added"))
        out_written = sem("out_written")

        def cols(w, c0, k=KD, n=CW):
            return (lambda s: ring[:, s, 0:k * n].rearrange("p (k c) -> p k c", k=k),
                    w.rearrange("(k p) c -> p k c", p=P)[:, :, c0:c0 + n])

        chunks = []
        QKV0 = 3 * HW
        for g in range(GROUPS):
            for part in range(3):
                n = len(chunks)
                chunks.append(cols(w_in, QKV0 + part * AW + g * CW) + (qkv_full, 4 * (n + 1)))
        HY_C = len(chunks)
        for j in range(HYT // 2):
            chunks.append(cols(w_in, j * CW) + (hy_full, 2 * (j + 1)))
        MIX_C = len(chunks)
        for j in range(4):
            for w, c0, k in ((w_gate, j * CW, KD), (w_gate, D + j * CW, KD), (w_up_hy, j * CW, HC)):
                chunks.append(cols(w, c0, k) + (mix_full, 2 * (j + 1)))
        OUT_C = len(chunks)
        for j in range(4):
            chunks.append(cols(w_out, j * CW) + (out_full, 4 * (j + 1)))
        KV_C = len(chunks)
        for j in range(4):
            chunks.append(cols(w_kv_mem, j * CW) + (kv_full, 2 * (j + 1)))
        QX_C = len(chunks)
        for j in range(2):
            chunks.append(cols(w_q_x, j * CW) + (qx_full, 2 * (j + 1)))
        XO_C = len(chunks)
        for j in range(2):
            chunks.append(cols(w_o_x, j * 512, 4, 512) + (xo_full, 4 * (j + 1)))
        MOE_C = len(chunks)
        STEP = 3 * FB
        assert STEP % RING == 0

        def slot(n):
            return n % RING

        def arrived(eng, n):
            eng.wait_ge(slot_loaded[slot(n)], 16 * (n // RING + 1))

        def wview(n, k=KD, c=CW):
            return ring[:, slot(n), 0:k * c].rearrange("p (k c) -> p k c", k=k)

        block = ctx.enter_context(nc.Block())

        @block.sync
        def _(sp):
            for n, (dst, src, _, _) in enumerate(chunks):
                if n >= RING:
                    sp.wait_ge(chunks[n - RING][2], chunks[n - RING][3])
                sp.dma_start(dst(slot(n)), src).then_inc(slot_loaded[slot(n)], 16)

            def expert_chunk(e, i):
                j, part = i // 3, i % 3
                dst = ring[:, slot(MOE_C + i), :]
                if part < 2:
                    w = (w_e_gate, w_e_up)[part]
                    src = w[e].rearrange("(k p) f -> p k f", p=P)[:, :, j * CW:(j + 1) * CW]
                    dst = dst.rearrange("p (k c) -> p k c", k=KD)
                else:
                    src = w_e_down[e, j * CW:(j + 1) * CW, :].rearrange("(k p) d -> p k d", p=P)
                    dst = dst.rearrange("p (k c) -> p k c", k=2)
                sp.dma_start(dst, src).then_inc(slot_loaded[slot(MOE_C + i)], 16)

            def freed_in_expert(i, base):
                j, part = i // 3, i % 3
                if part < 2:
                    sp.wait_ge(ab_full, base + j + 1)
                else:
                    sp.wait_ge(y_step, base + j + 1)

            for i in range(STEP):
                if i < RING:
                    sp.wait_ge(chunks[MOE_C - RING + i][2], chunks[MOE_C - RING + i][3])
                else:
                    freed_in_expert(i - RING, 0)
                expert_chunk(0, i)
            with sp.Fori(1, NE) as e:
                for i in range(STEP):
                    if i < RING:
                        freed_in_expert(STEP - RING + i, (e - 1) * FB)
                    else:
                        freed_in_expert(i - RING, e * FB)
                    expert_chunk(e, i)
            for a in range(NT):
                sp.wait_ge(norms["fin"]["scaled"], a + 1)
                sp.dma_start(out[0].rearrange("(m a) d -> m a d", a=NT)[:, a, :], hT_out(a)).then_inc(out_written, 16)
            sp.wait_ge(out_written, 16 * NT)

        @block.gpsimd
        def _(pool):
            pool.dma_start(vrow[0:8, 0, :], ln_mix_g.rearrange("(k p) -> k p", p=P)).then_inc(ld_vec, 16)
            pool.dma_start(vrow[8:16, 0, :], ln_x_g.rearrange("(k p) -> k p", p=P)).then_inc(ld_vec, 16)
            pool.dma_start(vrow[16:24, 0, :], ln_mem_g.rearrange("(k p) -> k p", p=P)).then_inc(ld_vec, 16)
            pool.dma_start(vrow[24:32, 0, :], ln_moe_g.rearrange("(k p) -> k p", p=P)).then_inc(ld_vec, 16)
            pool.dma_start(vrow[32:48, 0, :], b_gate.rearrange("(k p) -> k p", p=P)).then_inc(ld_vec, 16)
            pool.dma_start(vrow[48:66, 0, :], hy_conv_b.rearrange("(k p) -> k p", p=P)).then_inc(ld_vec, 16)
            pool.dma_start(vrow[66:78, 0, :], hy_skip.rearrange("o (k p) -> (o k) p", p=P)).then_inc(ld_vec, 16)
            pool.dma_start(vrow[0:54, 1, :], hy_conv_w.rearrange("s (k p) -> (s k) p", p=P)).then_inc(ld_vec, 16)
            pool.dma_start(wr[:, :, :], w_router.rearrange("(k p) e -> p k e", p=P)).then_inc(ld_wr, 16)
            pool.dma_start(rcos, c_rcos).then_inc(ld_rope, 16)
            pool.dma_start(rsin, c_rsin).then_inc(ld_rope, 16)
            pool.dma_start(masks, c_mask).then_inc(ld_mask, 16)
            pool.wait_ge(at_copied, NT)
            for dst, src in ((dftc, c_dftc), (dfts, c_dfts), (dftsk, c_dftsk), (idftc, c_idftc), (idfts, c_idfts)):
                pool.dma_start(dst, src).then_inc(ld_dft, 16)
            w3v = filt_w3.rearrange("k (o d c) -> k o d c", o=2, d=2)
            for u in range(2 * NU):
                o, th = u // NU, u % NU
                if u >= 1:
                    pool.wait_ge(f_full, 4 * u)
                pool.dma_start(w3u, w3v[:, o, :, th * CH:(th + 1) * CH]).then_inc(ld_w3, 16)
                if u >= 1:
                    pool.wait_ge(pchain, 4 * u)
                pool.dma_start(dec, c_decay[:, :, th * CH:(th + 1) * CH]).then_inc(ld_dec, 16)
                pool.wait_ge(ld_dec, 16 * (u + 1))
                pool.wait_ge(f_copied, 4 * (u + 1))
                if u >= 1:
                    pool.wait_ge(k_full, 4 * u)
                nc.gpsimd.tensor_tensor(ff, ff, dec, ALU.mult).then_inc(pchain, 1)
                link_n = 4 * u + 2
                nc.gpsimd.tensor_tensor(fb, fb, dec, ALU.mult).then_inc(pchain, 1)
                pool.wait_ge(pchain, link_n)
                nc.gpsimd.memset(fb[0:1, 0, :], 0.0).then_inc(pchain, 1)
                pool.wait_ge(pchain, link_n + 1)
                nc.gpsimd.tensor_tensor(fs, ff, fb, ALU.add).then_inc(pchain, 1)
                pool.wait_ge(pchain, link_n + 2)
                nc.gpsimd.tensor_tensor(ff, ff, fb, ALU.subtract).then_inc(f_sumdif, 1)
            pool.wait_ge(z_new, 2 * NU)
            pool.dma_start(wua, w_up_attn.rearrange("(k p) c -> p k c", p=P)).then_inc(ld_wua, 16)
            pool.wait_ge(prod, 2 * NU)
            pool.wait_ge(y_full, 2 * HC)
            pool.dma_start(mems, mem[0].rearrange("(m b) d -> m b d", b=MT)).then_inc(ld_mem, 16)
            pool.wait_ge(ox_full, XH)
            pool.wait_ge(xo_full, 8)
            pool.dma_start(iota, c_iota).then_inc(ld_moe, 16)
            pool.dma_start(tval, c_tval).then_inc(ld_moe, 16)
            pool.dma_start(gf, ln_f_g.partition_broadcast(P)).then_inc(ld_gf, 16)

        junk = UT[:, 5120:6144]

        def norm_scalar(act, tag, src, n):
            s = norms[tag]
            for a in range(n):
                if a >= 1:
                    act.wait_ge(s["sq"], a)
                nc.scalar.activation(junk, src[:, a, :], ACT.Square, accum_out=st[:, a:a + 1]).then_inc(s["sq"], 1)
            act.wait_ge(s["var"], 1)
            nc.scalar.activation(st[:, 12:12 + n], st[:, 8:8 + n], ACT.Sqrt).then_inc(s["sqrt"], 1)

        def norm_vector(dve, link, tag, src, dst, n):
            s = norms[tag]
            dve.wait_ge(s["sq"], n)
            nc.vector.tensor_scalar(st[:, 8:8 + n], st[:, 0:n], 1.0 / D, EPS, ALU.mult, ALU.add).then_inc(s["var"], 1)
            dve.wait_ge(s["sqrt"], 1)
            r, v, t = st[:, 16:16 + n], st[:, 8:8 + n], st[:, 20:20 + n]
            link(nc.vector.reciprocal(r, st[:, 12:12 + n]))
            link(nc.vector.tensor_tensor(t, r, r, ALU.mult))
            link(nc.vector.tensor_tensor(t, t, v, ALU.mult))
            link(nc.vector.tensor_scalar(t, t, -0.5, 1.5, ALU.mult, ALU.add))
            link(nc.vector.tensor_tensor(r, r, t, ALU.mult))
            if dst is not None:
                for a in range(n):
                    nc.vector.tensor_scalar(dst[:, a, :], src[:, a, :], st[:, 16 + a:17 + a], None,
                                            ALU.mult).then_inc(s["scaled"], 1)

        def norm_tensor(pe, tag, src, n, bank0):
            s = norms[tag]
            pe.wait_ge(s["scaled"], n)
            for k in range(KD):
                if k >= 4:
                    pe.wait_ge(s["evA" if k % 2 == 0 else "evV"], k // 2 - 1)
                for a in range(n):
                    mm = pe.transpose(ps[:, bank0 + k % 4, a * P:(a + 1) * P], src[:, a, k * P:(k + 1) * P], ident[:, :])
                mm.then_inc(s["turned"], 1)

        def norm_evac(eng, tag, dst, n, bank0, col, par):
            s = norms[tag]
            for k in range(par, KD, 2):
                eng.wait_ge(s["turned"], k + 1)
                src = ps[:, bank0 + k % 4, 0:n * P]
                if par == 0:
                    nc.scalar.activation(dst[:, k, :], src, ACT.Copy, scale=vcol[:, col + k:col + k + 1]).then_inc(s["evA"], 1)
                else:
                    nc.vector.tensor_scalar(dst[:, k, :], src, vcol[:, col + k:col + k + 1], None,
                                            ALU.mult).then_inc(s["evV"], 1)

        @block.scalar
        def _(act):
            act.dma_start(xs[:, :, :], x[0].rearrange("(m a) d -> m a d", a=NT)).then_inc(ld_x, 16)
            act.dma_start(ident[:, :], c_ident).then_inc(ld_ident, 16)
            act.dma_start(embT, c_embT).then_inc(ld_filt, 16)
            act.dma_start(fw1, filt_w1).then_inc(ld_filt, 16)
            act.dma_start(fw2, filt_w2).then_inc(ld_filt, 16)
            for i, v in enumerate((filt_b1, filt_freq1, filt_b2, filt_freq2)):
                act.dma_start(fcol[:, i:i + 1], v.rearrange("(p o) -> p o", o=1)).then_inc(ld_filt, 16)

            act.wait_ge(ld_x, 16)
            norm_scalar(act, "mix", xs, NT)
            act.wait_ge(vec_ready, 2)
            norm_evac(act, "mix", hT, NT, 0, V_MIX, 0)
            for i, dst in enumerate((h1T, h2T[:, :])):
                act.wait_ge(mlp_arg, i + 1)
                nc.scalar.activation(dst, farg, ACT.Sin).then_inc(mlp_sin, 1)

            for c in range(9):
                g, part = c // 3, c % 3
                for a in range(NT):
                    n = 4 * c + a
                    if part == 2:
                        act.wait_ge(qkv_full, n + 1)
                        nc.scalar.copy(vnat[:, a, g * CW:(g + 1) * CW], ps[:, n % 4, 0:CW]).then_inc(v_copied, 1)
                    else:
                        m = 8 * g + 4 * part + a
                        act.wait_ge(qk_turned, m + 1)
                        dst = (qT, kT)[part]
                        nc.scalar.copy(dst[:, g, :, a * P:(a + 1) * P],
                                       ps[:, 4 + m % 4, 0:2 * P].rearrange("p (r t) -> p r t", r=2)).then_inc(qk_copied, 1)

            def centre(m):
                act.wait_ge(hy_full, m + 1)
                nc.scalar.activation(uT[:, m, :], ps[:, m % 2, :], ACT.Identity, bias=vcol[:, V_CB + m:V_CB + m + 1],
                                     scale=vcol[:, V_CW + HYT + m:V_CW + HYT + m + 1]).then_inc(hy_centre, 1)

            for p in range(16):
                act.wait_ge(s_negmax, p + 1)
                nc.scalar.activation(Sb[:, p % 2, :], Sb[:, p % 2, :], ACT.Exp, bias=st[:, 34 + p % 2:35 + p % 2],
                                     accum_out=st[:, 36 + p % 2:37 + p % 2]).then_inc(s_exp, 1)
                if p == 0:
                    act.wait_ge(mlp_sin, 2)
                    act.wait_ge(norms["mix"]["evA"], 4)
                centre(p)
                act.wait_ge(p_turned, p + 1)
                if p >= 2:
                    act.wait_ge(o_full, p - 1)
                nc.scalar.copy(PTb[:, p % 2, :], psc(4, 6, NKEY)).then_inc(p_copied, 1)
            centre(16)
            centre(17)

            def filter_copies(u):
                for d, dst in ((0, ff), (1, fb)):
                    for j in range(2):
                        i = 4 * u + 2 * d + j
                        act.wait_ge(f_full, i + 1)
                        if u >= 1 and d == 0 and j == 0:
                            act.wait_ge(k_full, 4 * u)
                        if u >= 1 and d == 1 and j == 0:
                            act.wait_ge(f_sumdif, u)
                        nc.scalar.copy(dst[:, 2 * j:2 * j + 2, :], ps[:, 4 + i % 4, :].rearrange(
                            "p (a c) -> p a c", a=2)).then_inc(f_copied, 1)

            def even_copies(full, base, bank0, bufs, done):
                for i in range(4):
                    act.wait_ge(full, base + i + 1)
                    nc.scalar.copy(bufs[i % 2][:, i // 2, :], ps[:, bank0 + i, 0:CH]).then_inc(done, 1)

            def z_copies(u):
                o, th = u // NU, u % NU
                if u >= 1:
                    act.wait_ge(y_full, 2 * u)
                for a in range(NT):
                    act.wait_ge(z_turned, 4 * u + a + 1)
                    nc.scalar.copy(znat[:, a, :], ps[:, a, 0:CH]).then_inc(z_copied, 1)

            filter_copies(0)
            even_copies(k_full, 0, 4, [*EV(Kb[0])], k_even)
            for u in range(2 * NU):
                z_copies(u)
                even_copies(z_full, 4 * u, 0, EV(Zb), z_even)
                if u + 1 < 2 * NU:
                    filter_copies(u + 1)
                    if u >= 1:
                        act.wait_ge(y_full, 2 * u)
                    even_copies(k_full, 4 * (u + 1), 4, [*EV(Kb[(u + 1) % 2])], k_even)

            act.wait_ge(ld_mem, 16)
            norm_scalar(act, "mem", mems, MT)
            for m in range(KD):
                for s in range(2):
                    act.wait_ge(mix_full, m + 1)
                    if m >= 2:
                        act.wait_ge(mix_done, m - 1)
                    nc.scalar.activation(gs[:, m % 2, s, :], ps[:, 4 * (m % 2) + s, :], ACT.Sigmoid,
                                         bias=vcol[:, V_BG + 8 * s + m:V_BG + 8 * s + m + 1]).then_inc(mix_gate, 1)
            norm_evac(act, "mem", mnT, MT, 0, V_MEM, 0)
            act.wait_ge(out_added, 16)
            norm_scalar(act, "xa", xs, NT)
            for i in range(8):
                act.wait_ge(kv_full, i + 1)
                if i < 4:
                    nc.scalar.copy(kxT[:, i, :], ps[:, 4 + i % 4, 0:MEM]).then_inc(kv_copied, 1)
                else:
                    j, b = (i - 4) // 2, i % 2
                    nc.scalar.copy(vx[:, b, j * CW:(j + 1) * CW], ps[:, 4 + i % 4, 0:CW]).then_inc(kv_copied, 1)
            norm_evac(act, "xa", hT, NT, 0, V_X, 0)
            for h in range(XH):
                act.wait_ge(qx_full, h + 1)
                nc.scalar.copy(qxT[:, h, :], ps[:, 4 + h, :]).then_inc(qx_copied, 1)
            for h in range(XH):
                for a in range(NT):
                    act.wait_ge(sx_negmax, 4 * h + 2 * (a // 2) + 2)
                    if h >= 2 and a == 0:
                        act.wait_ge(px_turned, 2 * (h - 1))
                    c = 40 + (h % 2) * 4 + a
                    nc.scalar.activation(Px[:, h % 2, a, :], ps[:, 2 * (h % 2) + a // 2, (a % 2) * MEM:(a % 2 + 1) * MEM],
                                         ACT.Exp, bias=st[:, c:c + 1], scale=float(P) ** -0.5,
                                         accum_out=st[:, c + 8:c + 9]).then_inc(sx_exp, 1)
                act.wait_ge(px_turned, 2 * h + 2)
                if h >= 2:
                    act.wait_ge(ox_full, h - 1)
                nc.scalar.copy(PTx[:, h % 2, :, :], ps[:, 4:6, :]).then_inc(px_copied, 1)
                act.wait_ge(ox_full, h + 1)
                nc.scalar.copy(oxT[:, h, :], ps[:, 6, :]).then_inc(ox_copied, 1)
            act.wait_ge(xo_added, 8)
            norm_scalar(act, "moe", xs, NT)
            norm_evac(act, "moe", hT, NT, 0, V_MOE, 0)
            for a in range(NT):
                act.wait_ge(r_negmax, a + 1)
                nc.scalar.activation(lg[:, a, :], ps[:, 4 + a, 0:NE], ACT.Exp, bias=st[:, 40 + a:41 + a],
                                     accum_out=st[:, 44 + a:45 + a]).then_inc(r_exp, 1)
            with act.Fori(0, NE) as e:
                for j in range(FB):
                    act.wait_ge(ab_full, e * FB + (j + 1))
                    nc.scalar.activation(sil[:, j % 2, :], ps[0:CAP, j % 2, 0:CW], ACT.Silu).then_inc(silu_done, 1)
            act.wait_ge(sc_added, NE * 8)
            norm_scalar(act, "fin", xs, NT)

        @block.tensor
        def _(pe):
            def product(out_, pairs):
                last = len(pairs) - 1
                for i, (l, r) in enumerate(pairs):
                    mm = pe.matmul(out_, l, r, start=i == 0, stop=i == last)
                return mm

            pe.wait_ge(ld_ident, 16)
            pe.wait_ge(ld_vec, 16 * 8)
            pe.transpose(ps[:, 6, 0:V_ROWS], vrow[0:V_ROWS, 0, :], ident[0:V_ROWS, 0:V_ROWS]).then_inc(vec_turned, 1)
            pe.transpose(ps[:, 7, 0:54], vrow[0:54, 1, :], ident[0:54, 0:54]).then_inc(vec_turned, 1)
            pe.wait_ge(ld_filt, 16 * 7)
            pe.matmul(ps[0:FFN, 5, :], fw1, embT, start=True, stop=True).then_inc(mlp_mm, 1)
            norm_tensor(pe, "mix", hn, NT, 0)
            pe.wait_ge(mlp_sin, 1)
            pe.matmul(ps[0:FFN, 5, :], fw2, h1T, start=True, stop=True).then_inc(mlp_mm, 1)

            pe.wait_ge(norms["mix"]["evA"], 4)
            pe.wait_ge(norms["mix"]["evV"], 4)

            def turn_heads(m):
                pe.wait_ge(roped, m + 1)
                if m >= 4:
                    pe.wait_ge(qk_copied, m - 3)
                else:
                    pe.wait_ge(mlp_arg, 2)
                for r in range(2):
                    mm = pe.transpose(ps[:, 4 + m % 4, r * P:(r + 1) * P], rope_out[:, m % 2, r * P:(r + 1) * P], ident[:, :])
                mm.then_inc(qk_turned, 1)

            done = 0
            for c in range(9):
                g, part = c // 3, c % 3
                arrived(pe, c)
                for a in range(NT):
                    n = 4 * c + a
                    if n >= 4:
                        c4, a4 = c - 1, a
                        if c4 % 3 == 2:
                            pe.wait_ge(v_copied, 4 * (c4 // 3) + a4 + 1)
                        else:
                            pe.wait_ge(roped, 8 * (c4 // 3) + 4 * (c4 % 3) + a4 + 1)
                    product(ps[:, n % 4, 0:CW], [(hT[:, k, a * P:(a + 1) * P], wview(c)[:, k, :]) for k in range(KD)]
                            ).then_inc(qkv_full, 1)
                    if part < 2:
                        m = 8 * g + 4 * part + a
                        if m > done:
                            turn_heads(done)
                            done += 1
                    elif a == 0:
                        turn_heads(done)
                        done += 1

            def scores(p):
                a, h = p // 4, p % 4
                r, q0 = h // 2, 64 * (h % 2)
                if p == 0:
                    pe.wait_ge(qk_copied, 24)
                    pe.wait_ge(v_copied, 12)
                    pe.wait_ge(roped, 24)
                else:
                    pe.wait_ge(s_masked, p)
                q = lambda g: qT[q0:q0 + 64, g, r, a * P:(a + 1) * P]
                pe.matmul(ps[:, 2, :], q(0), kT[q0:q0 + 64, 0, r, :], start=True, stop=True)
                for g in (1, 2):
                    mm = pe.matmul(ps[:, 3, (g - 1) * P:g * P], q(g), kT[q0:q0 + 64, g, r, a * P:(a + 1) * P],
                                   start=True, stop=True)
                mm.then_inc(s_full, 1)

            def hyena_tile(m):
                if m % 2 == 0:
                    arrived(pe, HY_C + m // 2)
                if m >= 2:
                    pe.wait_ge(hy_conv, m - 1)
                c0 = (m % 2) * P
                product(ps[:, m % 2, :], [(wview(HY_C + m // 2)[:, k, c0:c0 + P], hT[:, k, :]) for k in range(KD)]
                        ).then_inc(hy_full, 1)

            def turn_probs(p):
                pe.wait_ge(s_exp, p + 1)
                if p >= 1:
                    pe.wait_ge(p_copied, p)
                for i in range(6):
                    mm = pe.transpose(ps[:, 4 + i // 4, (i % 4) * P:(i % 4 + 1) * P], Sb[:, p % 2, i * P:(i + 1) * P], ident[:, :])
                mm.then_inc(p_turned, 1)

            def values(p):
                a, h = p // 4, p % 4
                pe.wait_ge(p_copied, p + 1)
                if p >= 1:
                    pe.wait_ge(o_scaled, p)
                keys = [(0, b) for b in range(NT)] + [(1, a), (2, a)]
                product(ps[:, 6, 0:64], [(PTb[:, p % 2, i * P:(i + 1) * P], vnat[:, b, g * CW + h * 64:g * CW + h * 64 + 64])
                                         for i, (g, b) in enumerate(keys)]).then_inc(o_full, 1)

            def turn_attn(a):
                pe.wait_ge(o_scaled, 4 * a + 4)
                if a >= 1:
                    pe.wait_ge(at_copied, a)
                for r in range(2):
                    mm = pe.transpose(ps[:, 7, r * P:(r + 1) * P], anat[:, a % 2, r * P:(r + 1) * P], ident[:, :])
                mm.then_inc(at_turned, 1)

            scores(0)
            for p in range(16):
                hyena_tile(p)
                turn_probs(p)
                if p + 1 < 16:
                    scores(p + 1)
                if p % 4 == 0 and p > 0:
                    turn_attn(p // 4 - 1)
                values(p)
            hyena_tile(16)
            turn_attn(3)
            hyena_tile(17)

            def filter_time(u):
                pe.wait_ge(ld_w3, 16 * (u + 1))
                for d in range(2):
                    for j in range(2):
                        i = 4 * u + 2 * d + j
                        if u >= 1:
                            pe.wait_ge(k_ready, 4 * u)
                        elif i == 0:
                            pe.wait_ge(at_copied, NT)
                            pe.wait_ge(p_copied, 16)
                            pe.wait_ge(o_scaled, 16)
                        for s in range(2):
                            a = 2 * j + s
                            mm = pe.matmul(ps[:, 4 + i % 4, s * CH:(s + 1) * CH], h2T[:, a * P:(a + 1) * P], w3u[:, d, :],
                                           start=True, stop=True)
                        mm.then_inc(f_full, 1)

            def spectrum(u, bank0, cos_in, sin_in, full, special):
                for j in range(2):
                    fj = slice(j * P, (j + 1) * P)
                    product(ps[:, bank0 + 2 * j, 0:CH], [(dftc[:, a, fj], cos_in[:, a, :]) for a in (0, 2)])
                    product(ps[:, bank0 + 2 * j, CH:2 * CH], [(dftc[:, a, fj], cos_in[:, a, :]) for a in (1, 3)]
                            ).then_inc(full, 1)
                    if special and j == 0:
                        o_ = ps[:, bank0 + 1, 0:CH]
                        pe.matmul(o_, dftsk[:, 0, :], sin_in[:, 0, :], start=True, stop=False)
                        for a in (0, 2):
                            pe.matmul(o_[0:1, :], dfts[:, a, 0:1], cos_in[:, a, :], start=False, stop=False)
                        pe.matmul(o_, dftsk[:, 1, :], sin_in[:, 2, :], start=False, stop=True)
                    else:
                        product(ps[:, bank0 + 2 * j + 1, 0:CH], [(dfts[:, a, fj], sin_in[:, a, :]) for a in (0, 2)])
                    product(ps[:, bank0 + 2 * j + 1, CH:2 * CH], [(dfts[:, a, fj], sin_in[:, a, :]) for a in (1, 3)]
                            ).then_inc(full, 1)

            def filter_spectrum(u):
                pe.wait_ge(f_sumdif, u + 1)
                pe.wait_ge(f_copied, 4 * (u + 1))
                if u == 0:
                    pe.wait_ge(ld_dft, 16 * 5)
                spectrum(u, 4, fs, ff, k_full, True)

            def turn_z(u):
                th = u % NU
                if u < NU:
                    pe.wait_ge(hy_conv, 18 if u == 0 else 18)
                else:
                    pe.wait_ge(z_new, 2 * (u - NU + 1))
                for a in range(NT):
                    if u >= 1 and a == 0:
                        pe.wait_ge(z_new, 2 * u)
                    for s in range(2):
                        mm = pe.transpose(ps[:, a, s * P:(s + 1) * P], uT[:, 2 * th + s, a * P:(a + 1) * P], ident[:, :])
                    mm.then_inc(z_turned, 1)

            def z_spectrum(u):
                pe.wait_ge(z_copied, 4 * (u + 1))
                spectrum(u, 0, znat, znat, z_full, False)

            def inverse(u):
                pe.wait_ge(prod, u + 1)
                pe.wait_ge(z_ready, 4 * (u + 1))
                Ue, Uo = Kb[u % 2][0], Kb[u % 2][2]
                Ve, Vo = t3, t1
                for s in range(2):
                    cs = slice(s * P, (s + 1) * P)
                    for par, (U_, V_) in enumerate(((Ue, Ve), (Uo, Vo))):
                        o_ = ps[:, s, :].rearrange("p (i q t) -> p i q t", i=2, q=2)[:, :, par, :]
                        pairs = []
                        for j in range(2):
                            for src, mat in ((U_, idftc), (V_, idfts)):
                                pairs.append((src[:, j, cs], mat[:, j, :].rearrange(
                                    "p (i q t) -> p i q t", i=2, q=2)[:, :, par, :]))
                        mm = product(o_, pairs)
                    mm.then_inc(y_full, 1)

            filter_time(0)
            filter_spectrum(0)
            for u in range(2 * NU):
                turn_z(u)
                z_spectrum(u)
                if u + 1 < 2 * NU:
                    filter_time(u + 1)
                    filter_spectrum(u + 1)
                inverse(u)

            pe.wait_ge(z_new, 4 * NU)
            pe.wait_ge(k_ready, 8 * NU)
            pe.wait_ge(z_ready, 8 * NU)
            for m in range(KD):
                j, c0 = m // 2, (m % 2) * P
                c = MIX_C + 3 * j
                if m == 0:
                    pe.wait_ge(ld_wua, 16)
                if m % 2 == 0:
                    for i in range(3):
                        arrived(pe, c + i)
                if m >= 2:
                    pe.wait_ge(mix_done, m - 1)
                b = 4 * (m % 2)
                cs = slice(c0, c0 + P)
                product(ps[:, b, :], [(wview(c)[:, k, cs], hT[:, k, :]) for k in range(KD)])
                product(ps[:, b + 1, :], [(wview(c + 1)[:, k, cs], hT[:, k, :]) for k in range(KD)])
                product(ps[:, b + 2, :], [(wview(c + 2, HC)[:, k, cs], uT[:, k, :]) for k in range(HC)])
                product(ps[:, b + 3, :], [(wua[:, k, m * P:(m + 1) * P], attnT[:, k, :]) for k in range(2)]
                        ).then_inc(mix_full, 1)
            pe.wait_ge(mix_done, KD)
            pe.wait_ge(mix_gate, 2 * KD)
            norm_tensor(pe, "mem", mhn, MT, 0)
            for j in range(4):
                arrived(pe, OUT_C + j)
                for a in range(NT):
                    i = 4 * j + a
                    if i >= 4:
                        pe.wait_ge(out_added, i - 3)
                    product(ps[:, 4 + a, 0:CW], [(mixT[:, k, a * P:(a + 1) * P], wview(OUT_C + j)[:, k, :])
                                                 for k in range(KD)]).then_inc(out_full, 1)
            pe.wait_ge(norms["mem"]["evA"], 4)
            pe.wait_ge(norms["mem"]["evV"], 4)
            for i in range(8):
                if i % 2 == 0:
                    arrived(pe, KV_C + i // 2)
                w = wview(KV_C + i // 2)
                if i >= 4:
                    pe.wait_ge(kv_copied, i - 3)
                else:
                    pe.wait_ge(out_added, 13 + i)
                if i < 4:
                    c0 = (i % 2) * P
                    product(ps[:, 4 + i % 4, 0:MEM], [(w[:, k, c0:c0 + P], mnT[:, k, :]) for k in range(KD)]).then_inc(kv_full, 1)
                else:
                    b = i % 2
                    product(ps[:, 4 + i % 4, 0:CW], [(mnT[:, k, b * P:(b + 1) * P], w[:, k, :]) for k in range(KD)]
                            ).then_inc(kv_full, 1)
            norm_tensor(pe, "xa", hn, NT, 0)
            pe.wait_ge(norms["xa"]["evA"], 4)
            pe.wait_ge(norms["xa"]["evV"], 4)
            pe.wait_ge(kv_copied, 8)
            for h in range(XH):
                if h % 2 == 0:
                    arrived(pe, QX_C + h // 2)
                c0 = (h % 2) * P
                product(ps[:, 4 + h, :], [(wview(QX_C + h // 2)[:, k, c0:c0 + P], hT[:, k, :]) for k in range(KD)]
                        ).then_inc(qx_full, 1)

            def x_scores(h):
                pe.wait_ge(qx_copied, h + 1)
                for a in range(NT):
                    if h >= 2 and a == 0:
                        pe.wait_ge(sx_exp, 4 * (h - 1))
                    mm = pe.matmul(ps[:, 2 * (h % 2) + a // 2, (a % 2) * MEM:(a % 2 + 1) * MEM], qxT[:, h, a * P:(a + 1) * P],
                                   kxT[:, h, :], start=True, stop=True)
                    mm.then_inc(sx_full, 1)

            x_scores(0)
            for h in range(XH):
                if h + 1 < XH:
                    x_scores(h + 1)
                pe.wait_ge(sx_norm, 4 * (h + 1))
                if h == 0:
                    pe.wait_ge(qx_copied, XH)
                else:
                    pe.wait_ge(px_copied, h)
                for b in range(MT):
                    for a in range(NT):
                        mm = pe.transpose(ps[:, 4 + b, a * P:(a + 1) * P], Px[:, h % 2, a, b * P:(b + 1) * P], ident[:, :])
                    mm.then_inc(px_turned, 1)
                pe.wait_ge(px_copied, h + 1)
                if h >= 1:
                    pe.wait_ge(ox_copied, h)
                product(ps[:, 6, :], [(vx[:, b, h * P:(h + 1) * P], PTx[:, h % 2, b, :]) for b in range(MT)]).then_inc(ox_full, 1)
            pe.wait_ge(ox_copied, XH)
            for j in range(2):
                arrived(pe, XO_C + j)
                for a in range(NT):
                    i = 4 * j + a
                    if i >= 4:
                        pe.wait_ge(xo_added, i - 3)
                    product(ps[:, a, :], [(oxT[:, k, a * P:(a + 1) * P], wview(XO_C + j, 4, 512)[:, k, :])
                                          for k in range(XH)]).then_inc(xo_full, 1)
            pe.wait_ge(xo_added, 8)
            norm_tensor(pe, "moe", hn, NT, 0)
            pe.wait_ge(norms["moe"]["evA"], 4)
            pe.wait_ge(norms["moe"]["evV"], 4)
            pe.wait_ge(ld_wr, 16)
            for a in range(NT):
                product(ps[:, 4 + a, 0:NE], [(hT[:, k, a * P:(a + 1) * P], wr[:, k, :]) for k in range(KD)]).then_inc(r_full, 1)
            pe.wait_ge(r_aff, NT)
            for a in range(NT):
                mm = pe.transpose(ps[0:NE, 0, a * P:(a + 1) * P], aff[:, a, :], ident[:, :])
            mm.then_inc(r_turned, 1)
            pe.wait_ge(top_done, 1)
            pe.transpose(ps[:, 1, 0:NE], topf[:, :, :].rearrange("p r s -> p (r s)"), ident[0:NE, 0:NE])
            pe.transpose(ps[:, 1, NE:2 * NE], topv[:, :, :].rearrange("p r s -> p (r s)"), ident[0:NE, 0:NE]).then_inc(sel_turned, 1)
            for b in range(2):
                pe.matmul(ps[:, 2 + b, :], ones16, bdiag[:, 8 * b:8 * b + 8, :].rearrange("p e s -> p (e s)"),
                          start=True, stop=True).then_inc(sel_bcast, 1)
            pe.wait_ge(sel_ready, 2 * NT)
            pe.wait_ge(sel_cols, 2)
            with pe.Fori(0, NE) as e:
                def chunk_in(i):
                    n = MOE_C + i
                    pe.wait_ge(slot_loaded[slot(n)], e * (16 * STEP // RING) + 16 * (n // RING + 1))

                def gate_up(j):
                    chunk_in(3 * j)
                    chunk_in(3 * j + 1)
                    for k in range(KD):
                        for half in range(2):
                            mm = pe.matmul(ps[CAP * half:CAP * half + CAP, j % 2, 0:CW], xeT[:, k, :],
                                           wview(MOE_C + 3 * j + half)[:, k, :], start=k == 0, stop=k == KD - 1)
                    mm.then_inc(ab_full, 1)

                def down(j):
                    pe.wait_ge(hh_ready, e * FB + (j + 1))
                    for i in range(2):
                        mm = pe.matmul(ps[:, 2, (j % 2) * P + i * CAP:(j % 2) * P + (i + 1) * CAP], hh[:, j % 2, i * P:(i + 1) * P],
                                       ident[0:CAP, 0:CAP], start=True, stop=True)
                    mm.then_inc(hh_turned, 1)
                    chunk_in(3 * j + 2)
                    pe.wait_ge(hhT_ready, e * FB + (j + 1))
                    w = wview(MOE_C + 3 * j + 2, 2, D)
                    for i in range(2):
                        for half in range(2):
                            mm = pe.matmul(ps[CAP * half:CAP * half + CAP, 3, :], hhT[:, j % 2, i, :],
                                           w[:, i, half * 512:(half + 1) * 512], start=j == 0 and i == 0,
                                           stop=j == FB - 1 and i == 1)
                    mm.then_inc(y_step, 1)

                for k in range(KD):
                    for a in range(NT):
                        mm = pe.matmul(ps[:, 0, k * CAP:(k + 1) * CAP], hn[:, a, k * P:(k + 1) * P],
                                       Psel[:, a, bass.ds(e * CAP, CAP)], start=a == 0, stop=a == NT - 1)
                mm.then_inc(xe_full, 1)
                pe.wait_ge(xe_ready, e + 1)
                gate_up(0)
                for j in range(FB):
                    if j + 1 < FB:
                        gate_up(j + 1)
                    down(j)
                pe.wait_ge(ye_ready, e + 1)
                pe.wait_ge(pt_ready, e + 1)
                for a in range(NT):
                    b = 4 + 2 * (a % 2)
                    if a >= 2:
                        pe.wait_ge(sc_added, e * 8 + 2 * (a - 1))
                    for half in range(2):
                        pe.matmul(ps[:, b + half, :], PTe[CAP * half:CAP * half + CAP, a * P:(a + 1) * P],
                                  ye[CAP * half:CAP * half + CAP, :], start=True, stop=True).then_inc(sc_full, 1)

        @block.vector
        def _(dve):
            n = [0]

            def link(ins):
                n[0] += 1
                ins.then_inc(chain, 1)
                dve.wait_ge(chain, n[0])

            def reduce_angle(i):
                dve.wait_ge(mlp_mm, i + 1)
                if i == 1:
                    dve.wait_ge(mlp_sin, 1)
                link(nc.vector.tensor_scalar(farg, ps[0:FFN, 5, :], fcol[:, 2 * i:2 * i + 1], fcol[:, 2 * i + 1:2 * i + 2],
                                             ALU.add, ALU.mult))
                link(nc.vector.tensor_scalar(fk, farg, 1.0 / TWO_PI, MAGIC, ALU.mult, ALU.add))
                link(nc.vector.tensor_scalar(fk, fk, MAGIC, None, ALU.subtract))
                for c in (PI_A, PI_B, PI_C):
                    link(nc.vector.scalar_tensor_tensor(out=farg, in0=fk, scalar=-c, in1=farg, op0=ALU.mult, op1=ALU.add))
                nc.vector.tensor_scalar(farg, farg, 3.1415925, -3.1415925, ALU.min, ALU.max).then_inc(mlp_arg, 1)

            dve.wait_ge(vec_turned, 2)
            nc.vector.tensor_copy(vcol[:, 0:V_ROWS], ps[:, 6, 0:V_ROWS]).then_inc(vec_ready, 1)
            nc.vector.tensor_copy(vcol[:, V_CW:V_COLS], ps[:, 7, 0:54]).then_inc(vec_ready, 1)
            dve.wait_ge(vec_ready, 2)
            dve.wait_ge(ld_filt, 16 * 7)
            reduce_angle(0)
            dve.wait_ge(ld_x, 16)
            norm_vector(dve, link, "mix", xs, hn, NT)
            norm_evac(dve, "mix", hT, NT, 0, V_MIX, 1)
            reduce_angle(1)

            dve.wait_ge(ld_rope, 32)
            for g in range(GROUPS):
                for part in range(2):
                    for a in range(NT):
                        m = 8 * g + 4 * part + a
                        tile = 4 * (3 * g + part) + a
                        dve.wait_ge(qkv_full, tile + 1)
                        if m >= 1:
                            dve.wait_ge(roped, m)
                        src = ps[:, tile % 4, 0:CW].rearrange("p (h s c) -> p h s c", h=4, s=2)
                        A4 = ropeA.rearrange("p (h s c) -> p h s c", h=4, s=2)
                        B4 = ropeB.rearrange("p (h s c) -> p h s c", h=4, s=2)
                        cb = lambda t_, s: t_[:, a, s * 32:(s + 1) * 32].unsqueeze(1).to_broadcast([P, 4, 32])
                        for s in range(2):
                            nc.vector.tensor_tensor(A4[:, :, s, :], src[:, :, s, :], cb(rcos, s), ALU.mult)
                        nc.vector.tensor_tensor(B4[:, :, 0, :], src[:, :, 1, :], cb(rsin, 0), ALU.mult)
                        link(nc.vector.tensor_tensor(B4[:, :, 1, :], src[:, :, 0, :], cb(rsin, 1), ALU.mult))
                        if m >= 2:
                            dve.wait_ge(qk_turned, m - 1)
                        nc.vector.tensor_tensor(rope_out[:, m % 2, :], ropeA, ropeB, ALU.add).then_inc(roped, 1)

            def softmax_head(p):
                a = p // 4
                dve.wait_ge(s_full, p + 1)
                if p == 0:
                    dve.wait_ge(ld_mask, 16)
                    dve.wait_ge(qk_turned, 24)
                if p >= 2:
                    dve.wait_ge(p_turned, p - 1)
                nc.vector.scalar_tensor_tensor(out=Sb[:, p % 2, :], in0=psc(2, 4, NKEY), scalar=0.125, in1=masks[:, a, :],
                                               op0=ALU.mult, op1=ALU.add).then_inc(s_masked, 1)
                dve.wait_ge(s_masked, p + 1)
                link(nc.vector.tensor_reduce(st[:, 32 + p % 2:33 + p % 2], Sb[:, p % 2, :], AX.X, ALU.max))
                nc.vector.tensor_scalar(st[:, 34 + p % 2:35 + p % 2], st[:, 32 + p % 2:33 + p % 2], -1.0, None,
                                        ALU.mult).then_inc(s_negmax, 1)

            def conv_sides(m):
                dve.wait_ge(hy_centre, m + 1)
                L, R = vcol[:, V_CW + m:V_CW + m + 1], vcol[:, V_CW + 2 * HYT + m:V_CW + 2 * HYT + m + 1]
                src, dst, n3 = ps[:, m % 2, :], uT[:, m, :], 3 * P

                def tap(d0, s0, cnt, w):
                    return nc.vector.scalar_tensor_tensor(out=dst[:, d0:d0 + cnt], in0=src[:, s0:s0 + cnt], scalar=w,
                                                          in1=dst[:, d0:d0 + cnt], op0=ALU.mult, op1=ALU.add)
                tap(P, 0, n3, L)
                link(tap(1, n3, P - 1, L))
                tap(0, P, n3, R)
                tap(n3, 1, P - 1, R).then_inc(hy_conv, 1)

            def scale_heads(p):
                a, h = p // 4, p % 4
                dve.wait_ge(s_exp, p + 1)
                link(nc.vector.reciprocal(st[:, 38 + p % 2:39 + p % 2], st[:, 36 + p % 2:37 + p % 2]))
                dve.wait_ge(o_full, p + 1)
                if h == 0 and a >= 2:
                    dve.wait_ge(at_turned, a - 1)
                nc.vector.tensor_scalar(anat[:, a % 2, h * 64:(h + 1) * 64], ps[:, 6, 0:64], st[:, 38 + p % 2:39 + p % 2],
                                        None, ALU.mult).then_inc(o_scaled, 1)

            def copy_attn(a):
                dve.wait_ge(at_turned, a + 1)
                nc.vector.tensor_copy(attnT[:, :, a * P:(a + 1) * P],
                                      ps[:, 7, 0:2 * P].rearrange("p (r t) -> p r t", r=2)).then_inc(at_copied, 1)

            softmax_head(0)
            for p in range(16):
                conv_sides(p)
                if p + 1 < 16:
                    softmax_head(p + 1)
                if p % 4 == 0 and p > 0:
                    copy_attn(p // 4 - 1)
                scale_heads(p)
            conv_sides(16)
            copy_attn(3)
            conv_sides(17)

            TT = nc.vector.tensor_tensor

            def butterflies(base, full, even, bank0, B, done):
                for i in range(4):
                    j, s = i // 2, i % 2
                    dve.wait_ge(even, base + i + 1)
                    odd = ps[:, bank0 + i, CH:2 * CH]
                    e_ = EV(B)[s][:, j, :]
                    if s == 0:
                        link(nc.vector.tensor_tensor(B[0][:, j, :], e_, odd, ALU.add))
                        nc.vector.tensor_tensor(B[2][:, j, :], e_, odd, ALU.subtract).then_inc(done, 1)
                    else:
                        link(nc.vector.tensor_tensor(B[3][:, j, :], odd, e_, ALU.subtract))
                        nc.vector.tensor_tensor(B[1][:, j, :], e_, odd, ALU.add).then_inc(done, 1)

            def products(u):
                Zp, Z1, Zq, Z2 = ZP
                Kp, K1, Kq, K2 = Kb[u % 2]
                dve.wait_ge(z_ready, 4 * (u + 1))
                dve.wait_ge(k_ready, 4 * (u + 1))
                dve.wait_ge(z_full, 4 * (u + 1))
                if u >= 1:
                    dve.wait_ge(y_full, 2 * u)
                TT(t1, Zp, K1, ALU.mult)
                TT(t2, Zq, K2, ALU.mult)
                link(TT(t3, Z1, Kp, ALU.mult))
                link(TT(t1, t1, t3, ALU.add))
                link(TT(t3, Z2, Kq, ALU.mult))
                link(TT(t2, t2, t3, ALU.add))
                TT(t3, t1, t2, ALU.subtract)
                link(TT(t1, t1, t2, ALU.add))
                TT(t2[0:1, 0, :], Z1[0:1, 0, :], K2[0:1, 0, :], ALU.mult)
                link(TT(t2[0:1, 1, :], Z2[0:1, 0, :], K1[0:1, 0, :], ALU.mult))
                TT(t3[0:1, 0, :], t2[0:1, 0, :], t2[0:1, 1, :], ALU.add)
                TT(Zp, Zp, Kp, ALU.mult)
                TT(Zq, Zq, Kq, ALU.mult)
                TT(Z1, Z1, K1, ALU.mult)
                link(TT(Z2, Z2, K2, ALU.mult))
                TT(K1, Z1, Z2, ALU.add)
                link(TT(K2, Z1, Z2, ALU.subtract))
                nc.vector.tensor_copy(t1[0:1, 0, :], K2[0:1, 0, :])
                nc.vector.memset(K1[0:1, 0, :], 0.0)
                TT(Kp, Zp, Zq, ALU.add)
                link(TT(Kq, Zp, Zq, ALU.subtract))
                nc.vector.memset(K2[0:1, 0, :], 0.0)
                link(TT(Kp, Kp, K1, ALU.subtract))
                TT(Kq, Kq, K2, ALU.subtract).then_inc(prod, 1)

            def gate(u):
                o, th = u // NU, u % NU
                for s in range(2):
                    m = 2 * th + s
                    dve.wait_ge(y_full, 2 * u + s + 1)
                    link(nc.vector.scalar_tensor_tensor(out=uT[:, m, :], in0=uT[:, m, :],
                                                        scalar=vcol[:, V_SKIP + o * HC + m:V_SKIP + o * HC + m + 1],
                                                        in1=ps[:, s, :], op0=ALU.mult, op1=ALU.add))
                    TT(uT[:, m, :], uT[:, m, :], uT[:, (o + 1) * HC + m, :], ALU.mult).then_inc(z_new, 1)

            butterflies(0, k_full, k_even, 4, Kb[0], k_ready)
            for u in range(2 * NU):
                butterflies(4 * u, z_full, z_even, 0, ZP, z_ready)
                products(u)
                if u + 1 < 2 * NU:
                    butterflies(4 * (u + 1), k_full, k_even, 4, Kb[(u + 1) % 2], k_ready)
                gate(u)

            norm_vector(dve, link, "mem", mems, mhn, MT)
            for m in range(KD):
                b = 4 * (m % 2)
                dve.wait_ge(mix_gate, 2 * m + 2)
                nc.vector.tensor_tensor(mt[:, 0, :], gs[:, m % 2, 0, :], ps[:, b + 2, :], ALU.mult)
                link(nc.vector.tensor_tensor(mt[:, 1, :], gs[:, m % 2, 1, :], ps[:, b + 3, :], ALU.mult))
                nc.vector.tensor_tensor(mixT[:, m, :], mt[:, 0, :], mt[:, 1, :], ALU.add).then_inc(mix_done, 1)
                dve.wait_ge(mix_done, m + 1)
            norm_evac(dve, "mem", mnT, MT, 0, V_MEM, 1)
            for i in range(16):
                j, a = i // 4, i % 4
                dve.wait_ge(out_full, i + 1)
                dst = xs[:, a, j * CW:(j + 1) * CW]
                nc.vector.tensor_tensor(dst, dst, ps[:, 4 + a, 0:CW], ALU.add).then_inc(out_added, 1)
            dve.wait_ge(out_added, 16)
            dve.wait_ge(out_full, 16)
            norm_vector(dve, link, "xa", xs, hn, NT)
            norm_evac(dve, "xa", hT, NT, 0, V_X, 1)
            for h in range(XH):
                for a in range(NT):
                    c = 40 + (h % 2) * 4 + a
                    dve.wait_ge(sx_full, 4 * h + 2 * (a // 2) + 2)
                    link(nc.vector.tensor_reduce(st[:, 56 + a:57 + a],
                                                 ps[:, 2 * (h % 2) + a // 2, (a % 2) * MEM:(a % 2 + 1) * MEM], AX.X, ALU.max))
                    nc.vector.tensor_scalar(st[:, c:c + 1], st[:, 56 + a:57 + a], -float(P) ** -0.5, None,
                                            ALU.mult).then_inc(sx_negmax, 1)
                for a in range(NT):
                    c = 40 + (h % 2) * 4 + a
                    dve.wait_ge(sx_exp, 4 * h + a + 1)
                    link(nc.vector.reciprocal(st[:, 60 + a:61 + a], st[:, c + 8:c + 9]))
                    nc.vector.tensor_scalar(Px[:, h % 2, a, :], Px[:, h % 2, a, :], st[:, 60 + a:61 + a], None,
                                            ALU.mult).then_inc(sx_norm, 1)
            for i in range(8):
                j, a = i // 4, i % 4
                dve.wait_ge(xo_full, i + 1)
                dst = xs[:, a, j * 512:(j + 1) * 512]
                nc.vector.tensor_tensor(dst, dst, ps[:, a, :], ALU.add).then_inc(xo_added, 1)
            dve.wait_ge(xo_added, 8)
            norm_vector(dve, link, "moe", xs, hn, NT)
            norm_evac(dve, "moe", hT, NT, 0, V_MOE, 1)
            for a in range(NT):
                dve.wait_ge(r_full, a + 1)
                link(nc.vector.tensor_reduce(st[:, 56 + a:57 + a], ps[:, 4 + a, 0:NE], AX.X, ALU.max))
                nc.vector.tensor_scalar(st[:, 40 + a:41 + a], st[:, 56 + a:57 + a], -1.0, None, ALU.mult).then_inc(r_negmax, 1)
            dve.wait_ge(r_exp, NT)
            link(nc.vector.reciprocal(st[:, 60:64], st[:, 44:48]))
            for a in range(NT):
                nc.vector.tensor_scalar(aff[:, a, :], lg[:, a, :], st[:, 60 + a:61 + a], None, ALU.mult).then_inc(r_aff, 1)
            dve.wait_ge(r_turned, 1)
            link(nc.vector.tensor_copy(affT.rearrange("e (m a) -> e a m", a=NT),
                                       ps[0:NE, 0, :].rearrange("e (a m) -> e a m", a=NT)))
            for r in range(CAP // 8):
                v, ix = topv[:, 0, 8 * r:8 * r + 8], topi[:, 8 * r:8 * r + 8]
                link(nc.vector.max(v, affT))
                link(nc.vector.max_index(ix, v, affT))
                link(nc.vector.match_replace(affT, v, affT, -1.0))
            nc.vector.tensor_copy(topv[:, 1, :], topv[:, 0, :])
            nc.vector.tensor_copy(topf[:, 0, :], topi)
            link(nc.vector.tensor_copy(topf[:, 1, :], topi))
            nc.vector.memset(ones16, 1.0)
            TT(bdiag, topf[:, 0, :].unsqueeze(1).to_broadcast([NE, NE, CAP]),
               ident[0:NE, 0:NE].unsqueeze(2).to_broadcast([NE, NE, CAP]), ALU.mult).then_inc(top_done, 1)
            dve.wait_ge(sel_turned, 1)
            nc.vector.tensor_copy(icol, ps[:, 1, 0:NE]).then_inc(sel_cols, 1)
            nc.vector.tensor_copy(gcol, ps[:, 1, NE:2 * NE]).then_inc(sel_cols, 1)
            dve.wait_ge(ld_moe, 32)
            for b in range(2):
                dve.wait_ge(sel_bcast, b + 1)
                for a in range(NT):
                    nc.vector.tensor_scalar(Psel[:, a, b * 512:(b + 1) * 512], ps[:, 2 + b, :], tval[:, a:a + 1], None,
                                            ALU.is_equal).then_inc(sel_ready, 1)
            dve.wait_ge(sel_cols, 2)
            dve.wait_ge(sel_ready, 8)
            with dve.Fori(0, NE) as e:
                dve.wait_ge(xe_full, e + 1)
                TT(xeT, ps[:, 0, :].rearrange("p (k s) -> p k s", k=KD),
                   vcol[:, V_MOE:V_MOE + KD].unsqueeze(2).to_broadcast([P, KD, CAP]), ALU.mult).then_inc(xe_ready, 1)
                nc.vector.tensor_scalar(PTe, iota, icol[:, bass.ds(e, 1)], None, ALU.is_equal).then_inc(pt_ready, 1)
                for j in range(FB):
                    dve.wait_ge(silu_done, e * FB + (j + 1))
                    TT(hh[:, j % 2, :], sil[:, j % 2, :], ps[CAP:2 * CAP, j % 2, 0:CW], ALU.mult).then_inc(hh_ready, 1)
                    dve.wait_ge(hh_turned, e * FB + (j + 1))
                    nc.vector.tensor_copy(hhT[:, j % 2, :, :], ps[:, 2, (j % 2) * P:(j % 2 + 1) * P].rearrange(
                        "p (i s) -> p i s", i=2)).then_inc(hhT_ready, 1)
                dve.wait_ge(y_step, e * FB + FB)
                nc.vector.tensor_scalar(ye, ps[:, 3, :], gcol[:, bass.ds(e, 1)], None, ALU.mult).then_inc(ye_ready, 1)
                for a in range(NT):
                    for half in range(2):
                        dve.wait_ge(sc_full, e * 8 + (2 * a + half + 1))
                        dst = xs[:, a, half * 512:(half + 1) * 512]
                        TT(dst, dst, ps[:, 4 + 2 * (a % 2) + half, :], ALU.add).then_inc(sc_added, 1)
            dve.wait_ge(sc_added, NE * 8)
            norm_vector(dve, link, "fin", xs, None, NT)
            dve.wait_ge(ld_gf, 16)
            for a in range(NT):
                nc.vector.scalar_tensor_tensor(out=hT_out(a), in0=xs[:, a, :], scalar=st[:, 16 + a:17 + a], in1=gf,
                                               op0=ALU.mult, op1=ALU.mult).then_inc(norms["fin"]["scaled"], 1)


_INS = ["x", "mem", "ln_mix_g", "w_in", "hy_conv_w", "hy_conv_b", "filt_w1", "filt_b1", "filt_freq1",
        "filt_w2", "filt_b2", "filt_freq2", "filt_w3", "hy_skip", "w_up_hy", "w_up_attn", "w_gate", "b_gate",
        "w_out", "ln_x_g", "ln_mem_g", "w_q_x", "w_kv_mem", "w_o_x", "ln_moe_g", "w_router", "w_e_gate",
        "w_e_up", "w_e_down", "ln_f_g"]


def _constants():
    import math

    import numpy as np
    f = np.float32
    m, a = np.arange(P)[:, None], np.arange(NT)[None, :]
    t = 4 * m + a
    flat = t.T.reshape(-1)
    c = {"ident": np.eye(P, dtype=f)}
    tl = np.linspace(0.0, 1.0, SEQ, dtype=f)
    grid = (f(2.0 * math.pi) * np.arange(SEQ, dtype=f) / f(SEQ)).astype(f)
    bands = np.linspace(1e-4, 15, 16, dtype=f)
    arg = (bands[None, :] * grid[:, None]).astype(f)
    emb = np.concatenate([tl[:, None], np.cos(arg), -np.sin(arg)], axis=1).astype(f)
    c["embT"] = emb[flat].T
    deltas = np.linspace(math.log(1e-2) / 1.5, math.log(1e-2) / 0.3, HW, dtype=f)
    c["decay"] = np.exp(-tl[:, None] * np.abs(deltas)[None, :]).astype(f)[t]
    N, H = 2 * SEQ, SEQ // 2
    fr = np.arange(H)
    ang = 2 * np.pi * ((t[:, :, None] * fr) % N) / N
    quarter = 2 * np.pi * ((t * H) % N) / N
    even = (t % 2 == 0)
    co, si = np.cos(ang), np.sin(ang)
    sk = si[:, [0, 2], :P].copy()
    sk[:, :, 0] = 0.0
    si[:, :, 0] = np.where(even, np.cos(quarter), np.sin(quarter))
    c["dftc"], c["dfts"], c["dftsk"] = co, si, sk
    ia = 2 * np.pi * ((fr[:, None] * flat) % N) / N
    ic, isn = np.cos(ia) * 2 / N, np.sin(ia) * 2 / N
    ic[0] = 1.0 / N
    q = 2 * np.pi * ((flat * H) % N) / N
    isn[0] = np.where(flat % 2 == 0, -0.5 * np.cos(q), 0.5 * np.sin(q)) * 2 / N
    c["idftc"] = ic.reshape(2, P, SEQ).transpose(1, 0, 2)
    c["idfts"] = isn.reshape(2, P, SEQ).transpose(1, 0, 2)
    inv = (f(10000.0) ** (-np.arange(0, 64, 2, dtype=f) / f(64))).astype(f)
    ra = (t.astype(f)[:, :, None] * inv).astype(f)
    c["rcos"] = np.concatenate([np.cos(ra), np.cos(ra)], axis=2)
    c["rsin"] = np.concatenate([-np.sin(ra), np.sin(ra)], axis=2)
    ok0 = np.abs(t[:, :, None] - flat) <= 64
    rel = np.abs(np.arange(P)[:, None] - np.arange(P)[None, :])
    ok1 = np.repeat((rel <= 64)[:, None, :], NT, 1)
    ok2 = np.repeat((rel % 4 == 0)[:, None, :], NT, 1)
    c["mask"] = np.where(np.concatenate([ok0, ok1, ok2], axis=2), 0.0, -1e30)
    c["tval"] = t
    c["iota"] = np.repeat(flat[None, :], P, 0)
    return {k: np.ascontiguousarray(v.astype(f)) for k, v in c.items()}


_CONSTS = ["ident", "embT", "decay", "dftc", "dfts", "dftsk", "idftc", "idfts", "rcos", "rsin", "mask", "tval", "iota"]


def kernel(**inputs):
    import numpy as _np
    import concourse.bacc as _bacc
    from concourse import mybir as _mybir
    from concourse.bass_utils import run_bass_kernel_spmd as _run

    nc = _bacc.Bacc("TRN2", target_bir_lowering=False, num_devices=1)
    arrays, args = {}, []
    for name in _INS:
        arrays[f"in_{name}_dram"] = _np.ascontiguousarray(inputs[name])
    consts = _constants()
    for name in _CONSTS:
        arrays[f"c_{name}_dram"] = consts[name]
    for name, a in arrays.items():
        args.append(nc.dram_tensor(name, a.shape, _mybir.dt.from_np(a.dtype), kind="ExternalInput").ap())
    args.append(nc.dram_tensor("out_0_dram", (1, SEQ, D), F32, kind="ExternalOutput").ap())
    encoder_block(nc, *args)
    r = _run(nc, [arrays], core_ids=[0])
    return r.results[0]["out_0_dram"]
```

```python
from contextlib import ExitStack

import concourse.bass as bass
from concourse import mybir

F32 = mybir.dt.float32
U32 = mybir.dt.uint32
ALU = mybir.AluOpType
ACT = mybir.ActivationFunctionType
AX = mybir.AxisListType

P = 128
SEQ = 512
NT = SEQ // P
D = 1024
KD = D // P
MEM = 256
MT = MEM // P
EPS = 1e-6
HW = 768
HC = HW // P
HYT = 3 * HC
FFN = 64
EMB = 33
SLOTS_PER_HEAD = 4
GROUPS = 3
AW = GROUPS * SLOTS_PER_HEAD * 64
NKEY = SEQ + P + P
XH = 4
NE = 16
CAP = 2 * SEQ // NE
FF = 2048
CW = 256
RING = 8
RING0 = 3
CH = 256
NU = HW // CH
FB = FF // CW
TWO_PI = 6.283185307179586
MAGIC = 12582912.0
PI_A, PI_B = 6.28125, 0.0019350051879882812
PI_C = TWO_PI - PI_A - PI_B

V_MIX, V_X, V_MEM, V_MOE, V_BG, V_CB, V_SKIP = 0, 8, 16, 24, 32, 48, 66
V_ROWS = 78
V_CW = 78
V_COLS = V_CW + 54


def encoder_block(nc, x, mem, ln_mix_g, w_in, hy_conv_w, hy_conv_b, filt_w1, filt_b1, filt_freq1,
                  filt_w2, filt_b2, filt_freq2, filt_w3, hy_skip, w_up_hy, w_up_attn, w_gate, b_gate,
                  w_out, ln_x_g, ln_mem_g, w_q_x, w_kv_mem, w_o_x, ln_moe_g, w_router, w_e_gate,
                  w_e_up, w_e_down, ln_f_g,
                  c_ident, c_embT, c_decay, c_dftc, c_dfts, c_dftsk, c_idftc, c_idfts,
                  c_rcos, c_rsin, c_mask, c_tval, c_iota, out):
    ctx = ExitStack()
    with ctx:
        def sb(name, shape, dt=F32):
            return ctx.enter_context(nc.sbuf_tensor(name, shape, dt))

        def sem(name):
            return ctx.enter_context(nc.semaphore(name))

        ring = sb("ring", [P, RING, 2048])
        xs = sb("xs", [P, NT, D])
        hT = sb("hT", [P, KD, SEQ])
        UT = sb("UT", [P, 9216])
        W = sb("W", [P, 16896])
        attnT = sb("attnT", [P, 2, SEQ])
        ident = sb("ident", [P, P])
        vrow = W[:, 16384:16640].rearrange("p (a d) -> p a d", a=2)
        vcol = sb("vcol", [P, V_COLS])
        st = sb("st", [P, 64])
        fcol = sb("fcol", [FFN, 4])
        h2T = sb("h2T", [P, SEQ])

        uT = UT[:, :].rearrange("p (m t) -> p m t", t=SEQ)
        embT = UT[0:EMB, 0:512]
        fw1 = UT[0:EMB, 512:576]
        fw2 = UT[0:FFN, 576:640]
        farg = UT[0:FFN, 1024:1536]
        fk = UT[0:FFN, 1536:2048]
        h1T = UT[0:FFN, 2048:2560]

        hn = W[:, 0:4096].rearrange("p (a d) -> p a d", a=NT)
        vnat = W[:, 0:3072].rearrange("p (a c) -> p a c", a=NT)
        spare = ring[:, RING0:RING, :].rearrange("p s c -> p (s c)")
        qz = spare[:, 0:6144].rearrange("p (g h t) -> p g h t", g=GROUPS, h=SLOTS_PER_HEAD)
        kT = W[:, 6144:9216].rearrange("p (g r t) -> p g r t", g=GROUPS, r=2)
        masks = W[:, 9216:12288].rearrange("p (a k) -> p a k", a=NT)
        Sb = W[:, 12288:13824].rearrange("p (b k) -> p b k", b=2)
        PTb = W[:, 13824:15360].rearrange("p (b k) -> p b k", b=2)
        anat = W[:, 15360:15872].rearrange("p (b k) -> p b k", b=2)
        rcos = W[:, 15872:16128].rearrange("p (a k) -> p a k", a=NT)
        rsin = W[:, 16128:16384].rearrange("p (a k) -> p a k", a=NT)
        ropeA = W[:, 12288:12544]
        ropeB = W[:, 12544:12800]
        rope_out = W[:, 12800:13312].rearrange("p (b k) -> p b k", b=2)
        dftc = W[:, 0:1024].rearrange("p (a f) -> p a f", a=NT)
        dfts = W[:, 1024:2048].rearrange("p (a f) -> p a f", a=NT)
        idftc = W[:, 2048:3072].rearrange("p (j t) -> p j t", j=2)
        idfts = W[:, 3072:4096].rearrange("p (j t) -> p j t", j=2)
        dftsk = W[:, 4096:4352].rearrange("p (a f) -> p a f", a=2)
        Kb = [[W[:, 4352 + 2048 * b + 512 * i:4864 + 2048 * b + 512 * i].rearrange("p (j c) -> p j c", j=2)
               for i in range(4)] for b in range(2)]
        Zb = [W[:, 8448 + 512 * i:8960 + 512 * i].rearrange("p (j c) -> p j c", j=2) for i in range(4)]
        ff = W[:, 10496:11520].rearrange("p (a c) -> p a c", a=NT)
        fb = W[:, 11520:12544].rearrange("p (a c) -> p a c", a=NT)
        fs = W[:, 12544:13568].rearrange("p (a c) -> p a c", a=NT)
        gates = spare[:, 0:8192].rearrange("p (i t) -> p i t", i=2 * KD)
        znat = spare[:, 8192:9216].rearrange("p (a c) -> p a c", a=NT)
        t1 = W[:, 13568:14080].rearrange("p (j c) -> p j c", j=2)
        t2 = W[:, 14080:14592].rearrange("p (j c) -> p j c", j=2)
        t3 = W[:, 14592:15104].rearrange("p (j c) -> p j c", j=2)
        dec = W[:, 15104:16128].rearrange("p (a c) -> p a c", a=NT)
        w3u = W[:, 16128:16640].rearrange("p (d c) -> p d c", d=2)
        ZP = Zb
        EV = lambda B: (B[2], B[1])
        mixT = W[:, 0:4096].rearrange("p (m t) -> p m t", m=KD)
        mt = W[:, 6144:7168].rearrange("p (s t) -> p s t", s=2)
        mems = W[:, 7168:9216].rearrange("p (a d) -> p a d", a=MT)
        mnT = W[:, 9216:11264].rearrange("p (k t) -> p k t", k=KD)
        mhn = W[:, 11264:13312].rearrange("p (a d) -> p a d", a=MT)
        kxT = W[:, 13312:14336].rearrange("p (h t) -> p h t", h=XH)
        vx = W[:, 14336:15360].rearrange("p (b c) -> p b c", b=MT)
        qxT = UT[:, 0:2048].rearrange("p (h t) -> p h t", h=XH)
        oxT = UT[:, 2048:4096].rearrange("p (h t) -> p h t", h=XH)
        Px = UT[:, 4096:6144].rearrange("p (b a t) -> p b a t", b=2, a=NT)
        PTx = UT[:, 6144:8192].rearrange("p (b s t) -> p b s t", b=2, s=2)
        wua = UT[:, 3072:5120].rearrange("p (k c) -> p k c", k=2)
        hT_out = lambda a: hT[:, :, :].rearrange("p k t -> p (k t)")[:, a * D:(a + 1) * D]
        bidx = W[:, 4096:5120]
        Pg = W[:, 5120:5632].rearrange("p (a s) -> p a s", a=NT)
        PT = W[:, 5632:6656].rearrange("p (h t) -> p h t", h=2)
        Y = W[:, 6656:7680].rearrange("p (h c) -> p h c", h=2)
        iota = W[:, 8192:8704]
        xeT = W[:, 8704:9728].rearrange("p (k s) -> p k s", k=KD)
        sil = W[0:CAP, 9728:10240].rearrange("p (b f) -> p b f", b=2)
        hh = W[0:CAP, 10240:10752].rearrange("p (b f) -> p b f", b=2)
        hhT = W[:, 10752:11008].rearrange("p (b i s) -> p b i s", b=2, i=2)
        gf = W[:, 11520:12544]
        wr = sb("wr", [P, KD, NE])
        aff = W[:, 12544:12608].rearrange("p (a e) -> p a e", a=NT)
        lg = W[:, 12608:12672].rearrange("p (a e) -> p a e", a=NT)
        affT = W[0:NE, 12672:13184]
        topv = W[0:NE, 13184:13312].rearrange("p (r s) -> p r s", r=2)
        topi = W[0:NE, 13312:13376].bitcast(U32)
        topf = W[0:NE, 13376:13504].rearrange("p (r s) -> p r s", r=2)
        bdiag = W[0:NE, 13504:14528].rearrange("p (e s) -> p e s", e=NE)
        ones16 = W[0:NE, 14528:14656]
        gcol = W[:, 14656:14672]
        icol = W[:, 14672:14688].rearrange("p (h q) -> p h q", h=2)
        tval = W[:, 14688:14692]

        ps = ctx.enter_context(nc.psum_tensor("ps", [P, 8, 512], F32))

        def psc(b0, b1, n):
            return ps[:, b0:b1, :].rearrange("p b c -> p (b c)")[:, 0:n]

        ld_ident, ld_vec, ld_filt, ld_rope, ld_mask = (sem(n) for n in (
            "ld_ident", "ld_vec", "ld_filt", "ld_rope", "ld_mask"))
        ld_dft, ld_dec, ld_w3, ld_mem, ld_wr, ld_moe, ld_gf, ld_wua = (sem(n) for n in (
            "ld_dft", "ld_dec", "ld_w3", "ld_mem", "ld_wr", "ld_moe", "ld_gf", "ld_wua"))
        ld_x = [sem(f"ld_x{a}") for a in range(NT)]
        spare_zero, gate_full, gate_done = sem("spare_zero"), sem("gate_full"), sem("gate_done")
        slot_loaded = [sem(f"slot{i}_loaded") for i in range(RING)]
        vec_turned, vec_ready = sem("vec_turned"), sem("vec_ready")
        mlp_mm, mlp_arg, mlp_sin = sem("mlp_mm"), sem("mlp_arg"), sem("mlp_sin")
        chain = sem("dve_chain")
        pchain = sem("pool_chain")
        norms = {}
        for tag in ("mix", "mem", "xa", "moe", "fin"):
            norms[tag] = {n: sem(f"{tag}_{n}") for n in ("sq", "var", "sqrt", "scaled", "turned", "evA", "evV")}
        qkv_full, v_copied, roped, qk_turned, qk_copied = (sem(n) for n in (
            "qkv_full", "v_copied", "roped", "qk_turned", "qk_copied"))
        s_full, s_masked, s_negmax, s_exp, p_turned, p_copied, o_full, o_scaled, at_turned, at_copied = (sem(n) for n in (
            "s_full", "s_masked", "s_negmax", "s_exp", "p_turned", "p_copied", "o_full", "o_scaled",
            "at_turned", "at_copied"))
        hy_full, hy_centre, hy_conv = sem("hy_full"), sem("hy_centre"), sem("hy_conv")
        f_full, f_copied, f_sumdif, k_full, k_even, k_ready = (sem(n) for n in (
            "f_full", "f_copied", "f_sumdif", "k_full", "k_even", "k_ready"))
        z_turned, z_copied, z_full, z_even, z_ready, prod, y_full, z_new = (sem(n) for n in (
            "z_turned", "z_copied", "z_full", "z_even", "z_ready", "prod", "y_full", "z_new"))
        mix_full, mix_done = sem("mix_full"), sem("mix_done")
        out_full, out_added = sem("out_full"), sem("out_added")
        kv_full, kv_copied, qx_full, qx_copied = (sem(n) for n in ("kv_full", "kv_copied", "qx_full", "qx_copied"))
        sx_full, sx_negmax, sx_exp, sx_norm, px_turned, px_copied, ox_full, ox_copied, xo_full, xo_added = (sem(n) for n in (
            "sx_full", "sx_negmax", "sx_exp", "sx_norm", "px_turned", "px_copied", "ox_full", "ox_copied",
            "xo_full", "xo_added"))
        r_full, r_negmax, r_exp, r_aff, r_turned, r_affT, top_done, sel_turned, sel_cols, sel_bcast, pg_ready = (sem(n) for n in (
            "r_full", "r_negmax", "r_exp", "r_aff", "r_turned", "r_affT", "top_done", "sel_turned", "sel_cols",
            "sel_bcast", "pg_ready"))
        xe_full, xe_ready, ab_full, silu_done, hh_ready, hh_turned, hhT_ready, y_step, ye_ready, pt_ready, sc_full, sc_added = (sem(n) for n in (
            "xe_full", "xe_ready", "ab_full", "silu_done", "hh_ready", "hh_turned", "hhT_ready", "y_step",
            "ye_ready", "pt_ready", "sc_full", "sc_added"))
        out_written = sem("out_written")

        def cols(w, c0, k=KD, n=CW):
            return (lambda s: ring[:, s, 0:k * n].rearrange("p (k c) -> p k c", k=k),
                    w.rearrange("(k p) c -> p k c", p=P)[:, :, c0:c0 + n])

        chunks = []
        QKV0 = 3 * HW
        for g in range(GROUPS):
            for part in range(3):
                n = len(chunks)
                chunks.append(cols(w_in, QKV0 + part * AW + g * CW) + (qkv_full, 4 * (n + 1)))
        HY_C = len(chunks)
        for j in range(HYT // 2):
            chunks.append(cols(w_in, j * CW) + (hy_full, 2 * (j + 1)))
        GATE_C = len(chunks)
        for j in range(KD):
            chunks.append(cols(w_gate, j * CW) + (gate_full, 2 * (j + 1)))
        MIX_C = len(chunks)
        for j in range(4):
            chunks.append(cols(w_up_hy, j * CW, HC) + (mix_full, 2 * (j + 1)))
        OUT_C = len(chunks)
        for j in range(4):
            chunks.append(cols(w_out, j * CW) + (out_full, 4 * (j + 1)))
        KV_C = len(chunks)
        for j in range(4):
            chunks.append(cols(w_kv_mem, j * CW) + (kv_full, 2 * (j + 1)))
        QX_C = len(chunks)
        for j in range(2):
            chunks.append(cols(w_q_x, j * CW) + (qx_full, 2 * (j + 1)))
        XO_C = len(chunks)
        for j in range(2):
            chunks.append(cols(w_o_x, j * 512, 4, 512) + (xo_full, 4 * (j + 1)))
        MOE_C = len(chunks)
        STEP = 3 * FB
        assert MOE_C % RING0 == 0
        assert STEP % RING == 0

        slots, loads, before = [], [], []
        for n in range(MOE_C + 2 * RING):
            k = n % RING0 if n < MOE_C else (n - MOE_C + RING0) % RING
            earlier = [i for i in range(n) if slots[i] == k]
            slots.append(k)
            loads.append(len(earlier) + 1)
            before.append(earlier[-1] if earlier else None)

        def slot(n):
            return slots[n] if n < MOE_C else (n - MOE_C + RING0) % RING

        def load_count(n):
            if n < MOE_C + RING:
                return loads[n]
            return loads[MOE_C + (n - MOE_C) % RING] + (n - MOE_C) // RING

        def arrived(eng, n):
            eng.wait_ge(slot_loaded[slot(n)], 16 * load_count(n))

        def wview(n, k=KD, c=CW):
            return ring[:, slot(n), 0:k * c].rearrange("p (k c) -> p k c", k=k)

        block = ctx.enter_context(nc.Block())

        @block.sync
        def _(sp):
            sp.wait_ge(ld_x[NT - 1], 16)
            def expert_chunk(e, i):
                j, part = i // 3, i % 3
                dst = ring[:, slot(MOE_C + i), :]
                if part < 2:
                    w = (w_e_gate, w_e_up)[part]
                    src = w[e].rearrange("(k p) f -> p k f", p=P)[:, :, j * CW:(j + 1) * CW]
                    dst = dst.rearrange("p (k c) -> p k c", k=KD)
                else:
                    src = w_e_down[e, j * CW:(j + 1) * CW, :].rearrange("(k p) d -> p k d", p=P)
                    dst = dst.rearrange("p (k c) -> p k c", k=2)
                sp.dma_start(dst, src).then_inc(slot_loaded[slot(MOE_C + i)], 16)

            def freed_in_expert(i, base):
                j, part = i // 3, i % 3
                if part < 2:
                    sp.wait_ge(ab_full, base + j + 1)
                else:
                    sp.wait_ge(y_step, base + j + 1)

            for n, (dst, src, _, _) in enumerate(chunks):
                if n >= RING0:
                    sp.wait_ge(chunks[n - RING0][2], chunks[n - RING0][3])
                sp.dma_start(dst(slot(n)), src).then_inc(slot_loaded[slot(n)], 16)
                if n == OUT_C + RING0:
                    sp.wait_ge(mix_done, KD)
                    for i in range(RING - RING0):
                        expert_chunk(0, i)
            for i in range(RING - RING0, STEP):
                if i < RING:
                    c = MOE_C - RING + i
                    assert slot(c) == slot(MOE_C + i) and c + RING0 >= MOE_C
                    sp.wait_ge(chunks[c][2], chunks[c][3])
                else:
                    freed_in_expert(i - RING, 0)
                expert_chunk(0, i)
            with sp.Fori(1, NE) as e:
                for i in range(STEP):
                    if i < RING:
                        freed_in_expert(STEP - RING + i, (e - 1) * FB)
                    else:
                        freed_in_expert(i - RING, e * FB)
                    expert_chunk(e, i)
            for a in range(NT):
                sp.wait_ge(norms["fin"]["scaled"], a + 1)
                sp.dma_start(out[0].rearrange("(m a) d -> m a d", a=NT)[:, a, :], hT_out(a)).then_inc(out_written, 16)
            sp.wait_ge(out_written, 16 * NT)

        @block.gpsimd
        def _(pool):
            nc.gpsimd.memset(spare[:, 0:6144], 0.0).then_inc(spare_zero, 1)
            pool.wait_ge(spare_zero, 1)
            nc.gpsimd.memset(h2T[FFN:P, :], 0.0).then_inc(spare_zero, 1)
            pool.wait_ge(spare_zero, 2)
            pool.dma_start(vrow[0:8, 0, :], ln_mix_g.rearrange("(k p) -> k p", p=P)).then_inc(ld_vec, 16)
            pool.dma_start(vrow[8:16, 0, :], ln_x_g.rearrange("(k p) -> k p", p=P)).then_inc(ld_vec, 16)
            pool.dma_start(vrow[16:24, 0, :], ln_mem_g.rearrange("(k p) -> k p", p=P)).then_inc(ld_vec, 16)
            pool.dma_start(vrow[24:32, 0, :], ln_moe_g.rearrange("(k p) -> k p", p=P)).then_inc(ld_vec, 16)
            pool.dma_start(vrow[32:48, 0, :], b_gate.rearrange("(k p) -> k p", p=P)).then_inc(ld_vec, 16)
            pool.dma_start(vrow[48:66, 0, :], hy_conv_b.rearrange("(k p) -> k p", p=P)).then_inc(ld_vec, 16)
            pool.dma_start(vrow[66:78, 0, :], hy_skip.rearrange("o (k p) -> (o k) p", p=P)).then_inc(ld_vec, 16)
            pool.dma_start(vrow[0:54, 1, :], hy_conv_w.rearrange("s (k p) -> (s k) p", p=P)).then_inc(ld_vec, 16)
            pool.dma_start(wr[:, :, :], w_router.rearrange("(k p) e -> p k e", p=P)).then_inc(ld_wr, 16)
            pool.dma_start(rcos, c_rcos).then_inc(ld_rope, 16)
            pool.dma_start(rsin, c_rsin).then_inc(ld_rope, 16)
            pool.dma_start(masks, c_mask).then_inc(ld_mask, 16)
            pool.wait_ge(at_copied, NT)
            for dst, src in ((dftc, c_dftc), (dfts, c_dfts), (dftsk, c_dftsk), (idftc, c_idftc), (idfts, c_idfts)):
                pool.dma_start(dst, src).then_inc(ld_dft, 16)
            nc.gpsimd.memset(w3u[FFN:P, :, :], 0.0).then_inc(spare_zero, 1)
            pool.wait_ge(spare_zero, 3)
            w3v = filt_w3.rearrange("k (o d c) -> k o d c", o=2, d=2)
            for u in range(2 * NU):
                o, th = u // NU, u % NU
                if u >= 1:
                    pool.wait_ge(f_full, 4 * u)
                pool.dma_start(w3u[0:FFN, :, :], w3v[:, o, :, th * CH:(th + 1) * CH]).then_inc(ld_w3, 16)
                if u >= 1:
                    pool.wait_ge(pchain, 4 * u)
                pool.dma_start(dec, c_decay[:, :, th * CH:(th + 1) * CH]).then_inc(ld_dec, 16)
                pool.wait_ge(ld_dec, 16 * (u + 1))
                pool.wait_ge(f_copied, 4 * (u + 1))
                if u >= 1:
                    pool.wait_ge(k_full, 4 * u)
                nc.gpsimd.tensor_tensor(ff, ff, dec, ALU.mult).then_inc(pchain, 1)
                link_n = 4 * u + 2
                nc.gpsimd.tensor_tensor(fb, fb, dec, ALU.mult).then_inc(pchain, 1)
                pool.wait_ge(pchain, link_n)
                nc.gpsimd.memset(fb[0:1, 0, :], 0.0).then_inc(pchain, 1)
                pool.wait_ge(pchain, link_n + 1)
                nc.gpsimd.tensor_tensor(fs, ff, fb, ALU.add).then_inc(pchain, 1)
                pool.wait_ge(pchain, link_n + 2)
                nc.gpsimd.tensor_tensor(ff, ff, fb, ALU.subtract).then_inc(f_sumdif, 1)
            pool.wait_ge(z_new, 2 * NU)
            pool.dma_start(wua, w_up_attn.rearrange("(k p) c -> p k c", p=P)).then_inc(ld_wua, 16)
            pool.wait_ge(prod, 2 * NU)
            pool.wait_ge(y_full, 2 * HC)
            pool.dma_start(mems, mem[0].rearrange("(m b) d -> m b d", b=MT)).then_inc(ld_mem, 16)
            pool.wait_ge(ox_full, XH)
            pool.wait_ge(xo_full, 8)
            pool.dma_start(iota, c_iota).then_inc(ld_moe, 16)
            pool.dma_start(tval, c_tval).then_inc(ld_moe, 16)
            pool.dma_start(gf, ln_f_g.partition_broadcast(P)).then_inc(ld_gf, 16)

        def gate_tiles(u):
            per = [3, 3, 3, 3, 2, 2]
            return sum(per[:u]), sum(per[:u + 1])

        junk = UT[:, 5120:6144]

        def norm_scalar(act, tag, src, n, pieces, ready):
            s = norms[tag]
            w = D // pieces
            for i in range(n * pieces):
                j, a = i // n, i % n
                ready(a, j)
                if i >= 1:
                    act.wait_ge(s["sq"], i)
                c = a * pieces + j
                nc.scalar.activation(junk[:, 0:w], src[:, a, j * w:(j + 1) * w], ACT.Square,
                                     accum_out=st[:, c:c + 1]).then_inc(s["sq"], 1)
            act.wait_ge(s["var"], 1)
            nc.scalar.activation(st[:, 20:20 + n], st[:, 16:16 + n], ACT.Sqrt).then_inc(s["sqrt"], 1)

        def norm_vector(dve, link, tag, src, dst, n, pieces):
            s = norms[tag]
            dve.wait_ge(s["sq"], n * pieces)
            r, v, t = st[:, 24:24 + n], st[:, 16:16 + n], st[:, 28:28 + n]
            if pieces > 1:
                link(nc.vector.tensor_reduce(t, st[:, 0:n * pieces].rearrange("p (a j) -> p a j", a=n), AX.X, ALU.add))
                nc.vector.tensor_scalar(v, t, 1.0 / D, EPS, ALU.mult, ALU.add).then_inc(s["var"], 1)
            else:
                nc.vector.tensor_scalar(v, st[:, 0:n], 1.0 / D, EPS, ALU.mult, ALU.add).then_inc(s["var"], 1)
            dve.wait_ge(s["sqrt"], 1)
            link(nc.vector.reciprocal(r, st[:, 20:20 + n]))
            link(nc.vector.tensor_tensor(t, r, r, ALU.mult))
            link(nc.vector.tensor_tensor(t, t, v, ALU.mult))
            link(nc.vector.tensor_scalar(t, t, -0.5, 1.5, ALU.mult, ALU.add))
            link(nc.vector.tensor_tensor(r, r, t, ALU.mult))
            if dst is not None:
                for a in range(n):
                    nc.vector.tensor_scalar(dst[:, a, :], src[:, a, :], st[:, 24 + a:25 + a], None,
                                            ALU.mult).then_inc(s["scaled"], 1)

        def norm_tensor(pe, tag, src, n, bank0):
            s = norms[tag]
            pe.wait_ge(s["scaled"], n)
            for k in range(KD):
                if k >= 4:
                    pe.wait_ge(s["evA" if k % 2 == 0 else "evV"], k // 2 - 1)
                for a in range(n):
                    mm = pe.transpose(ps[:, bank0 + k % 4, a * P:(a + 1) * P], src[:, a, k * P:(k + 1) * P], ident[:, :])
                mm.then_inc(s["turned"], 1)

        def norm_evac(eng, tag, dst, n, bank0, col, par):
            s = norms[tag]
            for k in range(par, KD, 2):
                eng.wait_ge(s["turned"], k + 1)
                src = ps[:, bank0 + k % 4, 0:n * P]
                if par == 0:
                    nc.scalar.activation(dst[:, k, :], src, ACT.Copy, scale=vcol[:, col + k:col + k + 1]).then_inc(s["evA"], 1)
                else:
                    nc.vector.tensor_scalar(dst[:, k, :], src, vcol[:, col + k:col + k + 1], None,
                                            ALU.mult).then_inc(s["evV"], 1)

        @block.scalar
        def _(act):
            for a in range(NT):
                act.dma_start(xs[:, a, :], x[0].rearrange("(m a) d -> m a d", a=NT)[:, a, :]).then_inc(ld_x[a], 16)
            act.dma_start(ident[:, :], c_ident).then_inc(ld_ident, 16)
            act.dma_start(embT, c_embT).then_inc(ld_filt, 16)
            act.dma_start(fw1, filt_w1).then_inc(ld_filt, 16)
            act.dma_start(fw2, filt_w2).then_inc(ld_filt, 16)
            for i, v in enumerate((filt_b1, filt_freq1, filt_b2, filt_freq2)):
                act.dma_start(fcol[:, i:i + 1], v.rearrange("(p o) -> p o", o=1)).then_inc(ld_filt, 16)

            norm_scalar(act, "mix", xs, NT, 1, lambda a, j: act.wait_ge(ld_x[a], 16))
            act.wait_ge(vec_ready, 2)
            norm_evac(act, "mix", hT, NT, 0, V_MIX, 0)
            for i, dst in enumerate((h1T, h2T[0:FFN, :])):
                act.wait_ge(mlp_arg, i + 1)
                nc.scalar.activation(dst, farg, ACT.Sin).then_inc(mlp_sin, 1)

            for c in range(9):
                g, part = c // 3, c % 3
                for a in range(NT):
                    n = 4 * c + a
                    if part == 2:
                        act.wait_ge(qkv_full, n + 1)
                        nc.scalar.copy(vnat[:, a, g * CW:(g + 1) * CW], ps[:, n % 4, 0:CW]).then_inc(v_copied, 1)
                    else:
                        m = 8 * g + 4 * part + a
                        act.wait_ge(qk_turned, m + 1)
                        src = ps[:, 4 + m % 4, 0:2 * P].rearrange("p (r t) -> p r t", r=2)
                        if part == 0:
                            act.wait_ge(spare_zero, 1)
                            nc.scalar.copy(qz[0:64, g, 0:4:2, a * P:(a + 1) * P], src[0:64])
                            nc.scalar.copy(qz[64:P, g, 1:4:2, a * P:(a + 1) * P], src[64:P]).then_inc(qk_copied, 1)
                        else:
                            nc.scalar.copy(kT[:, g, :, a * P:(a + 1) * P], src).then_inc(qk_copied, 1)

            def centre(m):
                act.wait_ge(hy_full, m + 1)
                nc.scalar.activation(uT[:, m, :], ps[:, m % 2, :], ACT.Identity, bias=vcol[:, V_CB + m:V_CB + m + 1],
                                     scale=vcol[:, V_CW + HYT + m:V_CW + HYT + m + 1]).then_inc(hy_centre, 1)

            for p in range(16):
                act.wait_ge(s_negmax, p + 1)
                nc.scalar.activation(Sb[:, p % 2, :], Sb[:, p % 2, :], ACT.Exp, bias=st[:, 34 + p % 2:35 + p % 2],
                                     accum_out=st[:, 36 + p % 2:37 + p % 2]).then_inc(s_exp, 1)
                if p == 0:
                    act.wait_ge(mlp_sin, 2)
                    act.wait_ge(norms["mix"]["evA"], 4)
                centre(p)
                act.wait_ge(p_turned, p + 1)
                if p >= 2:
                    act.wait_ge(o_full, p - 1)
                nc.scalar.copy(PTb[:, p % 2, :], psc(4, 6, NKEY)).then_inc(p_copied, 1)
            centre(16)
            centre(17)

            def filter_copies(u):
                for d, dst in ((0, ff), (1, fb)):
                    for j in range(2):
                        i = 4 * u + 2 * d + j
                        act.wait_ge(f_full, i + 1)
                        if u >= 1 and d == 0 and j == 0:
                            act.wait_ge(k_full, 4 * u)
                        if u >= 1 and d == 1 and j == 0:
                            act.wait_ge(f_sumdif, u)
                        nc.scalar.copy(dst[:, 2 * j:2 * j + 2, :], ps[:, 4 + i % 4, :].rearrange(
                            "p (a c) -> p a c", a=2)).then_inc(f_copied, 1)

            def even_copies(full, base, bank0, bufs, done):
                for i in range(4):
                    act.wait_ge(full, base + i + 1)
                    nc.scalar.copy(bufs[i % 2][:, i // 2, :], ps[:, bank0 + i, 0:CH]).then_inc(done, 1)

            def z_copies(u):
                o, th = u // NU, u % NU
                if u >= 1:
                    act.wait_ge(z_full, 4 * u)
                for a in range(NT):
                    act.wait_ge(z_turned, 4 * u + a + 1)
                    nc.scalar.copy(znat[:, a, :], ps[:, a, 0:CH]).then_inc(z_copied, 1)

            filter_copies(0)
            z_copies(0)
            even_copies(k_full, 0, 4, EV(Kb[0]), k_even)
            filter_copies(1)
            for u in range(2 * NU):
                if u >= 1:
                    act.wait_ge(prod, u)
                even_copies(z_full, 4 * u, 0, EV(Zb), z_even)
                if u + 1 < 2 * NU:
                    if u >= 1:
                        act.wait_ge(y_full, 2 * u)
                    even_copies(k_full, 4 * (u + 1), 4, EV(Kb[(u + 1) % 2]), k_even)
                for i in range(*gate_tiles(u)):
                    act.wait_ge(gate_full, i + 1)
                    nc.scalar.activation(gates[:, i, :], ps[:, 2 + i % 2, :], ACT.Sigmoid,
                                         bias=vcol[:, V_BG + i:V_BG + i + 1]).then_inc(gate_done, 1)
                if u + 1 < 2 * NU:
                    z_copies(u + 1)
                if u + 2 < 2 * NU:
                    filter_copies(u + 2)

            norm_scalar(act, "mem", mems, MT, 1, lambda a, j: act.wait_ge(ld_mem, 16))
            norm_evac(act, "mem", mnT, MT, 0, V_MEM, 0)
            norm_scalar(act, "xa", xs, NT, 4, lambda a, j: act.wait_ge(out_added, 4 * j + a + 1))
            for i in range(8):
                act.wait_ge(kv_full, i + 1)
                if i < 4:
                    nc.scalar.copy(kxT[:, i, :], ps[:, 4 + i % 4, 0:MEM]).then_inc(kv_copied, 1)
                else:
                    j, b = (i - 4) // 2, i % 2
                    nc.scalar.copy(vx[:, b, j * CW:(j + 1) * CW], ps[:, 4 + i % 4, 0:CW]).then_inc(kv_copied, 1)
            norm_evac(act, "xa", hT, NT, 0, V_X, 0)
            for h in range(XH):
                act.wait_ge(qx_full, h + 1)
                nc.scalar.copy(qxT[:, h, :], ps[:, 4 + h, :]).then_inc(qx_copied, 1)
            for h in range(XH):
                for a in range(NT):
                    act.wait_ge(sx_negmax, 4 * h + 2 * (a // 2) + 2)
                    if h >= 2 and a == 0:
                        act.wait_ge(px_turned, 2 * (h - 1))
                    c = 40 + (h % 2) * 4 + a
                    nc.scalar.activation(Px[:, h % 2, a, :], ps[:, 2 * (h % 2) + a // 2, (a % 2) * MEM:(a % 2 + 1) * MEM],
                                         ACT.Exp, bias=st[:, c:c + 1], scale=float(P) ** -0.5,
                                         accum_out=st[:, c + 8:c + 9]).then_inc(sx_exp, 1)
                act.wait_ge(px_turned, 2 * h + 2)
                if h >= 2:
                    act.wait_ge(ox_full, h - 1)
                nc.scalar.copy(PTx[:, h % 2, :, :], ps[:, 4:6, :]).then_inc(px_copied, 1)
                act.wait_ge(ox_full, h + 1)
                nc.scalar.copy(oxT[:, h, :], ps[:, 6, :]).then_inc(ox_copied, 1)
            norm_scalar(act, "moe", xs, NT, 2, lambda a, j: act.wait_ge(xo_added, 4 * j + a + 1))
            norm_evac(act, "moe", hT, NT, 0, V_MOE, 0)
            for a in range(NT):
                act.wait_ge(r_negmax, a + 1)
                nc.scalar.activation(lg[:, a, :], ps[:, 4 + a, 0:NE], ACT.Exp, bias=st[:, 40 + a:41 + a],
                                     accum_out=st[:, 44 + a:45 + a]).then_inc(r_exp, 1)
            with act.Fori(0, NE) as e:
                for j in range(FB):
                    act.wait_ge(ab_full, e * FB + (j + 1))
                    nc.scalar.activation(sil[:, j % 2, :], ps[0:CAP, j % 2, 0:CW], ACT.Silu).then_inc(silu_done, 1)
            last = NE * 4 - 8
            norm_scalar(act, "fin", xs, NT, 1, lambda a, j: act.wait_ge(sc_added, last + 2 * a + 2))

        @block.tensor
        def _(pe):
            def product(out_, pairs):
                last = len(pairs) - 1
                for i, (l, r) in enumerate(pairs):
                    mm = pe.matmul(out_, l, r, start=i == 0, stop=i == last)
                return mm

            pe.wait_ge(ld_ident, 16)
            pe.wait_ge(ld_vec, 16 * 8)
            pe.transpose(ps[:, 6, 0:V_ROWS], vrow[0:V_ROWS, 0, :], ident[0:V_ROWS, 0:V_ROWS]).then_inc(vec_turned, 1)
            pe.transpose(ps[:, 7, 0:54], vrow[0:54, 1, :], ident[0:54, 0:54]).then_inc(vec_turned, 1)
            pe.wait_ge(ld_filt, 16 * 7)
            pe.matmul(ps[0:FFN, 5, :], fw1, embT, start=True, stop=True).then_inc(mlp_mm, 1)
            norm_tensor(pe, "mix", hn, NT, 0)
            pe.wait_ge(mlp_sin, 1)
            pe.matmul(ps[0:FFN, 5, :], fw2, h1T, start=True, stop=True).then_inc(mlp_mm, 1)

            pe.wait_ge(norms["mix"]["evA"], 4)
            pe.wait_ge(norms["mix"]["evV"], 4)

            def turn_heads(m):
                pe.wait_ge(roped, m + 1)
                if m >= 4:
                    pe.wait_ge(qk_copied, m - 3)
                else:
                    pe.wait_ge(mlp_arg, 2)
                for r in range(2):
                    mm = pe.transpose(ps[:, 4 + m % 4, r * P:(r + 1) * P], rope_out[:, m % 2, r * P:(r + 1) * P], ident[:, :])
                mm.then_inc(qk_turned, 1)

            done = 0
            for c in range(9):
                g, part = c // 3, c % 3
                arrived(pe, c)
                for a in range(NT):
                    n = 4 * c + a
                    if n >= 4:
                        c4, a4 = c - 1, a
                        if c4 % 3 == 2:
                            pe.wait_ge(v_copied, 4 * (c4 // 3) + a4 + 1)
                        else:
                            pe.wait_ge(roped, 8 * (c4 // 3) + 4 * (c4 % 3) + a4 + 1)
                    product(ps[:, n % 4, 0:CW], [(hT[:, k, a * P:(a + 1) * P], wview(c)[:, k, :]) for k in range(KD)]
                            ).then_inc(qkv_full, 1)
                    if part < 2:
                        m = 8 * g + 4 * part + a
                        if m > done:
                            turn_heads(done)
                            done += 1
                    elif a == 0:
                        turn_heads(done)
                        done += 1

            def scores(p):
                a, h = p // 4, p % 4
                r = h // 2
                if p == 0:
                    pe.wait_ge(qk_copied, 24)
                    pe.wait_ge(v_copied, 12)
                    pe.wait_ge(roped, 24)
                else:
                    pe.wait_ge(s_masked, p)
                pe.matmul(ps[:, 2, :], qz[:, 0, h, a * P:(a + 1) * P], kT[:, 0, r, :], start=True, stop=True)
                for g in (1, 2):
                    mm = pe.matmul(ps[:, 3, (g - 1) * P:g * P], qz[:, g, h, a * P:(a + 1) * P], kT[:, g, r, a * P:(a + 1) * P],
                                   start=True, stop=True)
                mm.then_inc(s_full, 1)

            def hyena_tile(m):
                if m % 2 == 0:
                    arrived(pe, HY_C + m // 2)
                if m >= 2:
                    pe.wait_ge(hy_conv, m - 1)
                c0 = (m % 2) * P
                product(ps[:, m % 2, :], [(wview(HY_C + m // 2)[:, k, c0:c0 + P], hT[:, k, :]) for k in range(KD)]
                        ).then_inc(hy_full, 1)

            def turn_probs(p):
                pe.wait_ge(s_exp, p + 1)
                if p >= 1:
                    pe.wait_ge(p_copied, p)
                for i in range(6):
                    mm = pe.transpose(ps[:, 4 + i // 4, (i % 4) * P:(i % 4 + 1) * P], Sb[:, p % 2, i * P:(i + 1) * P], ident[:, :])
                mm.then_inc(p_turned, 1)

            def values(p):
                a, h = p // 4, p % 4
                pe.wait_ge(p_copied, p + 1)
                if p >= 1:
                    pe.wait_ge(o_scaled, p)
                keys = [(0, b) for b in range(NT)] + [(1, a), (2, a)]
                product(ps[:, 6, 0:64], [(PTb[:, p % 2, i * P:(i + 1) * P], vnat[:, b, g * CW + h * 64:g * CW + h * 64 + 64])
                                         for i, (g, b) in enumerate(keys)]).then_inc(o_full, 1)

            def turn_attn(a):
                pe.wait_ge(o_scaled, 4 * a + 4)
                if a >= 1:
                    pe.wait_ge(at_copied, a)
                for r in range(2):
                    mm = pe.transpose(ps[:, 7, r * P:(r + 1) * P], anat[:, a % 2, r * P:(r + 1) * P], ident[:, :])
                mm.then_inc(at_turned, 1)

            scores(0)
            for p in range(16):
                hyena_tile(p)
                turn_probs(p)
                if p + 1 < 16:
                    scores(p + 1)
                if p % 4 == 0 and p > 0:
                    turn_attn(p // 4 - 1)
                values(p)
            hyena_tile(16)
            turn_attn(3)
            hyena_tile(17)

            def filter_time(u):
                pe.wait_ge(ld_w3, 16 * (u + 1))
                if u == 0:
                    pe.wait_ge(spare_zero, 3)
                for d in range(2):
                    for j in range(2):
                        i = 4 * u + 2 * d + j
                        if u >= 1:
                            pe.wait_ge(k_ready, 4 * u)
                        elif i == 0:
                            pe.wait_ge(at_copied, NT)
                            pe.wait_ge(p_copied, 16)
                            pe.wait_ge(o_scaled, 16)
                        for s in range(2):
                            a = 2 * j + s
                            mm = pe.matmul(ps[:, 4 + i % 4, s * CH:(s + 1) * CH], h2T[:, a * P:(a + 1) * P], w3u[:, d, :],
                                           start=True, stop=True)
                        mm.then_inc(f_full, 1)

            def spectrum(u, bank0, cos_in, sin_in, full, special):
                for j in range(2):
                    fj = slice(j * P, (j + 1) * P)
                    product(ps[:, bank0 + 2 * j, 0:CH], [(dftc[:, a, fj], cos_in[:, a, :]) for a in (0, 2)])
                    product(ps[:, bank0 + 2 * j, CH:2 * CH], [(dftc[:, a, fj], cos_in[:, a, :]) for a in (1, 3)]
                            ).then_inc(full, 1)
                    if special and j == 0:
                        o_ = ps[:, bank0 + 1, 0:CH]
                        pe.matmul(o_, dftsk[:, 0, :], sin_in[:, 0, :], start=True, stop=False)
                        for a in (0, 2):
                            pe.matmul(o_[0:1, :], dfts[:, a, 0:1], cos_in[:, a, :], start=False, stop=False)
                        pe.matmul(o_, dftsk[:, 1, :], sin_in[:, 2, :], start=False, stop=True)
                    else:
                        product(ps[:, bank0 + 2 * j + 1, 0:CH], [(dfts[:, a, fj], sin_in[:, a, :]) for a in (0, 2)])
                    product(ps[:, bank0 + 2 * j + 1, CH:2 * CH], [(dfts[:, a, fj], sin_in[:, a, :]) for a in (1, 3)]
                            ).then_inc(full, 1)

            def filter_spectrum(u):
                pe.wait_ge(f_sumdif, u + 1)
                pe.wait_ge(f_copied, 4 * (u + 1))
                if u == 0:
                    pe.wait_ge(ld_dft, 16 * 5)
                spectrum(u, 4, fs, ff, k_full, True)

            def turn_z(u):
                th = u % NU
                if u < NU:
                    pe.wait_ge(hy_conv, HYT)
                else:
                    pe.wait_ge(z_new, 2 * (u - NU + 1))
                if u >= 1:
                    pe.wait_ge(z_ready, 4 * u)
                    pe.wait_ge(gate_done, gate_tiles(u)[0])
                for a in range(NT):
                    for s in range(2):
                        mm = pe.transpose(ps[:, a, s * P:(s + 1) * P], uT[:, 2 * th + s, a * P:(a + 1) * P], ident[:, :])
                    mm.then_inc(z_turned, 1)

            def gate_tile(i):
                if i % 2 == 0:
                    arrived(pe, GATE_C + i // 2)
                if i >= 2:
                    pe.wait_ge(gate_done, i - 1)
                c0 = (i % 2) * P
                product(ps[:, 2 + i % 2, :], [(wview(GATE_C + i // 2)[:, k, c0:c0 + P], hT[:, k, :]) for k in range(KD)]
                        ).then_inc(gate_full, 1)

            def z_spectrum(u):
                pe.wait_ge(z_copied, 4 * (u + 1))
                if u >= 1:
                    pe.wait_ge(z_new, 2 * u)
                spectrum(u, 0, znat, znat, z_full, False)

            def inverse(u):
                pe.wait_ge(prod, u + 1)
                if u + 1 < 2 * NU:
                    pe.wait_ge(z_copied, 4 * (u + 2))
                Ue, Uo = Kb[u % 2][0], Kb[u % 2][2]
                Ve, Vo = t3, t1
                for s in range(2):
                    cs = slice(s * P, (s + 1) * P)
                    for par, (U_, V_) in enumerate(((Ue, Ve), (Uo, Vo))):
                        o_ = ps[:, s, :].rearrange("p (i q t) -> p i q t", i=2, q=2)[:, :, par, :]
                        pairs = []
                        for j in range(2):
                            for src, mat in ((U_, idftc), (V_, idfts)):
                                pairs.append((src[:, j, cs], mat[:, j, :].rearrange(
                                    "p (i q t) -> p i q t", i=2, q=2)[:, :, par, :]))
                        mm = product(o_, pairs)
                    mm.then_inc(y_full, 1)

            filter_time(0)
            turn_z(0)
            filter_spectrum(0)
            filter_time(1)
            for u in range(2 * NU):
                z_spectrum(u)
                if u + 1 < 2 * NU:
                    filter_spectrum(u + 1)
                pe.wait_ge(z_ready, 4 * (u + 1))
                for i in range(*gate_tiles(u)):
                    gate_tile(i)
                if u + 1 < 2 * NU:
                    turn_z(u + 1)
                inverse(u)
                if u + 2 < 2 * NU:
                    filter_time(u + 2)

            pe.wait_ge(z_new, 4 * NU)
            pe.wait_ge(k_ready, 8 * NU)
            pe.wait_ge(z_ready, 8 * NU)
            pe.wait_ge(gate_done, 2 * KD)
            for m in range(KD):
                j, c0 = m // 2, (m % 2) * P
                if m == 0:
                    pe.wait_ge(ld_wua, 16)
                if m % 2 == 0:
                    arrived(pe, MIX_C + j)
                if m >= 2:
                    pe.wait_ge(mix_done, m - 1)
                b = 4 + 2 * (m % 2)
                product(ps[:, b, :], [(wview(MIX_C + j, HC)[:, k, c0:c0 + P], uT[:, k, :]) for k in range(HC)])
                product(ps[:, b + 1, :], [(wua[:, k, m * P:(m + 1) * P], attnT[:, k, :]) for k in range(2)]
                        ).then_inc(mix_full, 1)
            norm_tensor(pe, "mem", mhn, MT, 0)
            pe.wait_ge(mix_done, KD)
            for j in range(4):
                arrived(pe, OUT_C + j)
                for a in range(NT):
                    i = 4 * j + a
                    if i >= 4:
                        pe.wait_ge(out_added, i - 3)
                    product(ps[:, 4 + a, 0:CW], [(mixT[:, k, a * P:(a + 1) * P], wview(OUT_C + j)[:, k, :])
                                                 for k in range(KD)]).then_inc(out_full, 1)
            pe.wait_ge(norms["mem"]["evA"], 4)
            pe.wait_ge(norms["mem"]["evV"], 4)
            for i in range(8):
                if i % 2 == 0:
                    arrived(pe, KV_C + i // 2)
                w = wview(KV_C + i // 2)
                if i >= 4:
                    pe.wait_ge(kv_copied, i - 3)
                else:
                    pe.wait_ge(out_added, 13 + i)
                if i < 4:
                    c0 = (i % 2) * P
                    product(ps[:, 4 + i % 4, 0:MEM], [(w[:, k, c0:c0 + P], mnT[:, k, :]) for k in range(KD)]).then_inc(kv_full, 1)
                else:
                    b = i % 2
                    product(ps[:, 4 + i % 4, 0:CW], [(mnT[:, k, b * P:(b + 1) * P], w[:, k, :]) for k in range(KD)]
                            ).then_inc(kv_full, 1)
            norm_tensor(pe, "xa", hn, NT, 0)
            pe.wait_ge(norms["xa"]["evA"], 4)
            pe.wait_ge(norms["xa"]["evV"], 4)
            pe.wait_ge(kv_copied, 8)
            for h in range(XH):
                if h % 2 == 0:
                    arrived(pe, QX_C + h // 2)
                c0 = (h % 2) * P
                product(ps[:, 4 + h, :], [(wview(QX_C + h // 2)[:, k, c0:c0 + P], hT[:, k, :]) for k in range(KD)]
                        ).then_inc(qx_full, 1)

            def x_scores(h):
                pe.wait_ge(qx_copied, h + 1)
                for a in range(NT):
                    if h >= 2 and a == 0:
                        pe.wait_ge(sx_exp, 4 * (h - 1))
                    mm = pe.matmul(ps[:, 2 * (h % 2) + a // 2, (a % 2) * MEM:(a % 2 + 1) * MEM], qxT[:, h, a * P:(a + 1) * P],
                                   kxT[:, h, :], start=True, stop=True)
                    mm.then_inc(sx_full, 1)

            x_scores(0)
            for h in range(XH):
                if h + 1 < XH:
                    x_scores(h + 1)
                pe.wait_ge(sx_norm, 4 * (h + 1))
                if h == 0:
                    pe.wait_ge(qx_copied, XH)
                else:
                    pe.wait_ge(px_copied, h)
                for b in range(MT):
                    for a in range(NT):
                        mm = pe.transpose(ps[:, 4 + b, a * P:(a + 1) * P], Px[:, h % 2, a, b * P:(b + 1) * P], ident[:, :])
                    mm.then_inc(px_turned, 1)
                pe.wait_ge(px_copied, h + 1)
                if h >= 1:
                    pe.wait_ge(ox_copied, h)
                product(ps[:, 6, :], [(vx[:, b, h * P:(h + 1) * P], PTx[:, h % 2, b, :]) for b in range(MT)]).then_inc(ox_full, 1)
            pe.wait_ge(ox_copied, XH)
            for j in range(2):
                arrived(pe, XO_C + j)
                for a in range(NT):
                    i = 4 * j + a
                    if i >= 4:
                        pe.wait_ge(xo_added, i - 3)
                    product(ps[:, a, :], [(oxT[:, k, a * P:(a + 1) * P], wview(XO_C + j, 4, 512)[:, k, :])
                                          for k in range(XH)]).then_inc(xo_full, 1)
            pe.wait_ge(xo_added, 8)
            norm_tensor(pe, "moe", hn, NT, 0)
            pe.wait_ge(norms["moe"]["evA"], 4)
            pe.wait_ge(norms["moe"]["evV"], 4)
            pe.wait_ge(ld_wr, 16)
            for a in range(NT):
                product(ps[:, 4 + a, 0:NE], [(hT[:, k, a * P:(a + 1) * P], wr[:, k, :]) for k in range(KD)]).then_inc(r_full, 1)
            pe.wait_ge(r_aff, NT)
            for a in range(NT):
                mm = pe.transpose(ps[0:NE, 0, a * P:(a + 1) * P], aff[:, a, :], ident[:, :])
            mm.then_inc(r_turned, 1)
            pe.wait_ge(top_done, 1)
            pe.transpose(ps[:, 1, 0:NE], topf[:, :, :].rearrange("p r s -> p (r s)"), ident[0:NE, 0:NE])
            pe.transpose(ps[:, 1, NE:2 * NE], topv[:, :, :].rearrange("p r s -> p (r s)"), ident[0:NE, 0:NE]).then_inc(sel_turned, 1)
            for b in range(2):
                pe.matmul(ps[:, 2 + b, :], ones16, bdiag[:, 8 * b:8 * b + 8, :].rearrange("p e s -> p (e s)"),
                          start=True, stop=True).then_inc(sel_bcast, 1)
            def gather(n):
                pe.wait_ge(pg_ready, n)
                for k in range(KD):
                    for a in range(NT):
                        mm = pe.matmul(ps[:, k // 4, (k % 4) * P:(k % 4 + 1) * P], hn[:, a, k * P:(k + 1) * P],
                                       Pg[:, a, :], start=a == 0, stop=a == NT - 1)
                mm.then_inc(xe_full, 1)

            def expert_pair(q, last):
                def gate_up(x, j):
                    e, i = 2 * q + x, 3 * j
                    for c in (i, i + 1):
                        n = MOE_C + c
                        pe.wait_ge(slot_loaded[slot(n)], e * (16 * STEP // RING) + 16 * load_count(n))
                    for k in range(KD):
                        for half in range(2):
                            mm = pe.matmul(ps[CAP * half:CAP * half + CAP, j % 2, 0:CW], xeT[:, k, x * CAP:(x + 1) * CAP],
                                           wview(MOE_C + i + half)[:, k, :], start=k == 0, stop=k == KD - 1)
                    mm.then_inc(ab_full, 1)

                def down(x, j):
                    e = 2 * q + x
                    pe.wait_ge(hh_ready, e * FB + (j + 1))
                    for i in range(2):
                        mm = pe.matmul(ps[:, 2, (j % 2) * P + i * CAP:(j % 2) * P + (i + 1) * CAP], hh[:, j % 2, i * P:(i + 1) * P],
                                       ident[0:CAP, 0:CAP], start=True, stop=True)
                    mm.then_inc(hh_turned, 1)
                    n = MOE_C + 3 * j + 2
                    pe.wait_ge(slot_loaded[slot(n)], e * (16 * STEP // RING) + 16 * load_count(n))
                    pe.wait_ge(hhT_ready, e * FB + (j + 1))
                    if j == 0 and x == 1:
                        pe.wait_ge(ye_ready, 4 * q + 2)
                    w = wview(n, 2, D)
                    for i in range(2):
                        for row in range(2):
                            half = row ^ x
                            mm = pe.matmul(ps[CAP * row:CAP * row + CAP, 3, :], hhT[:, j % 2, i, :],
                                           w[:, i, half * 512:(half + 1) * 512], start=j == 0 and i == 0,
                                           stop=j == FB - 1 and i == 1)
                    mm.then_inc(y_step, 1)

                pe.wait_ge(xe_ready, q + 1)
                for x in range(2):
                    for j in range(FB):
                        if x == 0 and j == 0:
                            gate_up(0, 0)
                        if j + 1 < FB:
                            gate_up(x, j + 1)
                        elif x == 0:
                            gate_up(1, 0)
                        down(x, j)
                if not last:
                    gather(q + 2)
                pe.wait_ge(ye_ready, 4 * q + 4)
                pe.wait_ge(pt_ready, 2 * q + 2)
                for a in range(NT):
                    if a >= 2:
                        pe.wait_ge(sc_added, q * 8 + 2 * (a - 1))
                    for half in range(2):
                        pe.matmul(ps[:, 4 + 2 * (a % 2) + half, :], PT[:, half, a * P:(a + 1) * P], Y[:, half, :],
                                  start=True, stop=True).then_inc(sc_full, 1)

            gather(1)
            with pe.Fori(0, NE // 2 - 1) as q:
                expert_pair(q, False)
            expert_pair(NE // 2 - 1, True)

        @block.vector
        def _(dve):
            n = [0]

            def link(ins):
                n[0] += 1
                ins.then_inc(chain, 1)
                dve.wait_ge(chain, n[0])

            def reduce_angle(i):
                dve.wait_ge(mlp_mm, i + 1)
                if i == 1:
                    dve.wait_ge(mlp_sin, 1)
                link(nc.vector.tensor_scalar(farg, ps[0:FFN, 5, :], fcol[:, 2 * i:2 * i + 1], fcol[:, 2 * i + 1:2 * i + 2],
                                             ALU.add, ALU.mult))
                link(nc.vector.tensor_scalar(fk, farg, 1.0 / TWO_PI, MAGIC, ALU.mult, ALU.add))
                link(nc.vector.tensor_scalar(fk, fk, MAGIC, None, ALU.subtract))
                for c in (PI_A, PI_B, PI_C):
                    link(nc.vector.scalar_tensor_tensor(out=farg, in0=fk, scalar=-c, in1=farg, op0=ALU.mult, op1=ALU.add))
                nc.vector.tensor_scalar(farg, farg, 3.1415925, -3.1415925, ALU.min, ALU.max).then_inc(mlp_arg, 1)

            dve.wait_ge(vec_turned, 2)
            nc.vector.tensor_copy(vcol[:, 0:V_ROWS], ps[:, 6, 0:V_ROWS]).then_inc(vec_ready, 1)
            nc.vector.tensor_copy(vcol[:, V_CW:V_COLS], ps[:, 7, 0:54]).then_inc(vec_ready, 1)
            dve.wait_ge(vec_ready, 2)
            dve.wait_ge(ld_filt, 16 * 7)
            reduce_angle(0)
            norm_vector(dve, link, "mix", xs, hn, NT, 1)
            norm_evac(dve, "mix", hT, NT, 0, V_MIX, 1)
            reduce_angle(1)

            dve.wait_ge(ld_rope, 32)
            for g in range(GROUPS):
                for part in range(2):
                    for a in range(NT):
                        m = 8 * g + 4 * part + a
                        tile = 4 * (3 * g + part) + a
                        dve.wait_ge(qkv_full, tile + 1)
                        if m >= 1:
                            dve.wait_ge(roped, m)
                        src = ps[:, tile % 4, 0:CW].rearrange("p (h s c) -> p h s c", h=4, s=2)
                        A4 = ropeA.rearrange("p (h s c) -> p h s c", h=4, s=2)
                        B4 = ropeB.rearrange("p (h s c) -> p h s c", h=4, s=2)
                        cb = lambda t_, s: t_[:, a, s * 32:(s + 1) * 32].unsqueeze(1).to_broadcast([P, 4, 32])
                        for s in range(2):
                            nc.vector.tensor_tensor(A4[:, :, s, :], src[:, :, s, :], cb(rcos, s), ALU.mult)
                        nc.vector.tensor_tensor(B4[:, :, 0, :], src[:, :, 1, :], cb(rsin, 0), ALU.mult)
                        link(nc.vector.tensor_tensor(B4[:, :, 1, :], src[:, :, 0, :], cb(rsin, 1), ALU.mult))
                        if m >= 2:
                            dve.wait_ge(qk_turned, m - 1)
                        nc.vector.tensor_tensor(rope_out[:, m % 2, :], ropeA, ropeB, ALU.add).then_inc(roped, 1)

            def softmax_head(p):
                a = p // 4
                dve.wait_ge(s_full, p + 1)
                if p == 0:
                    dve.wait_ge(ld_mask, 16)
                    dve.wait_ge(qk_turned, 24)
                if p >= 2:
                    dve.wait_ge(p_turned, p - 1)
                nc.vector.scalar_tensor_tensor(out=Sb[:, p % 2, :], in0=psc(2, 4, NKEY), scalar=0.125, in1=masks[:, a, :],
                                               op0=ALU.mult, op1=ALU.add).then_inc(s_masked, 1)
                dve.wait_ge(s_masked, p + 1)
                link(nc.vector.tensor_reduce(st[:, 32 + p % 2:33 + p % 2], Sb[:, p % 2, :], AX.X, ALU.max))
                nc.vector.tensor_scalar(st[:, 34 + p % 2:35 + p % 2], st[:, 32 + p % 2:33 + p % 2], -1.0, None,
                                        ALU.mult).then_inc(s_negmax, 1)

            def conv_sides(m):
                dve.wait_ge(hy_centre, m + 1)
                L, R = vcol[:, V_CW + m:V_CW + m + 1], vcol[:, V_CW + 2 * HYT + m:V_CW + 2 * HYT + m + 1]
                src, dst, n3 = ps[:, m % 2, :], uT[:, m, :], 3 * P

                def tap(d0, s0, cnt, w):
                    return nc.vector.scalar_tensor_tensor(out=dst[:, d0:d0 + cnt], in0=src[:, s0:s0 + cnt], scalar=w,
                                                          in1=dst[:, d0:d0 + cnt], op0=ALU.mult, op1=ALU.add)
                tap(P, 0, n3, L)
                link(tap(1, n3, P - 1, L))
                tap(0, P, n3, R)
                tap(n3, 1, P - 1, R).then_inc(hy_conv, 1)

            def scale_heads(p):
                a, h = p // 4, p % 4
                dve.wait_ge(s_exp, p + 1)
                link(nc.vector.reciprocal(st[:, 38 + p % 2:39 + p % 2], st[:, 36 + p % 2:37 + p % 2]))
                dve.wait_ge(o_full, p + 1)
                if h == 0 and a >= 2:
                    dve.wait_ge(at_turned, a - 1)
                nc.vector.tensor_scalar(anat[:, a % 2, h * 64:(h + 1) * 64], ps[:, 6, 0:64], st[:, 38 + p % 2:39 + p % 2],
                                        None, ALU.mult).then_inc(o_scaled, 1)

            def copy_attn(a):
                dve.wait_ge(at_turned, a + 1)
                nc.vector.tensor_copy(attnT[:, :, a * P:(a + 1) * P],
                                      ps[:, 7, 0:2 * P].rearrange("p (r t) -> p r t", r=2)).then_inc(at_copied, 1)

            softmax_head(0)
            for p in range(16):
                conv_sides(p)
                if p + 1 < 16:
                    softmax_head(p + 1)
                if p % 4 == 0 and p > 0:
                    copy_attn(p // 4 - 1)
                scale_heads(p)
            conv_sides(16)
            copy_attn(3)
            conv_sides(17)

            TT = nc.vector.tensor_tensor

            def butterflies(base, full, even, bank0, B, done):
                for i in range(4):
                    j, s = i // 2, i % 2
                    dve.wait_ge(even, base + i + 1)
                    odd = ps[:, bank0 + i, CH:2 * CH]
                    e_ = EV(B)[s][:, j, :]
                    if s == 0:
                        link(nc.vector.tensor_tensor(B[0][:, j, :], e_, odd, ALU.add))
                        nc.vector.tensor_tensor(B[2][:, j, :], e_, odd, ALU.subtract).then_inc(done, 1)
                    else:
                        link(nc.vector.tensor_tensor(B[3][:, j, :], odd, e_, ALU.subtract))
                        nc.vector.tensor_tensor(B[1][:, j, :], e_, odd, ALU.add).then_inc(done, 1)

            def products(u):
                Zp, Z1, Zq, Z2 = ZP
                Kp, K1, Kq, K2 = Kb[u % 2]
                dve.wait_ge(z_ready, 4 * (u + 1))
                dve.wait_ge(k_ready, 4 * (u + 1))
                if u >= 1:
                    dve.wait_ge(y_full, 2 * u)
                TT(t1, Zp, K1, ALU.mult)
                TT(t2, Zq, K2, ALU.mult)
                link(TT(t3, Z1, Kp, ALU.mult))
                link(TT(t1, t1, t3, ALU.add))
                link(TT(t3, Z2, Kq, ALU.mult))
                link(TT(t2, t2, t3, ALU.add))
                TT(t3, t1, t2, ALU.subtract)
                link(TT(t1, t1, t2, ALU.add))
                TT(t2[0:1, 0, :], Z1[0:1, 0, :], K2[0:1, 0, :], ALU.mult)
                link(TT(t2[0:1, 1, :], Z2[0:1, 0, :], K1[0:1, 0, :], ALU.mult))
                TT(t3[0:1, 0, :], t2[0:1, 0, :], t2[0:1, 1, :], ALU.add)
                TT(Zp, Zp, Kp, ALU.mult)
                TT(Zq, Zq, Kq, ALU.mult)
                TT(Z1, Z1, K1, ALU.mult)
                link(TT(Z2, Z2, K2, ALU.mult))
                TT(K1, Z1, Z2, ALU.add)
                link(TT(K2, Z1, Z2, ALU.subtract))
                nc.vector.tensor_copy(t1[0:1, 0, :], K2[0:1, 0, :])
                nc.vector.memset(K1[0:1, 0, :], 0.0)
                TT(Kp, Zp, Zq, ALU.add)
                link(TT(Kq, Zp, Zq, ALU.subtract))
                nc.vector.memset(K2[0:1, 0, :], 0.0)
                link(TT(Kp, Kp, K1, ALU.subtract))
                TT(Kq, Kq, K2, ALU.subtract).then_inc(prod, 1)

            def gate(u):
                o, th = u // NU, u % NU
                for s in range(2):
                    m = 2 * th + s
                    dve.wait_ge(y_full, 2 * u + s + 1)
                    link(nc.vector.scalar_tensor_tensor(out=uT[:, m, :], in0=uT[:, m, :],
                                                        scalar=vcol[:, V_SKIP + o * HC + m:V_SKIP + o * HC + m + 1],
                                                        in1=ps[:, s, :], op0=ALU.mult, op1=ALU.add))
                    TT(uT[:, m, :], uT[:, m, :], uT[:, (o + 1) * HC + m, :], ALU.mult).then_inc(z_new, 1)

            butterflies(0, k_full, k_even, 4, Kb[0], k_ready)
            for u in range(2 * NU):
                butterflies(4 * u, z_full, z_even, 0, ZP, z_ready)
                products(u)
                if u + 1 < 2 * NU:
                    butterflies(4 * (u + 1), k_full, k_even, 4, Kb[(u + 1) % 2], k_ready)
                gate(u)

            norm_vector(dve, link, "mem", mems, mhn, MT, 1)
            for m in range(KD):
                b = 4 + 2 * (m % 2)
                dve.wait_ge(mix_full, m + 1)
                if m == 0:
                    dve.wait_ge(gate_done, 2 * KD)
                nc.vector.tensor_tensor(mt[:, 0, :], gates[:, m, :], ps[:, b, :], ALU.mult)
                link(nc.vector.tensor_tensor(mt[:, 1, :], gates[:, KD + m, :], ps[:, b + 1, :], ALU.mult))
                nc.vector.tensor_tensor(mixT[:, m, :], mt[:, 0, :], mt[:, 1, :], ALU.add).then_inc(mix_done, 1)
                dve.wait_ge(mix_done, m + 1)
            norm_evac(dve, "mem", mnT, MT, 0, V_MEM, 1)
            for i in range(16):
                j, a = i // 4, i % 4
                dve.wait_ge(out_full, i + 1)
                dst = xs[:, a, j * CW:(j + 1) * CW]
                nc.vector.tensor_tensor(dst, dst, ps[:, 4 + a, 0:CW], ALU.add).then_inc(out_added, 1)
            dve.wait_ge(out_added, 16)
            dve.wait_ge(out_full, 16)
            norm_vector(dve, link, "xa", xs, hn, NT, 4)
            norm_evac(dve, "xa", hT, NT, 0, V_X, 1)
            for h in range(XH):
                for a in range(NT):
                    c = 40 + (h % 2) * 4 + a
                    dve.wait_ge(sx_full, 4 * h + 2 * (a // 2) + 2)
                    link(nc.vector.tensor_reduce(st[:, 56 + a:57 + a],
                                                 ps[:, 2 * (h % 2) + a // 2, (a % 2) * MEM:(a % 2 + 1) * MEM], AX.X, ALU.max))
                    nc.vector.tensor_scalar(st[:, c:c + 1], st[:, 56 + a:57 + a], -float(P) ** -0.5, None,
                                            ALU.mult).then_inc(sx_negmax, 1)
                for a in range(NT):
                    c = 40 + (h % 2) * 4 + a
                    dve.wait_ge(sx_exp, 4 * h + a + 1)
                    link(nc.vector.reciprocal(st[:, 60 + a:61 + a], st[:, c + 8:c + 9]))
                    nc.vector.tensor_scalar(Px[:, h % 2, a, :], Px[:, h % 2, a, :], st[:, 60 + a:61 + a], None,
                                            ALU.mult).then_inc(sx_norm, 1)
            for i in range(8):
                j, a = i // 4, i % 4
                dve.wait_ge(xo_full, i + 1)
                dst = xs[:, a, j * 512:(j + 1) * 512]
                nc.vector.tensor_tensor(dst, dst, ps[:, a, :], ALU.add).then_inc(xo_added, 1)
            dve.wait_ge(xo_added, 8)
            norm_vector(dve, link, "moe", xs, hn, NT, 2)
            norm_evac(dve, "moe", hT, NT, 0, V_MOE, 1)
            for a in range(NT):
                dve.wait_ge(r_full, a + 1)
                link(nc.vector.tensor_reduce(st[:, 56 + a:57 + a], ps[:, 4 + a, 0:NE], AX.X, ALU.max))
                nc.vector.tensor_scalar(st[:, 40 + a:41 + a], st[:, 56 + a:57 + a], -1.0, None, ALU.mult).then_inc(r_negmax, 1)
            dve.wait_ge(r_exp, NT)
            link(nc.vector.reciprocal(st[:, 60:64], st[:, 44:48]))
            for a in range(NT):
                nc.vector.tensor_scalar(aff[:, a, :], lg[:, a, :], st[:, 60 + a:61 + a], None, ALU.mult).then_inc(r_aff, 1)
            dve.wait_ge(r_turned, 1)
            link(nc.vector.tensor_copy(affT.rearrange("e (m a) -> e a m", a=NT),
                                       ps[0:NE, 0, :].rearrange("e (a m) -> e a m", a=NT)))
            for r in range(CAP // 8):
                v, ix = topv[:, 0, 8 * r:8 * r + 8], topi[:, 8 * r:8 * r + 8]
                link(nc.vector.max(v, affT))
                link(nc.vector.max_index(ix, v, affT))
                link(nc.vector.match_replace(affT, v, affT, -1.0))
            nc.vector.tensor_copy(topv[:, 1, :], topv[:, 0, :])
            nc.vector.tensor_copy(topf[:, 0, :], topi)
            link(nc.vector.tensor_copy(topf[:, 1, :], topi))
            nc.vector.memset(ones16, 1.0)
            TT(bdiag, topf[:, 0, :].unsqueeze(1).to_broadcast([NE, NE, CAP]),
               ident[0:NE, 0:NE].unsqueeze(2).to_broadcast([NE, NE, CAP]), ALU.mult).then_inc(top_done, 1)
            dve.wait_ge(sel_turned, 1)
            for h in range(2):
                for row in range(2):
                    nc.vector.tensor_copy(icol[CAP * row:CAP * row + CAP, h, :],
                                          ps[CAP * row:CAP * row + CAP, 1, (row ^ h):NE:2]).then_inc(sel_cols, 1)
            nc.vector.tensor_copy(gcol, ps[:, 1, NE:2 * NE]).then_inc(sel_cols, 1)
            dve.wait_ge(sel_bcast, 2)
            nc.vector.tensor_copy(bidx, psc(2, 4, NE * CAP)).then_inc(sel_cols, 1)
            dve.wait_ge(ld_moe, 32)
            dve.wait_ge(sel_cols, 6)

            def gather_table(q):
                nc.vector.tensor_tensor(Pg, bidx[:, bass.ds(q * P, P)].unsqueeze(1).to_broadcast([P, NT, P]),
                                        tval.unsqueeze(2).to_broadcast([P, NT, P]), ALU.is_equal).then_inc(pg_ready, 1)

            def gathered(n):
                dve.wait_ge(xe_full, n)
                TT(xeT, psc(0, 2, KD * P).rearrange("p (k s) -> p k s", k=KD),
                   vcol[:, V_MOE:V_MOE + KD].unsqueeze(2).to_broadcast([P, KD, P]), ALU.mult).then_inc(xe_ready, 1)

            def expert_pair(q, last):
                if not last:
                    gather_table(q + 1)
                for h in range(2):
                    nc.vector.tensor_scalar(PT[:, h, :], iota, icol[:, h, bass.ds(q, 1)], None, ALU.is_equal).then_inc(pt_ready, 1)
                for x in range(2):
                    e = 2 * q + x
                    for j in range(FB):
                        dve.wait_ge(silu_done, e * FB + (j + 1))
                        TT(hh[:, j % 2, :], sil[:, j % 2, :], ps[CAP:2 * CAP, j % 2, 0:CW], ALU.mult).then_inc(hh_ready, 1)
                        dve.wait_ge(hh_turned, e * FB + (j + 1))
                        nc.vector.tensor_copy(hhT[:, j % 2, :, :], ps[:, 2, (j % 2) * P:(j % 2 + 1) * P].rearrange(
                            "p (i s) -> p i s", i=2)).then_inc(hhT_ready, 1)
                    dve.wait_ge(y_step, e * FB + FB)
                    for row in range(2):
                        r = slice(CAP * row, CAP * row + CAP)
                        nc.vector.tensor_scalar(Y[r, row ^ x, :], ps[r, 3, :], gcol[r, bass.ds(e, 1)], None,
                                                ALU.mult).then_inc(ye_ready, 1)
                if not last:
                    gathered(q + 2)
                for a in range(NT):
                    for half in range(2):
                        dve.wait_ge(sc_full, q * 8 + (2 * a + half + 1))
                        dst = xs[:, a, half * 512:(half + 1) * 512]
                        TT(dst, dst, ps[:, 4 + 2 * (a % 2) + half, :], ALU.add).then_inc(sc_added, 1)

            gather_table(0)
            gathered(1)
            with dve.Fori(0, NE // 2 - 1) as q:
                expert_pair(q, False)
            expert_pair(NE // 2 - 1, True)
            dve.wait_ge(sc_added, NE * 4)
            norm_vector(dve, link, "fin", xs, None, NT, 1)
            dve.wait_ge(ld_gf, 16)
            for a in range(NT):
                nc.vector.scalar_tensor_tensor(out=hT_out(a), in0=xs[:, a, :], scalar=st[:, 24 + a:25 + a], in1=gf,
                                               op0=ALU.mult, op1=ALU.mult).then_inc(norms["fin"]["scaled"], 1)


_INS = ["x", "mem", "ln_mix_g", "w_in", "hy_conv_w", "hy_conv_b", "filt_w1", "filt_b1", "filt_freq1",
        "filt_w2", "filt_b2", "filt_freq2", "filt_w3", "hy_skip", "w_up_hy", "w_up_attn", "w_gate", "b_gate",
        "w_out", "ln_x_g", "ln_mem_g", "w_q_x", "w_kv_mem", "w_o_x", "ln_moe_g", "w_router", "w_e_gate",
        "w_e_up", "w_e_down", "ln_f_g"]


def _constants():
    import math

    import numpy as np
    f = np.float32
    m, a = np.arange(P)[:, None], np.arange(NT)[None, :]
    t = 4 * m + a
    flat = t.T.reshape(-1)
    c = {"ident": np.eye(P, dtype=f)}
    tl = np.linspace(0.0, 1.0, SEQ, dtype=f)
    grid = (f(2.0 * math.pi) * np.arange(SEQ, dtype=f) / f(SEQ)).astype(f)
    bands = np.linspace(1e-4, 15, 16, dtype=f)
    arg = (bands[None, :] * grid[:, None]).astype(f)
    emb = np.concatenate([tl[:, None], np.cos(arg), -np.sin(arg)], axis=1).astype(f)
    c["embT"] = emb[flat].T
    deltas = np.linspace(math.log(1e-2) / 1.5, math.log(1e-2) / 0.3, HW, dtype=f)
    c["decay"] = np.exp(-tl[:, None] * np.abs(deltas)[None, :]).astype(f)[t]
    N, H = 2 * SEQ, SEQ // 2
    fr = np.arange(H)
    ang = 2 * np.pi * ((t[:, :, None] * fr) % N) / N
    quarter = 2 * np.pi * ((t * H) % N) / N
    even = (t % 2 == 0)
    co, si = np.cos(ang), np.sin(ang)
    sk = si[:, [0, 2], :P].copy()
    sk[:, :, 0] = 0.0
    si[:, :, 0] = np.where(even, np.cos(quarter), np.sin(quarter))
    c["dftc"], c["dfts"], c["dftsk"] = co, si, sk
    ia = 2 * np.pi * ((fr[:, None] * flat) % N) / N
    ic, isn = np.cos(ia) * 2 / N, np.sin(ia) * 2 / N
    ic[0] = 1.0 / N
    q = 2 * np.pi * ((flat * H) % N) / N
    isn[0] = np.where(flat % 2 == 0, -0.5 * np.cos(q), 0.5 * np.sin(q)) * 2 / N
    c["idftc"] = ic.reshape(2, P, SEQ).transpose(1, 0, 2)
    c["idfts"] = isn.reshape(2, P, SEQ).transpose(1, 0, 2)
    inv = (f(10000.0) ** (-np.arange(0, 64, 2, dtype=f) / f(64))).astype(f)
    ra = (t.astype(f)[:, :, None] * inv).astype(f)
    c["rcos"] = np.concatenate([np.cos(ra), np.cos(ra)], axis=2)
    c["rsin"] = np.concatenate([-np.sin(ra), np.sin(ra)], axis=2)
    ok0 = np.abs(t[:, :, None] - flat) <= 64
    rel = np.abs(np.arange(P)[:, None] - np.arange(P)[None, :])
    ok1 = np.repeat((rel <= 64)[:, None, :], NT, 1)
    ok2 = np.repeat((rel % 4 == 0)[:, None, :], NT, 1)
    c["mask"] = np.where(np.concatenate([ok0, ok1, ok2], axis=2), 0.0, -1e30)
    c["tval"] = t
    c["iota"] = np.repeat(flat[None, :], P, 0)
    return {k: np.ascontiguousarray(v.astype(f)) for k, v in c.items()}


_CONSTS = ["ident", "embT", "decay", "dftc", "dfts", "dftsk", "idftc", "idfts", "rcos", "rsin", "mask", "tval", "iota"]


def kernel(**inputs):
    import numpy as _np
    import concourse.bacc as _bacc
    from concourse import mybir as _mybir
    from concourse.bass_utils import run_bass_kernel_spmd as _run

    nc = _bacc.Bacc("TRN2", target_bir_lowering=False, num_devices=1)
    arrays, args = {}, []
    for name in _INS:
        arrays[f"in_{name}_dram"] = _np.ascontiguousarray(inputs[name])
    consts = _constants()
    for name in _CONSTS:
        arrays[f"c_{name}_dram"] = consts[name]
    for name, a in arrays.items():
        args.append(nc.dram_tensor(name, a.shape, _mybir.dt.from_np(a.dtype), kind="ExternalInput").ap())
    args.append(nc.dram_tensor("out_0_dram", (1, SEQ, D), F32, kind="ExternalOutput").ap())
    encoder_block(nc, *args)
    r = _run(nc, [arrays], core_ids=[0])
    return r.results[0]["out_0_dram"]
```

```python
from contextlib import ExitStack

import concourse.bass as bass
from concourse import mybir

F32 = mybir.dt.float32
ALU = mybir.AluOpType
ACT = mybir.ActivationFunctionType
AX = mybir.AxisListType

P = 128
SEQ = 512
NT = SEQ // P
D = 1024
KD = D // P
MEM = 256
MT = MEM // P
EPS = 1e-6
HW = 768
HC = HW // P
HYT = 3 * HC
FFN = 64
EMB = 33
SLOTS_PER_HEAD = 4
GROUPS = 3
AW = GROUPS * SLOTS_PER_HEAD * 64
NKEY = SEQ + P + P
XH = 4
NE = 16
CAP = 2 * SEQ // NE
FF = 2048
CW = 256
RING = 16
RING0 = 3
OWN = 8
CH = 256
NU = HW // CH
BW = 512
FB = FF // BW
TWO_PI = 6.283185307179586
MAGIC = 12582912.0
PI_A, PI_B = 6.28125, 0.0019350051879882812
PI_C = TWO_PI - PI_A - PI_B

V_MIX, V_X, V_MEM, V_MOE, V_BG, V_CB, V_SKIP = 0, 8, 16, 24, 32, 48, 66
V_ROWS = 78
V_CW = 78
V_COLS = V_CW + 54


def encoder_block(nc, x, mem, w_in, filt_w1, filt_w2, filt_w3, w_up_hy, w_up_attn, w_gate, w_out, w_q_x,
                  w_kv_mem, w_o_x, w_router, w_e_gate, w_e_up, w_e_down, ln_f_g, vectors, taps, filt_vectors,
                  c_ident, c_embT, c_decay, c_dftc, c_dfts, c_dftsk, c_idftc, c_idfts,
                  c_rcos, c_rsin, c_mask, c_slot_no, c_count, c_sum4, out):
    ctx = ExitStack()
    with ctx:
        def sb(name, shape, dt=F32):
            return ctx.enter_context(nc.sbuf_tensor(name, shape, dt))

        def sem(name):
            return ctx.enter_context(nc.semaphore(name))

        ring = sb("ring", [P, OWN, 2048])
        xs = sb("xs", [P, NT, D])
        hT = sb("hT", [P, KD, SEQ])
        UT = sb("UT", [P, 9216])
        W = sb("W", [P, 16896])
        attnT = sb("attnT", [P, 2, SEQ])
        ident = sb("ident", [P, P])
        vrow = W[:, 16384:16640].rearrange("p (a d) -> p a d", a=2)
        vcol = sb("vcol", [P, V_COLS])
        st = sb("st", [P, 64])
        eps = sb("eps", [P, 2])
        fcol = sb("fcol", [FFN, 4])
        h2T = sb("h2T", [P, SEQ])

        uT = UT[:, :].rearrange("p (m t) -> p m t", t=SEQ)
        embT = UT[0:EMB, 0:512]
        fw1 = UT[0:EMB, 512:576]
        fw2 = UT[0:FFN, 576:640]
        farg = UT[0:FFN, 1024:1536]
        fk = UT[0:FFN, 1536:2048]
        h1T = UT[0:FFN, 2048:2560]

        hn = W[:, 0:4096].rearrange("p (a d) -> p a d", a=NT)
        vnat = W[:, 0:3072].rearrange("p (a c) -> p a c", a=NT)
        spare = ring[:, RING0:OWN, :].rearrange("p s c -> p (s c)")
        qz = spare[:, 0:6144].rearrange("p (g h t) -> p g h t", g=GROUPS, h=SLOTS_PER_HEAD)
        kT = W[:, 6144:9216].rearrange("p (g r t) -> p g r t", g=GROUPS, r=2)
        masks = W[:, 9216:12288].rearrange("p (a k) -> p a k", a=NT)
        Sb = W[:, 12288:13824].rearrange("p (b k) -> p b k", b=2)
        PTb = W[:, 13824:15360].rearrange("p (b k) -> p b k", b=2)
        rcos = W[:, 15872:16128].rearrange("p (a k) -> p a k", a=NT)
        rsin = W[:, 16128:16384].rearrange("p (a k) -> p a k", a=NT)
        ropeA = W[:, 12288:12544]
        ropeB = W[:, 12544:12800]
        rope_out = W[:, 12800:13312].rearrange("p (b k) -> p b k", b=2)
        idftc = W[:, 0:1024].rearrange("p (j t) -> p j t", j=2)
        idfts = W[:, 1024:2048].rearrange("p (j t) -> p j t", j=2)
        fs = W[:, 3072:4096].rearrange("p (a c) -> p a c", a=NT)
        dftc = W[:, 4096:5120].rearrange("p (a f) -> p a f", a=NT)
        dfts = W[:, 5120:6144].rearrange("p (a f) -> p a f", a=NT)
        Kb = [[W[:, 6144 + 2048 * b + 512 * i:6656 + 2048 * b + 512 * i].rearrange("p (j c) -> p j c", j=2)
               for i in range(4)] for b in range(2)]
        Zb = [W[:, 10240 + 512 * i:10752 + 512 * i].rearrange("p (j c) -> p j c", j=2) for i in range(4)]
        t1 = W[:, 12288:12800].rearrange("p (j c) -> p j c", j=2)
        t2 = W[:, 12800:13312].rearrange("p (j c) -> p j c", j=2)
        t3 = W[:, 13312:13824].rearrange("p (j c) -> p j c", j=2)
        dftsk = W[:, 15872:16128].rearrange("p (a f) -> p a f", a=2)
        w3u = W[:, 16384:16896].rearrange("p (d c) -> p d c", d=2)
        gates = spare[:, 0:8192].rearrange("p (i t) -> p i t", i=2 * KD)
        ff = spare[:, 6144:7168].rearrange("p (a c) -> p a c", a=NT)
        fb = spare[:, 7168:8192].rearrange("p (a c) -> p a c", a=NT)
        znat = spare[:, 8192:9216].rearrange("p (a c) -> p a c", a=NT)
        dec = spare[:, 9216:10240].rearrange("p (a c) -> p a c", a=NT)
        ZP = Zb
        EV = lambda B: (B[2], B[1])
        mixT = W[:, 0:4096].rearrange("p (m t) -> p m t", m=KD)
        mt = W[:, 6144:7168].rearrange("p (s t) -> p s t", s=2)
        mems = W[:, 7168:9216].rearrange("p (a d) -> p a d", a=MT)
        mnT = W[:, 9216:11264].rearrange("p (k t) -> p k t", k=KD)
        mhn = W[:, 11264:13312].rearrange("p (a d) -> p a d", a=MT)
        kxT = W[:, 13312:14336].rearrange("p (h t) -> p h t", h=XH)
        vx = W[:, 14336:15360].rearrange("p (b c) -> p b c", b=MT)
        qxT = UT[:, 0:2048].rearrange("p (h t) -> p h t", h=XH)
        oxT = UT[:, 2048:4096].rearrange("p (h t) -> p h t", h=XH)
        Px = UT[:, 4096:6144].rearrange("p (b a t) -> p b a t", b=2, a=NT)
        PTx = UT[:, 6144:8192].rearrange("p (b s t) -> p b s t", b=2, s=2)
        wua = UT[:, 3072:5120].rearrange("p (k c) -> p k c", k=2)
        hT_out = lambda a: hT[:, :, :].rearrange("p k t -> p (k t)")[:, a * D:(a + 1) * D]
        up_to = W[:, 4096:4224]
        ones = W[:, 4224:4352]
        Pw = W[:, 4352:4864].rearrange("p (a s) -> p a s", a=NT)
        Pg = W[:, 5120:5632].rearrange("p (a s) -> p a s", a=NT)
        PT = W[:, 5632:6656].rearrange("p (h t) -> p h t", h=2)
        Y = W[:, 6656:7680].rearrange("p (h c) -> p h c", h=2)
        xeT = W[:, 8704:9728].rearrange("p (k s) -> p k s", k=KD)
        sil = W[0:CAP, 9728:10752].rearrange("p (b f) -> p b f", b=2)
        hh = W[0:CAP, 10752:11776].rearrange("p (b f) -> p b f", b=2)
        hhT = W[:, 11776:12288].rearrange("p (b i s) -> p b i s", b=2, i=4)
        gf = UT[:, 8192:9216]
        wr = sb("wr", [P, KD, 32])
        sum4 = sb("sum4", [P, NE])
        lgT = W[:, 8704:9216]
        aff = W[:, 7680:7744].rearrange("p (a e) -> p a e", a=NT)
        lg = W[:, 7744:7808].rearrange("p (a e) -> p a e", a=NT)
        affT = UT[0:NE, 8192:8704]
        top8 = W[0:NE, 7808:7816]
        chosenT = W[0:NE, 8192:8704]
        chosen = W[:, 7824:7888].rearrange("p (a e) -> p a e", a=NT)
        place_of = W[:, 7888:7952].rearrange("p (a e) -> p a e", a=NT)
        slot_no = W[:, 7952:8016]

        def slot_memory(k):
            if k < OWN:
                return ring[:, k, :]
            if k < OWN + 4:
                return UT[:, 2048 * (k - OWN):2048 * (k - OWN + 1)]
            if k < OWN + 6:
                return W[:, 12544 + 2048 * (k - OWN - 4):12544 + 2048 * (k - OWN - 3)]
            return hT[:, :, :].rearrange("p k t -> p (k t)")[:, 2048 * (k - OWN - 6):2048 * (k - OWN - 5)]

        ps = ctx.enter_context(nc.psum_tensor("ps", [P, 8, 512], F32))

        def psc(b0, b1, n):
            return ps[:, b0:b1, :].rearrange("p b c -> p (b c)")[:, 0:n]

        ld_ident, ld_vec, ld_filt, ld_rope, ld_mask = (sem(n) for n in (
            "ld_ident", "ld_vec", "ld_filt", "ld_rope", "ld_mask"))
        ld_dft, ld_dec, ld_w3, ld_mem, ld_wr, ld_moe, ld_gf, ld_wua = (sem(n) for n in (
            "ld_dft", "ld_dec", "ld_w3", "ld_mem", "ld_wr", "ld_moe", "ld_gf", "ld_wua"))
        ld_idft = sem("ld_idft")
        ld_x = [sem(f"ld_x{a}") for a in range(NT)]
        spare_zero, gate_full, gate_done = sem("spare_zero"), sem("gate_full"), sem("gate_done")
        slot_loaded = [sem(f"slot{i}_loaded") for i in range(RING)]
        eps_ready, table_loaded = sem("eps_ready"), sem("table_loaded")
        vec_turned, vec_ready = sem("vec_turned"), sem("vec_ready")
        mlp_mm, mlp_arg, mlp_sin = sem("mlp_mm"), sem("mlp_arg"), sem("mlp_sin")
        chain = sem("dve_chain")
        pchain = sem("pool_chain")
        norms = {}
        for tag in ("mix", "mem", "xa", "moe", "fin"):
            names = ["sq", "sqrt", "scaled"]
            if tag in ("mem", "xa"):
                names.append("var")
            names += ["turned", "evA", "evV"] if tag != "fin" else ["rooted", "evA"]
            norms[tag] = {n: sem(f"{tag}_{n}") for n in names}
        qkv_full, v_copied, roped, qk_turned, qk_copied = (sem(n) for n in (
            "qkv_full", "v_copied", "roped", "qk_turned", "qk_copied"))
        s_full, s_masked, s_negmax, s_exp, p_scaled, p_turned, p_copied, o_full, at_copied = (sem(n) for n in (
            "s_full", "s_masked", "s_negmax", "s_exp", "p_scaled", "p_turned", "p_copied", "o_full",
            "at_copied"))
        hy_full, hy_centre, hy_conv = sem("hy_full"), sem("hy_centre"), sem("hy_conv")
        f_full, f_copied, f_sumdif, k_full, k_even, k_ready = (sem(n) for n in (
            "f_full", "f_copied", "f_sumdif", "k_full", "k_even", "k_ready"))
        z_turned, z_copied, z_full, z_even, z_ready, prod, y_full, z_new = (sem(n) for n in (
            "z_turned", "z_copied", "z_full", "z_even", "z_ready", "prod", "y_full", "z_new"))
        mix_full, mix_done = sem("mix_full"), sem("mix_done")
        out_full, out_added = sem("out_full"), sem("out_added")
        kv_full, kv_copied, qx_full, qx_copied = (sem(n) for n in ("kv_full", "kv_copied", "qx_full", "qx_copied"))
        sx_full, sx_negmax, sx_exp, sx_norm, px_turned, px_copied, ox_full, ox_copied, xo_full, xo_added = (sem(n) for n in (
            "sx_full", "sx_negmax", "sx_exp", "sx_norm", "px_turned", "px_copied", "ox_full", "ox_copied",
            "xo_full", "xo_added"))
        r_full, r_shifted, r_exp, r_aff, r_turned, top_done, sel_turned, sel_copied, sel_counted, pg_ready = (sem(n) for n in (
            "r_full", "r_shifted", "r_exp", "r_aff", "r_turned", "top_done", "sel_turned", "sel_copied",
            "sel_counted", "pg_ready"))
        pw_ready, pt_turned = sem("pw_ready"), sem("pt_turned")
        rp_full, rp_copied = sem("rp_full"), [sem("rp_copied0"), sem("rp_copied1")]
        (xe_full, xe_ready, ab_full, silu_done, hh_ready, hh_turned, hhT_ready, y_step, ye_ready, pt_ready, sc_full,
         sc_added) = (sem(n) for n in (
            "xe_full", "xe_ready", "ab_full", "silu_done", "hh_ready", "hh_turned", "hhT_ready", "y_step",
            "ye_ready", "pt_ready", "sc_full", "sc_added"))
        out_written = sem("out_written")

        def cols(w, c0, k=KD, n=CW):
            return (lambda s: ring[:, s, 0:k * n].rearrange("p (k c) -> p k c", k=k),
                    w.rearrange("(k p) c -> p k c", p=P)[:, :, c0:c0 + n])

        chunks = []
        QKV0 = 3 * HW
        for g in range(GROUPS):
            for part in range(3):
                n = len(chunks)
                chunks.append(cols(w_in, QKV0 + part * AW + g * CW) + (qkv_full, 4 * (n + 1)))
        HY_C = len(chunks)
        for j in range(HYT // 2):
            chunks.append(cols(w_in, j * CW) + (hy_full, 2 * (j + 1)))
        GATE_C = len(chunks)
        for j in range(KD):
            chunks.append(cols(w_gate, j * CW) + (gate_full, 2 * (j + 1)))
        MIX_C = len(chunks)
        for j in range(4):
            chunks.append(cols(w_up_hy, j * CW, HC) + (mix_full, 2 * (j + 1)))
        OUT_C = len(chunks)
        for j in range(4):
            chunks.append(cols(w_out, j * CW) + (out_full, 4 * (j + 1)))
        KV_C = len(chunks)
        for j in range(4):
            chunks.append(cols(w_kv_mem, j * CW) + (kv_full, 2 * (j + 1)))
        QX_C = len(chunks)
        for j in range(2):
            chunks.append(cols(w_q_x, j * CW) + (qx_full, 2 * (j + 1)))
        XO_C = len(chunks)
        for j in range(2):
            chunks.append(cols(w_o_x, j * 512, 4, 512) + (xo_full, 7 + j))
        MOE_C = len(chunks)
        GATE, UP, DOWN = range(3)
        steps = [(ex, j) for ex in range(2) for j in range(FB)]
        pair = []
        for i, (ex, j) in enumerate(steps):
            pair += [(ex, part, j, part2) for part2 in range(2) for part in (GATE, UP)]
            if i >= 1:
                pair += [(*steps[i - 1][:1], DOWN, steps[i - 1][1], part2) for part2 in range(2)]
        pair += [(1, DOWN, FB - 1, part2) for part2 in range(2)]
        place = {c: i for i, c in enumerate(pair)}
        assert MOE_C % RING0 == 0
        assert len(pair) % RING == 0

        slots, loads = [], []
        for n in range(MOE_C + 2 * RING):
            k = n % RING0 if n < MOE_C else (n - MOE_C + RING0) % RING
            earlier = [i for i in range(n) if slots[i] == k]
            slots.append(k)
            loads.append(len(earlier) + 1)

        def slot(n):
            return slots[n] if n < MOE_C else (n - MOE_C + RING0) % RING

        def load_count(n):
            if n < MOE_C + RING:
                return loads[n]
            return loads[MOE_C + (n - MOE_C) % RING] + (n - MOE_C) // RING

        def arrived(eng, n):
            eng.wait_ge(slot_loaded[slot(n)], 16 * load_count(n))

        def wview(n, k=KD, c=CW):
            return slot_memory(slot(n))[:, 0:k * c].rearrange("p (k c) -> p k c", k=k)

        block = ctx.enter_context(nc.Block())

        @block.sync
        def _(sp):
            def token_tile(a):
                sp.dma_start(xs[:, a, :], x[0].rearrange("(m a) d -> m a d", a=NT)[:, a, :]).then_inc(ld_x[a], 16)

            token_tile(0)
            sp.dma_start(ident[:, :], c_ident).then_inc(ld_ident, 16)
            token_tile(1)
            sp.dma_start(vrow[0:V_ROWS, 0, :], vectors).then_inc(ld_vec, 16)
            sp.dma_start(vrow[0:V_COLS - V_CW, 1, :], taps).then_inc(ld_vec, 16)
            token_tile(2)
            token_tile(3)
            def expert_chunk(q, i):
                ex, part, j, part2 = pair[i]
                e = 2 * q + ex
                dst = slot_memory(slot(MOE_C + i))
                if part != DOWN:
                    w = (w_e_gate, w_e_up)[part]
                    src = w[e].rearrange("(k p) f -> p k f", p=P)[:, 4 * part2:4 * part2 + 4, j * BW:(j + 1) * BW]
                    dst = dst.rearrange("p (k c) -> p k c", k=4)
                else:
                    r0 = j * BW + part2 * 2 * P
                    src = w_e_down[e, r0:r0 + 2 * P, :].rearrange("(k p) d -> p k d", p=P)
                    dst = dst.rearrange("p (k c) -> p k c", k=2)
                sp.dma_start(dst, src).then_inc(slot_loaded[slot(MOE_C + i)], 16)

            def freed_in_pair(q, i):
                ex, part, j, part2 = pair[i]
                halves = q * 4 * FB + (2 * (ex * FB + j) + part2 + 1)
                if part != DOWN:
                    sp.wait_ge(ab_full, halves)
                else:
                    sp.wait_ge(y_step, halves)

            for n, (dst, src, _, _) in enumerate(chunks):
                if n >= RING0:
                    sp.wait_ge(chunks[n - RING0][2], chunks[n - RING0][3])
                sp.dma_start(dst(slot(n)), src).then_inc(slot_loaded[slot(n)], 16)
                if n == OUT_C + RING0:
                    sp.wait_ge(mix_done, KD)
                    for i in range(OWN - RING0):
                        expert_chunk(0, i)
            sp.wait_ge(xo_full, 8)
            for i in (*range(OWN - RING0, OWN - RING0 + 6), *range(RING - RING0, RING)):
                expert_chunk(0, i)
            sp.wait_ge(r_full, NT)
            for i in range(OWN - RING0 + 6, RING - RING0):
                expert_chunk(0, i)
            for i in range(RING, len(pair)):
                freed_in_pair(0, i - RING)
                expert_chunk(0, i)
            with sp.Fori(1, NE // 2) as q:
                for i in range(len(pair)):
                    if i < RING:
                        freed_in_pair(q - 1, len(pair) - RING + i)
                    else:
                        freed_in_pair(q, i - RING)
                    expert_chunk(q, i)
            for a in range(NT):
                sp.wait_ge(norms["fin"]["scaled"], a + 1)
                sp.dma_start(out[0].rearrange("(m a) d -> m a d", a=NT)[:, a, :], hT_out(a)).then_inc(out_written, 16)
            sp.wait_ge(out_written, 16 * NT)

        @block.gpsimd
        def _(pool):
            pool.dma_start(embT, c_embT).then_inc(ld_filt, 16)
            pool.dma_start(fw1, filt_w1).then_inc(ld_filt, 16)
            pool.dma_start(fw2, filt_w2).then_inc(ld_filt, 16)
            pool.dma_start(fcol[:, :], filt_vectors).then_inc(ld_filt, 16)
            pool.dma_start(rcos, c_rcos).then_inc(ld_rope, 16)
            pool.dma_start(rsin, c_rsin).then_inc(ld_rope, 16)
            pool.dma_start(masks, c_mask).then_inc(ld_mask, 16)
            nc.gpsimd.memset(wr[:, :, :], 0.0).then_inc(spare_zero, 1)
            pool.wait_ge(spare_zero, 1)
            pool.dma_start(wr[:, :, 0:NE], w_router.rearrange("(k p) e -> p k e", p=P)).then_inc(ld_wr, 16)
            pool.dma_start(sum4[:, :], c_sum4).then_inc(ld_wr, 16)
            nc.gpsimd.memset(spare[:, 0:6144], 0.0).then_inc(spare_zero, 1)
            pool.wait_ge(spare_zero, 2)
            nc.gpsimd.memset(h2T[FFN:P, :], 0.0).then_inc(spare_zero, 1)
            pool.wait_ge(spare_zero, 3)
            pool.wait_ge(vec_turned, 2)
            nc.gpsimd.memset(w3u[FFN:P, :, :], 0.0).then_inc(spare_zero, 1)
            pool.wait_ge(spare_zero, 4)
            w3v = filt_w3.rearrange("k (o d c) -> k o d c", o=2, d=2)
            for u in range(2 * NU):
                o, th = u // NU, u % NU
                if u >= 1:
                    pool.wait_ge(f_full, 4 * u)
                pool.dma_start(w3u[0:FFN, :, :], w3v[:, o, :, th * CH:(th + 1) * CH]).then_inc(ld_w3, 16)
                if u >= 1:
                    pool.wait_ge(pchain, 4 * u)
                pool.dma_start(dec, c_decay[:, :, th * CH:(th + 1) * CH]).then_inc(ld_dec, 16)
                if u == 0:
                    for dst, src in ((dftc, c_dftc), (dfts, c_dfts)):
                        pool.dma_start(dst, src).then_inc(ld_dft, 16)
                    pool.wait_ge(roped, 24)
                    pool.dma_start(dftsk, c_dftsk).then_inc(ld_dft, 16)
                if u == 1:
                    pool.wait_ge(o_full, 8)
                    for dst, src in ((idftc, c_idftc), (idfts, c_idfts)):
                        pool.dma_start(dst, src).then_inc(ld_idft, 16)
                pool.wait_ge(ld_dec, 16 * (u + 1))
                pool.wait_ge(f_copied, 4 * (u + 1))
                if u >= 1:
                    pool.wait_ge(k_full, 4 * u)
                nc.gpsimd.tensor_tensor(ff, ff, dec, ALU.mult).then_inc(pchain, 1)
                link_n = 4 * u + 2
                nc.gpsimd.tensor_tensor(fb, fb, dec, ALU.mult).then_inc(pchain, 1)
                pool.wait_ge(pchain, link_n)
                nc.gpsimd.memset(fb[0:1, 0, :], 0.0).then_inc(pchain, 1)
                pool.wait_ge(pchain, link_n + 1)
                nc.gpsimd.tensor_tensor(fs, ff, fb, ALU.add).then_inc(pchain, 1)
                pool.wait_ge(pchain, link_n + 2)
                nc.gpsimd.tensor_tensor(ff, ff, fb, ALU.subtract).then_inc(f_sumdif, 1)
            pool.wait_ge(z_new, 2 * NU)
            pool.dma_start(wua, w_up_attn.rearrange("(k p) c -> p k c", p=P)).then_inc(ld_wua, 16)
            pool.wait_ge(prod, 2 * NU)
            pool.wait_ge(y_full, 2 * HC)
            pool.dma_start(mems, mem[0].rearrange("(m b) d -> m b d", b=MT)).then_inc(ld_mem, 16)
            pool.wait_ge(ox_full, XH)
            pool.wait_ge(xo_full, 8)
            pool.dma_start(slot_no, c_slot_no).then_inc(ld_moe, 16)
            pool.dma_start(W[:, 4096:4352], c_count).then_inc(ld_moe, 16)
            pool.wait_ge(top_done, 1)
            pool.dma_start(gf, ln_f_g.partition_broadcast(P)).then_inc(ld_gf, 16)

        def gate_tiles(u):
            per = [3, 3, 2, 3, 2, 3]
            return sum(per[:u]), sum(per[:u + 1])

        def turn_banks(u):
            following = (gate_tiles(u)[0] - 1) % 2
            return (following, 1 - following)

        def scratch(tag):
            if tag == "fin":
                return W[:, 8704:9728]
            return UT[:, 5120:6144] if tag in ("mix", "mem") else UT[:, 8192:9216]

        def norm_scalar(act, tag, src, n, pieces, ready):
            s = norms[tag]
            w = D // pieces
            junk = scratch(tag)
            for i in range(n * pieces):
                j, a = i // n, i % n
                ready(a, j)
                if i >= 1:
                    act.wait_ge(s["sq"], i)
                c = a * pieces + j
                nc.scalar.activation(junk[:, 0:w], src[:, a, j * w:(j + 1) * w], ACT.Square,
                                     accum_out=st[:, c:c + 1]).then_inc(s["sq"], 1)
            act.wait_ge(s["var"], 1)
            nc.scalar.activation(st[:, 20:20 + n], st[:, 16:16 + n], ACT.Sqrt).then_inc(s["sqrt"], 1)

        def norm_vector(dve, link, tag, src, dst, n, pieces):
            s = norms[tag]
            dve.wait_ge(s["sq"], n * pieces)
            r, v, t = st[:, 24:24 + n], st[:, 16:16 + n], st[:, 28:28 + n]
            if pieces > 1:
                link(nc.vector.tensor_reduce(t, st[:, 0:n * pieces].rearrange("p (a j) -> p a j", a=n), AX.X, ALU.add))
                nc.vector.tensor_scalar(v, t, 1.0 / D, EPS, ALU.mult, ALU.add).then_inc(s["var"], 1)
            else:
                nc.vector.tensor_scalar(v, st[:, 0:n], 1.0 / D, EPS, ALU.mult, ALU.add).then_inc(s["var"], 1)
            dve.wait_ge(s["sqrt"], 1)
            link(nc.vector.reciprocal(r, st[:, 20:20 + n]))
            link(nc.vector.tensor_tensor(t, r, r, ALU.mult))
            link(nc.vector.tensor_tensor(t, t, v, ALU.mult))
            link(nc.vector.tensor_scalar(t, t, -0.5, 1.5, ALU.mult, ALU.add))
            link(nc.vector.tensor_tensor(r, r, t, ALU.mult))
            for a in range(n):
                nc.vector.tensor_scalar(dst[:, a, :], src[:, a, :], st[:, 24 + a:25 + a], None,
                                        ALU.mult).then_inc(s["scaled"], 1)

        def norm_tensor(pe, tag, src, n, bank0):
            s = norms[tag]
            pe.wait_ge(s["scaled"], n)
            for k in range(KD):
                if k >= 4:
                    pe.wait_ge(s["evA" if k % 2 == 0 else "evV"], k // 2 - 1)
                for a in range(n):
                    mm = pe.transpose(ps[:, bank0 + k % 4, a * P:(a + 1) * P], src[:, a, k * P:(k + 1) * P], ident[:, :])
                mm.then_inc(s["turned"], 1)

        def square_root(act, tag, src, a):
            s = norms[tag]
            if a >= 1:
                act.wait_ge(s["sq"], a)
            nc.scalar.activation(scratch(tag), src[:, a, :], ACT.Square, accum_out=st[:, a:a + 1]).then_inc(s["sq"], 1)
            act.wait_ge(s["sq"], a + 1)
            nc.scalar.activation(st[:, 20 + a:21 + a], st[:, a:a + 1], ACT.Sqrt, bias=eps[:, 0:1],
                                 scale=1.0 / D).then_inc(s["sqrt"], 1)

        def tiles_scalar(act, tag, src, ready):
            for a in range(NT):
                ready(a)
                square_root(act, tag, src, a)

        def load_sqrt(act):
            nc.scalar.activation(eps[:, 1:2], eps[:, 0:1], ACT.Sqrt).then_inc(table_loaded, 1)

        def tile_root(dve, link, tag, a):
            s = norms[tag]
            v, q, r, t = (st[:, c + a:c + a + 1] for c in (16, 20, 24, 28))
            dve.wait_ge(s["sqrt"], a + 1)
            nc.vector.tensor_scalar(v, st[:, a:a + 1], 1.0 / D, EPS, ALU.mult, ALU.add)
            link(nc.vector.reciprocal(r, q))
            link(nc.vector.tensor_tensor(t, r, r, ALU.mult))
            link(nc.vector.tensor_tensor(t, t, v, ALU.mult))
            link(nc.vector.tensor_scalar(t, t, -0.5, 1.5, ALU.mult, ALU.add))
            if tag == "fin":
                nc.vector.tensor_tensor(r, r, t, ALU.mult).then_inc(s["rooted"], 1)
            else:
                link(nc.vector.tensor_tensor(r, r, t, ALU.mult))

        def tile_vector(dve, link, tag, src, dst, a):
            tile_root(dve, link, tag, a)
            nc.vector.tensor_scalar(dst[:, a, :], src[:, a, :], st[:, 24 + a:25 + a], None,
                                    ALU.mult).then_inc(norms[tag]["scaled"], 1)

        def tile_turn(pe, tag, src, a, banks):
            s = norms[tag]
            pe.wait_ge(s["scaled"], a + 1)
            for k in range(KD):
                if a == 2 and k % 2 == 0 and banks[0] == banks[1]:
                    pe.wait_ge(s["evA" if k // 2 % 2 == 0 else "evV"], k // 4 + 1)
                c0 = (k % 2) * 2 * P + (a % 2) * P
                mm = pe.transpose(ps[:, banks[a // 2] + k // 2, c0:c0 + P], src[:, a, k * P:(k + 1) * P], ident[:, :])
                if a % 2 == 1 and k % 2 == 1:
                    mm.then_inc(s["turned"], 1)

        def pair_evac(eng, tag, dst, half, banks, col, par):
            s = norms[tag]
            for b in (par, par + 2):
                eng.wait_ge(s["turned"], 4 * half + b + 1)
                for i in range(2):
                    k = 2 * b + i
                    d_ = dst[:, k, 2 * half * P:2 * (half + 1) * P]
                    src = ps[:, banks[half] + b, i * 2 * P:(i + 1) * 2 * P]
                    if par == 0:
                        ins = nc.scalar.activation(d_, src, ACT.Copy, scale=vcol[:, col + k:col + k + 1])
                    else:
                        ins = nc.vector.tensor_scalar(d_, src, vcol[:, col + k:col + k + 1], None, ALU.mult)
                ins.then_inc(s["evA" if par == 0 else "evV"], 1)

        def norm_evac(eng, tag, dst, n, bank0, col, par):
            s = norms[tag]
            for k in range(par, KD, 2):
                eng.wait_ge(s["turned"], k + 1)
                src = ps[:, bank0 + k % 4, 0:n * P]
                if par == 0:
                    nc.scalar.activation(dst[:, k, :], src, ACT.Copy, scale=vcol[:, col + k:col + k + 1]).then_inc(s["evA"], 1)
                else:
                    nc.vector.tensor_scalar(dst[:, k, :], src, vcol[:, col + k:col + k + 1], None,
                                            ALU.mult).then_inc(s["evV"], 1)

        @block.scalar
        def _(act):
            act.wait_ge(eps_ready, 1)
            load_sqrt(act)
            tiles_scalar(act, "mix", xs, lambda a: act.wait_ge(ld_x[a], 16))
            act.wait_ge(vec_ready, 2)
            for half in range(2):
                pair_evac(act, "mix", hT, half, (0, 4), V_MIX, 0)
            for i, dst in enumerate((h1T, h2T[0:FFN, :])):
                act.wait_ge(mlp_arg, i + 1)
                nc.scalar.activation(dst, farg, ACT.Sin).then_inc(mlp_sin, 1)

            for c in range(9):
                g, part = c // 3, c % 3
                for a in range(NT):
                    n = 4 * c + a
                    if part == 2:
                        act.wait_ge(qkv_full, n + 1)
                        nc.scalar.copy(vnat[:, a, g * CW:(g + 1) * CW], ps[:, n % 4, 0:CW]).then_inc(v_copied, 1)
                    else:
                        m = 8 * g + 4 * part + a
                        act.wait_ge(qk_turned, m + 1)
                        src = ps[:, 4 + m % 4, 0:2 * P].rearrange("p (r t) -> p r t", r=2)
                        if part == 0:
                            act.wait_ge(spare_zero, 2)
                            nc.scalar.copy(qz[0:64, g, 0:4:2, a * P:(a + 1) * P], src[0:64])
                            nc.scalar.copy(qz[64:P, g, 1:4:2, a * P:(a + 1) * P], src[64:P]).then_inc(qk_copied, 1)
                        else:
                            nc.scalar.copy(kT[:, g, :, a * P:(a + 1) * P], src).then_inc(qk_copied, 1)

            def filter_copies(u):
                for d, dst in ((0, ff), (1, fb)):
                    for j in range(2):
                        i = 4 * u + 2 * d + j
                        act.wait_ge(f_full, i + 1)
                        if u >= 1 and d == 0 and j == 0:
                            act.wait_ge(k_full, 4 * u)
                        if u >= 1 and d == 1 and j == 0:
                            act.wait_ge(f_sumdif, u)
                        nc.scalar.copy(dst[:, 2 * j:2 * j + 2, :], ps[:, 4 + i % 4, :].rearrange(
                            "p (a c) -> p a c", a=2)).then_inc(f_copied, 1)

            def centre(m):
                act.wait_ge(hy_full, m + 1)
                nc.scalar.activation(uT[:, m, :], ps[:, m % 2, :], ACT.Identity, bias=vcol[:, V_CB + m:V_CB + m + 1],
                                     scale=vcol[:, V_CW + HYT + m:V_CW + HYT + m + 1]).then_inc(hy_centre, 1)

            filter_copies(0)
            for p in range(16):
                act.wait_ge(s_negmax, p + 1)
                nc.scalar.activation(Sb[:, p % 2, :], Sb[:, p % 2, :], ACT.Exp, bias=st[:, 34 + p % 2:35 + p % 2],
                                     accum_out=st[:, 36 + p % 2:37 + p % 2]).then_inc(s_exp, 1)
                if p == 0:
                    act.wait_ge(mlp_sin, 2)
                    act.wait_ge(norms["mix"]["evA"], 4)
                centre(p)
                act.wait_ge(p_turned, p + 1)
                if p >= 2:
                    act.wait_ge(o_full, p // 2)
                nc.scalar.copy(PTb[:, p % 2, :], psc(4, 6, NKEY)).then_inc(p_copied, 1)
            centre(16)
            centre(17)

            def even_copies(full, base, bank0, bufs, done):
                for i in range(4):
                    act.wait_ge(full, base + i + 1)
                    nc.scalar.copy(bufs[i % 2][:, i // 2, :], ps[:, bank0 + i, 0:CH]).then_inc(done, 1)

            def z_copies(u):
                o, th = u // NU, u % NU
                if u >= 1:
                    act.wait_ge(z_full, 4 * u)
                for i, b in enumerate(turn_banks(u)):
                    act.wait_ge(z_turned, 2 * u + i + 1)
                    nc.scalar.copy(znat[:, 2 * i:2 * i + 2, :], ps[:, 2 + b, :].rearrange(
                        "p (a c) -> p a c", a=2)).then_inc(z_copied, 1)

            z_copies(0)
            even_copies(k_full, 0, 4, EV(Kb[0]), k_even)
            for u in range(2 * NU):
                if u >= 1:
                    act.wait_ge(prod, u)
                even_copies(z_full, 4 * u, 0, EV(Zb), z_even)
                if u == 0:
                    filter_copies(1)
                elif u + 1 < 2 * NU:
                    act.wait_ge(y_full, 2 * u)
                    even_copies(k_full, 4 * (u + 1), 4, EV(Kb[(u + 1) % 2]), k_even)
                first, end = gate_tiles(u)
                for i in range(first, end):
                    if i == end - 1:
                        if u == 0:
                            even_copies(k_full, 4, 4, EV(Kb[1]), k_even)
                        if u + 2 < 2 * NU:
                            filter_copies(u + 2)
                        if u + 1 < 2 * NU:
                            z_copies(u + 1)
                    act.wait_ge(gate_full, i + 1)
                    nc.scalar.activation(gates[:, i, :], ps[:, 2 + i % 2, :], ACT.Sigmoid,
                                         bias=vcol[:, V_BG + i:V_BG + i + 1]).then_inc(gate_done, 1)

            norm_scalar(act, "mem", mems, MT, 1, lambda a, j: act.wait_ge(ld_mem, 16))
            norm_evac(act, "mem", mnT, MT, 0, V_MEM, 0)
            norm_scalar(act, "xa", xs, NT, 4, lambda a, j: act.wait_ge(out_added, 4 * j + a + 1))
            for i in range(8):
                act.wait_ge(kv_full, i + 1)
                if i < 4:
                    nc.scalar.copy(kxT[:, i, :], ps[:, 4 + i % 4, 0:MEM]).then_inc(kv_copied, 1)
                else:
                    j, b = (i - 4) // 2, i % 2
                    nc.scalar.copy(vx[:, b, j * CW:(j + 1) * CW], ps[:, 4 + i % 4, 0:CW]).then_inc(kv_copied, 1)
            norm_evac(act, "xa", hT, NT, 0, V_X, 0)
            def load_exp():
                nc.scalar.activation(eps[:, 1:2], eps[:, 0:1], ACT.Exp).then_inc(table_loaded, 1)

            load_exp()

            def qx_copy(h):
                act.wait_ge(qx_full, h + 1)
                nc.scalar.copy(qxT[:, h, :], ps[:, 4 + h, :]).then_inc(qx_copied, 1)

            def x_exp(h):
                for a in range(NT):
                    act.wait_ge(sx_negmax, 4 * h + 2 * (a // 2) + 2)
                    if h >= 2 and a == 0:
                        act.wait_ge(px_turned, 2 * (h - 1))
                    c = 40 + (h % 2) * 4 + a
                    nc.scalar.activation(Px[:, h % 2, a, :], ps[:, 2 * (h % 2) + a // 2, (a % 2) * MEM:(a % 2 + 1) * MEM],
                                         ACT.Exp, bias=st[:, c:c + 1], scale=float(P) ** -0.5,
                                         accum_out=st[:, c + 8:c + 9]).then_inc(sx_exp, 1)

            def px_copy(h):
                if h >= 2:
                    act.wait_ge(ox_full, h - 1)
                for b in range(MT):
                    act.wait_ge(px_turned, 2 * h + b + 1)
                    nc.scalar.copy(PTx[:, h % 2, b, :], ps[:, 4 + 2 * (h % 2) + b, :]).then_inc(px_copied, 1)

            def ox_copy(h):
                act.wait_ge(ox_full, h + 1)
                nc.scalar.copy(oxT[:, h, :], ps[:, 4 + 2 * (h % 2), :]).then_inc(ox_copied, 1)

            qx_copy(0)
            qx_copy(1)
            x_exp(0)
            qx_copy(2)
            x_exp(1)
            for h in range(XH):
                px_copy(h)
                if h == 0:
                    qx_copy(3)
                if h + 2 < XH:
                    x_exp(h + 2)
                if h >= 1:
                    ox_copy(h - 1)
            ox_copy(XH - 1)
            act.wait_ge(table_loaded, 2)
            load_sqrt(act)
            for a in range(NT):
                act.wait_ge(xo_added, 2 * a + 2)
                square_root(act, "moe", xs, a)
                if a == 2:
                    pair_evac(act, "moe", hT, 0, (4, 4), V_MOE, 0)
            pair_evac(act, "moe", hT, 1, (4, 4), V_MOE, 0)
            act.wait_ge(rp_full, 1)
            nc.scalar.copy(lgT[:, 0:2 * P], ps[:, 0, 0:2 * P]).then_inc(rp_copied[0], 1)
            act.wait_ge(table_loaded, 3)
            load_exp()
            act.wait_ge(r_shifted, 1)
            nc.scalar.activation(lg, lg, ACT.Exp).then_inc(r_exp, 1)
            with act.Fori(0, NE // 2) as q:
                for x in range(2):
                    for j in range(FB):
                        e = 2 * q + x
                        act.wait_ge(ab_full, e * (2 * FB) + 2 * (j + 1))
                        nc.scalar.activation(sil[:, j % 2, :], ps[0:CAP, j % 2, :], ACT.Silu).then_inc(silu_done, 1)
                        if x == 0 and j == 0:
                            for h in range(2):
                                act.wait_ge(pt_turned, 2 * q + (h + 1))
                                nc.scalar.copy(PT[:, h, :], ps[:, 4 + h, :]).then_inc(pt_ready, 1)
            act.wait_ge(table_loaded, 4)
            load_sqrt(act)
            s = norms["fin"]
            for a in range(NT + 1):
                if a < NT:
                    act.wait_ge(sc_added, NE * 4 - 8 + 2 * a + 2)
                    square_root(act, "fin", xs, a)
                if a >= 1:
                    act.wait_ge(s["rooted"], a)
                    nc.scalar.activation(hn[:, a - 1, :], xs[:, a - 1, :], ACT.Copy,
                                         scale=st[:, 23 + a:24 + a]).then_inc(s["evA"], 1)

        @block.tensor
        def _(pe):
            def product(out_, pairs):
                last = len(pairs) - 1
                for i, (l, r) in enumerate(pairs):
                    mm = pe.matmul(out_, l, r, start=i == 0, stop=i == last)
                return mm

            pe.wait_ge(ld_ident, 16)
            tile_turn(pe, "mix", hn, 0, (0, 4))
            tile_turn(pe, "mix", hn, 1, (0, 4))
            pe.wait_ge(ld_vec, 32)
            pe.transpose(ps[:, 6, 0:V_ROWS], vrow[0:V_ROWS, 0, :], ident[0:V_ROWS, 0:V_ROWS]).then_inc(vec_turned, 1)
            pe.transpose(ps[:, 7, 0:54], vrow[0:54, 1, :], ident[0:54, 0:54]).then_inc(vec_turned, 1)
            pe.wait_ge(vec_ready, 2)
            for a in (2, 3):
                tile_turn(pe, "mix", hn, a, (0, 4))

            pe.wait_ge(norms["mix"]["evA"], 4)
            pe.wait_ge(norms["mix"]["evV"], 4)
            pe.wait_ge(ld_filt, 16 * 4)
            pe.matmul(ps[0:FFN, 7, :], fw1, embT, start=True, stop=True).then_inc(mlp_mm, 1)

            def turn_heads(m):
                pe.wait_ge(roped, m + 1)
                if m >= 4:
                    pe.wait_ge(qk_copied, m - 3)
                elif m == 3:
                    pe.wait_ge(mlp_arg, 2)
                for r in range(2):
                    mm = pe.transpose(ps[:, 4 + m % 4, r * P:(r + 1) * P], rope_out[:, m % 2, r * P:(r + 1) * P], ident[:, :])
                mm.then_inc(qk_turned, 1)

            done = 0
            for c in range(9):
                g, part = c // 3, c % 3
                arrived(pe, c)
                for a in range(NT):
                    n = 4 * c + a
                    if n == 3:
                        pe.wait_ge(mlp_sin, 1)
                        pe.matmul(ps[0:FFN, 7, :], fw2, h1T, start=True, stop=True).then_inc(mlp_mm, 1)
                    if n >= 4:
                        c4, a4 = c - 1, a
                        if c4 % 3 == 2:
                            pe.wait_ge(v_copied, 4 * (c4 // 3) + a4 + 1)
                        else:
                            pe.wait_ge(roped, 8 * (c4 // 3) + 4 * (c4 % 3) + a4 + 1)
                    product(ps[:, n % 4, 0:CW], [(hT[:, k, a * P:(a + 1) * P], wview(c)[:, k, :]) for k in range(KD)]
                            ).then_inc(qkv_full, 1)
                    if part < 2:
                        m = 8 * g + 4 * part + a
                        if m > done:
                            turn_heads(done)
                            done += 1
                    elif a == 0:
                        turn_heads(done)
                        done += 1

            def scores(p):
                a, h = p // 4, p % 4
                r = h // 2
                if p == 0:
                    pe.wait_ge(qk_copied, 24)
                    pe.wait_ge(v_copied, 12)
                    pe.wait_ge(roped, 24)
                else:
                    pe.wait_ge(s_masked, p)
                pe.matmul(ps[:, 2, :], qz[:, 0, h, a * P:(a + 1) * P], kT[:, 0, r, :], start=True, stop=True)
                for g in (1, 2):
                    mm = pe.matmul(ps[:, 3, (g - 1) * P:g * P], qz[:, g, h, a * P:(a + 1) * P], kT[:, g, r, a * P:(a + 1) * P],
                                   start=True, stop=True)
                mm.then_inc(s_full, 1)

            def hyena_tile(m):
                if m % 2 == 0:
                    arrived(pe, HY_C + m // 2)
                if m >= 2:
                    pe.wait_ge(hy_conv, m - 1)
                c0 = (m % 2) * P
                product(ps[:, m % 2, :], [(wview(HY_C + m // 2)[:, k, c0:c0 + P], hT[:, k, :]) for k in range(KD)]
                        ).then_inc(hy_full, 1)

            def turn_probs(p):
                pe.wait_ge(p_scaled, p + 1)
                if p >= 1:
                    pe.wait_ge(p_copied, p)
                else:
                    pe.wait_ge(f_copied, 4)
                for i in range(6):
                    mm = pe.transpose(ps[:, 4 + i // 4, (i % 4) * P:(i % 4 + 1) * P], Sb[:, p % 2, i * P:(i + 1) * P],
                                      ident[:, :])
                mm.then_inc(p_turned, 1)

            def values(n):
                pe.wait_ge(p_copied, 2 * n + 2)
                if n >= 1:
                    pe.wait_ge(at_copied, n)
                a = n // 2
                keys = [(0, b) for b in range(NT)] + [(1, a), (2, a)]
                for i, (g, b) in enumerate(keys):
                    for x in range(2):
                        c0 = g * CW + (n % 2) * P + x * 64
                        mm = pe.matmul(ps[64 * x:64 * x + 64, 6, 0:P], vnat[:, b, c0:c0 + 64], PTb[:, x, i * P:(i + 1) * P],
                                       start=i == 0, stop=i == 5)
                mm.then_inc(o_full, 1)

            def filter_time(u):
                pe.wait_ge(ld_w3, 16 * (u + 1))
                if u == 0:
                    pe.wait_ge(spare_zero, 4)
                for d in range(2):
                    for j in range(2):
                        i = 4 * u + 2 * d + j
                        if u >= 1:
                            pe.wait_ge(k_ready, 4 * u)
                        elif i == 0:
                            pe.wait_ge(qk_copied, 24)
                        for s in range(2):
                            a = 2 * j + s
                            mm = pe.matmul(ps[:, 4 + i % 4, s * CH:(s + 1) * CH], h2T[:, a * P:(a + 1) * P], w3u[:, d, :],
                                           start=True, stop=True)
                        mm.then_inc(f_full, 1)

            scores(0)
            filter_time(0)
            for p in range(16):
                hyena_tile(p)
                turn_probs(p)
                if p + 1 < 16:
                    scores(p + 1)
                if p % 2 == 1:
                    values(p // 2)
            hyena_tile(16)
            hyena_tile(17)

            def spectrum(u, bank0, cos_in, sin_in, full, special, upper_free=lambda: None):
                for j in range(2):
                    if j == 1:
                        upper_free()
                    fj = slice(j * P, (j + 1) * P)
                    product(ps[:, bank0 + 2 * j, 0:CH], [(dftc[:, a, fj], cos_in[:, a, :]) for a in (0, 2)])
                    product(ps[:, bank0 + 2 * j, CH:2 * CH], [(dftc[:, a, fj], cos_in[:, a, :]) for a in (1, 3)]
                            ).then_inc(full, 1)
                    if special and j == 0:
                        o_ = ps[:, bank0 + 1, 0:CH]
                        pe.matmul(o_, dftsk[:, 0, :], sin_in[:, 0, :], start=True, stop=False)
                        for a in (0, 2):
                            pe.matmul(o_[0:1, :], dfts[:, a, 0:1], cos_in[:, a, :], start=False, stop=False)
                        pe.matmul(o_, dftsk[:, 1, :], sin_in[:, 2, :], start=False, stop=True)
                    else:
                        product(ps[:, bank0 + 2 * j + 1, 0:CH], [(dfts[:, a, fj], sin_in[:, a, :]) for a in (0, 2)])
                    product(ps[:, bank0 + 2 * j + 1, CH:2 * CH], [(dfts[:, a, fj], sin_in[:, a, :]) for a in (1, 3)]
                            ).then_inc(full, 1)

            def filter_spectrum(u):
                pe.wait_ge(f_sumdif, u + 1)
                pe.wait_ge(f_copied, 4 * (u + 1))
                if u == 0:
                    pe.wait_ge(ld_dft, 16 * 3)
                    pe.wait_ge(p_copied, 16)
                    pe.wait_ge(at_copied, 8)
                spectrum(u, 4, fs, ff, k_full, True)

            def turn_z(u):
                th = u % NU
                if u < NU:
                    pe.wait_ge(hy_conv, 2 * th + 2)
                else:
                    pe.wait_ge(z_new, 2 * (u - NU + 1))
                if u == 0:
                    pe.wait_ge(s_exp, 16)
                else:
                    pe.wait_ge(gate_done, gate_tiles(u)[0] - 1)
                for i, b in enumerate(turn_banks(u)):
                    for c in range(4):
                        a, s = 2 * i + c // 2, c % 2
                        mm = pe.transpose(ps[:, 2 + b, c * P:(c + 1) * P], uT[:, 2 * th + s, a * P:(a + 1) * P], ident[:, :])
                    mm.then_inc(z_turned, 1)

            def gate_tile(i):
                if i % 2 == 0:
                    arrived(pe, GATE_C + i // 2)
                if i >= 2:
                    pe.wait_ge(gate_done, i - 1)
                c0 = (i % 2) * P
                product(ps[:, 2 + i % 2, :], [(wview(GATE_C + i // 2)[:, k, c0:c0 + P], hT[:, k, :]) for k in range(KD)]
                        ).then_inc(gate_full, 1)

            def z_spectrum(u):
                pe.wait_ge(z_copied, 2 * (u + 1))
                if u == 0:
                    pe.wait_ge(hy_conv, HYT)
                else:
                    pe.wait_ge(z_new, 2 * u)
                spectrum(u, 0, znat, znat, z_full, False,
                         lambda: pe.wait_ge(gate_done, gate_tiles(u)[0]) if u >= 1 else None)

            def inverse(u):
                pe.wait_ge(prod, u + 1)
                if u == 0:
                    pe.wait_ge(ld_idft, 32)
                Ue, Uo = Kb[u % 2][0], Kb[u % 2][2]
                Ve, Vo = t3, t1
                for s in range(2):
                    cs = slice(s * P, (s + 1) * P)
                    for par, (U_, V_) in enumerate(((Ue, Ve), (Uo, Vo))):
                        o_ = ps[:, s, :].rearrange("p (i q t) -> p i q t", i=2, q=2)[:, :, par, :]
                        pairs = []
                        for j in range(2):
                            for src, mat in ((U_, idftc), (V_, idfts)):
                                pairs.append((src[:, j, cs], mat[:, j, :].rearrange(
                                    "p (i q t) -> p i q t", i=2, q=2)[:, :, par, :]))
                        mm = product(o_, pairs)
                    mm.then_inc(y_full, 1)

            turn_z(0)
            filter_spectrum(0)
            for u in range(2 * NU):
                z_spectrum(u)
                if u == 0:
                    filter_time(1)
                elif u + 1 < 2 * NU:
                    filter_spectrum(u + 1)
                pe.wait_ge(z_ready, 4 * (u + 1))
                first, end = gate_tiles(u)
                for i in range(first, end - 1):
                    gate_tile(i)
                if u == 0:
                    filter_spectrum(1)
                inverse(u)
                if u + 2 < 2 * NU:
                    filter_time(u + 2)
                if u + 1 < 2 * NU:
                    turn_z(u + 1)
                    pe.wait_ge(z_copied, 2 * (u + 1) + 1)
                gate_tile(end - 1)

            pe.wait_ge(z_new, 4 * NU)
            pe.wait_ge(k_ready, 8 * NU)
            pe.wait_ge(z_ready, 8 * NU)
            pe.wait_ge(gate_done, 2 * KD)
            for m in range(KD):
                j, c0 = m // 2, (m % 2) * P
                if m == 0:
                    pe.wait_ge(ld_wua, 16)
                if m % 2 == 0:
                    arrived(pe, MIX_C + j)
                if m >= 2:
                    pe.wait_ge(mix_done, m - 1)
                b = 4 + 2 * (m % 2)
                product(ps[:, b, :], [(wview(MIX_C + j, HC)[:, k, c0:c0 + P], uT[:, k, :]) for k in range(HC)])
                product(ps[:, b + 1, :], [(wua[:, k, m * P:(m + 1) * P], attnT[:, k, :]) for k in range(2)]
                        ).then_inc(mix_full, 1)
            norm_tensor(pe, "mem", mhn, MT, 0)
            pe.wait_ge(mix_done, KD)
            for j in range(4):
                arrived(pe, OUT_C + j)
                for a in range(NT):
                    i = 4 * j + a
                    if i >= 4:
                        pe.wait_ge(out_added, i - 3)
                    product(ps[:, 4 + a, 0:CW], [(mixT[:, k, a * P:(a + 1) * P], wview(OUT_C + j)[:, k, :])
                                                 for k in range(KD)]).then_inc(out_full, 1)
            pe.wait_ge(norms["mem"]["evA"], 4)
            pe.wait_ge(norms["mem"]["evV"], 4)
            for i in range(8):
                if i % 2 == 0:
                    arrived(pe, KV_C + i // 2)
                w = wview(KV_C + i // 2)
                if i >= 4:
                    pe.wait_ge(kv_copied, i - 3)
                else:
                    pe.wait_ge(out_added, 13 + i)
                if i < 4:
                    c0 = (i % 2) * P
                    product(ps[:, 4 + i % 4, 0:MEM], [(w[:, k, c0:c0 + P], mnT[:, k, :]) for k in range(KD)]).then_inc(kv_full, 1)
                else:
                    b = i % 2
                    product(ps[:, 4 + i % 4, 0:CW], [(mnT[:, k, b * P:(b + 1) * P], w[:, k, :]) for k in range(KD)]
                            ).then_inc(kv_full, 1)
            norm_tensor(pe, "xa", hn, NT, 0)
            pe.wait_ge(norms["xa"]["evA"], 4)
            pe.wait_ge(norms["xa"]["evV"], 4)
            pe.wait_ge(kv_copied, 8)
            def queries(h):
                if h % 2 == 0:
                    arrived(pe, QX_C + h // 2)
                c0 = (h % 2) * P
                product(ps[:, 4 + h, :], [(wview(QX_C + h // 2)[:, k, c0:c0 + P], hT[:, k, :]) for k in range(KD)]
                        ).then_inc(qx_full, 1)

            def x_scores(h):
                pe.wait_ge(qx_copied, h + 1)
                for a in range(NT):
                    if h >= 2 and a == 0:
                        pe.wait_ge(sx_exp, 4 * (h - 1))
                    mm = pe.matmul(ps[:, 2 * (h % 2) + a // 2, (a % 2) * MEM:(a % 2 + 1) * MEM], qxT[:, h, a * P:(a + 1) * P],
                                   kxT[:, h, :], start=True, stop=True)
                    mm.then_inc(sx_full, 1)

            def x_turn(h):
                pe.wait_ge(sx_norm, 4 * (h + 1))
                if h < 2:
                    pe.wait_ge(qx_copied, 2 * h + 2)
                else:
                    pe.wait_ge(ox_copied, h - 1)
                    pe.wait_ge(px_copied, 2 * (h - 1))
                for b in range(MT):
                    for a in range(NT):
                        mm = pe.transpose(ps[:, 4 + 2 * (h % 2) + b, a * P:(a + 1) * P], Px[:, h % 2, a, b * P:(b + 1) * P],
                                          ident[:, :])
                    mm.then_inc(px_turned, 1)

            def x_values(h):
                pe.wait_ge(px_copied, 2 * (h + 1))
                product(ps[:, 4 + 2 * (h % 2), :], [(vx[:, b, h * P:(h + 1) * P], PTx[:, h % 2, b, :])
                                                    for b in range(MT)]).then_inc(ox_full, 1)

            queries(0)
            queries(1)
            x_scores(0)
            queries(2)
            x_scores(1)
            for h in range(XH):
                x_turn(h)
                if h == 0:
                    queries(3)
                if h + 2 < XH:
                    x_scores(h + 2)
                if h >= 1:
                    x_values(h - 1)
            x_values(XH - 1)
            pe.wait_ge(ox_copied, XH)
            arrived(pe, XO_C)
            arrived(pe, XO_C + 1)
            for a in range(NT):
                for j in range(2):
                    i = 2 * a + j
                    if i >= 4:
                        pe.wait_ge(xo_added, i - 3)
                    product(ps[:, i % 4, :], [(oxT[:, k, a * P:(a + 1) * P], wview(XO_C + j, 4, 512)[:, k, :])
                                              for k in range(XH)]).then_inc(xo_full, 1)
                if a in (1, 2):
                    tile_turn(pe, "moe", hn, a - 1, (4, 4))
            def partial_logits(half):
                pe.wait_ge(xo_added, 5 + half)
                pe.wait_ge(norms["moe"]["evA"], 2 * half + 2)
                pe.wait_ge(norms["moe"]["evV"], 2 * half + 2)
                for k in range(KD):
                    g = 32 * (k % 4)
                    mm = pe.matmul(ps[g:g + 32, half, 0:2 * P], wr[:, k, :], hT[:, k, 2 * half * P:2 * (half + 1) * P],
                                   start=k < 4, stop=k >= 4)
                mm.then_inc(rp_full, 1)

            pe.wait_ge(ld_wr, 32)
            tile_turn(pe, "moe", hn, 2, (4, 4))
            partial_logits(0)
            tile_turn(pe, "moe", hn, 3, (4, 4))
            partial_logits(1)
            for a in range(NT):
                pe.wait_ge(rp_copied[a // 2], 1)
                pe.matmul(ps[:, 4, a * NE:(a + 1) * NE], lgT[:, a * P:(a + 1) * P], sum4[:, :],
                          start=True, stop=True).then_inc(r_full, 1)
            pe.wait_ge(r_aff, 1)
            for a in range(NT):
                mm = pe.transpose(ps[0:NE, 0, a * P:(a + 1) * P], aff[:, a, :], ident[:, :])
            mm.then_inc(r_turned, 1)
            pe.wait_ge(top_done, 1)
            for a in range(NT):
                mm = pe.transpose(ps[:, 1, a * NE:(a + 1) * NE], chosenT[:, a * P:(a + 1) * P], ident[0:NE, 0:NE])
            mm.then_inc(sel_turned, 1)
            pe.wait_ge(sel_copied, 1)
            pe.wait_ge(ld_moe, 32)
            pe.matmul(ps[:, 2, 0:NT * NE], up_to, chosen[:, :, :].rearrange("p a e -> p (a e)"), start=True, stop=False)
            for d in range(1, NT):
                mm = pe.matmul(ps[:, 2, d * NE:NT * NE], ones, chosen[:, 0:NT - d, :].rearrange("p a e -> p (a e)"),
                               start=False, stop=d == NT - 1)
            mm.then_inc(sel_counted, 1)
            def gather(n):
                pe.wait_ge(pg_ready, 2 * n)
                for k in range(KD):
                    for a in range(NT):
                        mm = pe.matmul(ps[:, k // 4, (k % 4) * P:(k % 4 + 1) * P], hn[:, a, k * P:(k + 1) * P],
                                       Pg[:, a, :], start=a == 0, stop=a == NT - 1)
                    if k % 4 == 3:
                        mm.then_inc(xe_full, 1)

            def turn_table(q):
                pe.wait_ge(pw_ready, 2 * q + 2)
                for h in range(2):
                    for a in range(NT):
                        for row in range(2):
                            x = row ^ h
                            mm = pe.matmul(ps[CAP * row:CAP * row + CAP, 4 + h, a * P:(a + 1) * P],
                                           Pw[:, a, x * CAP:(x + 1) * CAP], ident[:, :], start=True, stop=True)
                    mm.then_inc(pt_turned, 1)

            def expert_pair(q, last):
                def gate_up(x, j):
                    for k in range(KD):
                        chunk = [MOE_C + place[x, part, j, k // 4] for part in (GATE, UP)]
                        if k % 4 == 0:
                            if x == 0 and j == 0:
                                pe.wait_ge(xe_ready, 2 * q + (k // 4 + 1))
                            for n in chunk:
                                pe.wait_ge(slot_loaded[slot(n)], q * (16 * len(pair) // RING) + 16 * load_count(n))
                        for half in range(2):
                            mm = pe.matmul(ps[CAP * half:CAP * half + CAP, j % 2, :], xeT[:, k, x * CAP:(x + 1) * CAP],
                                           wview(chunk[half], 4, BW)[:, k % 4, :], start=k == 0, stop=k == KD - 1)
                        if k % 4 == 3:
                            mm.then_inc(ab_full, 1)

                def down(x, j):
                    e = 2 * q + x
                    pe.wait_ge(hh_ready, e * FB + (j + 1))
                    for i in range(4):
                        c0 = (j % 2) * 2 * P + i * CAP
                        mm = pe.matmul(ps[:, 2, c0:c0 + CAP], hh[:, j % 2, i * P:(i + 1) * P], ident[0:CAP, 0:CAP],
                                       start=True, stop=True)
                    mm.then_inc(hh_turned, 1)
                    pe.wait_ge(hhT_ready, e * FB + (j + 1))
                    if j == 0 and x == 1:
                        pe.wait_ge(ye_ready, 4 * q + 2)
                    for i in range(4):
                        n = MOE_C + place[x, DOWN, j, i // 2]
                        w = wview(n, 2, D)
                        if i % 2 == 0:
                            pe.wait_ge(slot_loaded[slot(n)], q * (16 * len(pair) // RING) + 16 * load_count(n))
                        for row in range(2):
                            half = row ^ x
                            mm = pe.matmul(ps[CAP * row:CAP * row + CAP, 3, :], hhT[:, j % 2, i, :],
                                           w[:, i % 2, half * 512:(half + 1) * 512], start=j == 0 and i == 0,
                                           stop=j == FB - 1 and i == 3)
                        if i % 2 == 1:
                            mm.then_inc(y_step, 1)

                for x in range(2):
                    for j in range(FB):
                        if x == 0 and j == 0:
                            gate_up(0, 0)
                            turn_table(q)
                        if j + 1 < FB:
                            gate_up(x, j + 1)
                        elif x == 0:
                            gate_up(1, 0)
                        down(x, j)
                if not last:
                    gather(q + 2)
                pe.wait_ge(ye_ready, 4 * q + 4)
                pe.wait_ge(pt_ready, 2 * q + 2)
                for a in range(NT):
                    if a >= 2:
                        pe.wait_ge(sc_added, q * 8 + 2 * (a - 1))
                    for half in range(2):
                        pe.matmul(ps[:, 4 + 2 * (a % 2) + half, :], PT[:, half, a * P:(a + 1) * P], Y[:, half, :],
                                  start=True, stop=True).then_inc(sc_full, 1)

            gather(1)
            with pe.Fori(0, NE // 2 - 1) as q:
                expert_pair(q, False)
            expert_pair(NE // 2 - 1, True)

        @block.vector
        def _(dve):
            n = [0]

            def link(ins):
                n[0] += 1
                ins.then_inc(chain, 1)
                dve.wait_ge(chain, n[0])

            def reduce_angle(i):
                dve.wait_ge(mlp_mm, i + 1)
                if i == 1:
                    dve.wait_ge(mlp_sin, 1)
                link(nc.vector.tensor_scalar(farg, ps[0:FFN, 7, :], fcol[:, 2 * i:2 * i + 1], fcol[:, 2 * i + 1:2 * i + 2],
                                             ALU.add, ALU.mult))
                link(nc.vector.tensor_scalar(fk, farg, 1.0 / TWO_PI, MAGIC, ALU.mult, ALU.add))
                link(nc.vector.tensor_scalar(fk, fk, MAGIC, None, ALU.subtract))
                for c in (PI_A, PI_B, PI_C):
                    link(nc.vector.scalar_tensor_tensor(out=farg, in0=fk, scalar=-c, in1=farg, op0=ALU.mult, op1=ALU.add))
                nc.vector.tensor_scalar(farg, farg, 3.1415925, -3.1415925, ALU.min, ALU.max).then_inc(mlp_arg, 1)

            nc.vector.memset(eps[:, 0:1], EPS).then_inc(eps_ready, 1)
            for a in (0, 1):
                tile_vector(dve, link, "mix", xs, hn, a)
            dve.wait_ge(vec_turned, 2)
            nc.vector.tensor_copy(vcol[:, 0:V_ROWS], ps[:, 6, 0:V_ROWS]).then_inc(vec_ready, 1)
            nc.vector.tensor_copy(vcol[:, V_CW:V_COLS], ps[:, 7, 0:54]).then_inc(vec_ready, 1)
            dve.wait_ge(vec_ready, 2)
            for a in (2, 3):
                tile_vector(dve, link, "mix", xs, hn, a)
            for half in range(2):
                pair_evac(dve, "mix", hT, half, (0, 4), V_MIX, 1)
            dve.wait_ge(ld_filt, 16 * 4)
            reduce_angle(0)

            dve.wait_ge(ld_rope, 32)
            for g in range(GROUPS):
                for part in range(2):
                    for a in range(NT):
                        m = 8 * g + 4 * part + a
                        tile = 4 * (3 * g + part) + a
                        dve.wait_ge(qkv_full, tile + 1)
                        if m >= 1:
                            dve.wait_ge(roped, m)
                        src = ps[:, tile % 4, 0:CW].rearrange("p (h s c) -> p h s c", h=4, s=2)
                        A4 = ropeA.rearrange("p (h s c) -> p h s c", h=4, s=2)
                        B4 = ropeB.rearrange("p (h s c) -> p h s c", h=4, s=2)
                        cb = lambda t_, s: t_[:, a, s * 32:(s + 1) * 32].unsqueeze(1).to_broadcast([P, 4, 32])
                        for s in range(2):
                            nc.vector.tensor_tensor(A4[:, :, s, :], src[:, :, s, :], cb(rcos, s), ALU.mult)
                        nc.vector.tensor_tensor(B4[:, :, 0, :], src[:, :, 1, :], cb(rsin, 0), ALU.mult)
                        link(nc.vector.tensor_tensor(B4[:, :, 1, :], src[:, :, 0, :], cb(rsin, 1), ALU.mult))
                        if m >= 2:
                            dve.wait_ge(qk_turned, m - 1)
                        nc.vector.tensor_tensor(rope_out[:, m % 2, :], ropeA, ropeB, ALU.add).then_inc(roped, 1)
                        if m == 2:
                            reduce_angle(1)

            def softmax_head(p):
                a = p // 4
                dve.wait_ge(s_full, p + 1)
                if p == 0:
                    dve.wait_ge(ld_mask, 16)
                    dve.wait_ge(qk_turned, 24)
                if p >= 2:
                    dve.wait_ge(p_turned, p - 1)
                nc.vector.scalar_tensor_tensor(out=Sb[:, p % 2, :], in0=psc(2, 4, NKEY), scalar=0.125, in1=masks[:, a, :],
                                               op0=ALU.mult, op1=ALU.add).then_inc(s_masked, 1)
                dve.wait_ge(s_masked, p + 1)
                link(nc.vector.tensor_reduce(st[:, 32 + p % 2:33 + p % 2], Sb[:, p % 2, :], AX.X, ALU.max))
                nc.vector.tensor_scalar(st[:, 34 + p % 2:35 + p % 2], st[:, 32 + p % 2:33 + p % 2], -1.0, None,
                                        ALU.mult).then_inc(s_negmax, 1)

            def conv_sides(m):
                dve.wait_ge(hy_centre, m + 1)
                L, R = vcol[:, V_CW + m:V_CW + m + 1], vcol[:, V_CW + 2 * HYT + m:V_CW + 2 * HYT + m + 1]
                src, dst, n3 = ps[:, m % 2, :], uT[:, m, :], 3 * P

                def tap(d0, s0, cnt, w):
                    return nc.vector.scalar_tensor_tensor(out=dst[:, d0:d0 + cnt], in0=src[:, s0:s0 + cnt], scalar=w,
                                                          in1=dst[:, d0:d0 + cnt], op0=ALU.mult, op1=ALU.add)
                tap(P, 0, n3, L)
                link(tap(1, n3, P - 1, L))
                tap(0, P, n3, R)
                tap(n3, 1, P - 1, R).then_inc(hy_conv, 1)

            def scale_probs(p):
                dve.wait_ge(s_exp, p + 1)
                link(nc.vector.reciprocal(st[:, 38 + p % 2:39 + p % 2], st[:, 36 + p % 2:37 + p % 2]))
                nc.vector.tensor_scalar(Sb[:, p % 2, :], Sb[:, p % 2, :], st[:, 38 + p % 2:39 + p % 2], None,
                                        ALU.mult).then_inc(p_scaled, 1)

            def copy_attn(n):
                dve.wait_ge(o_full, n + 1)
                nc.vector.tensor_copy(attnT[:, n % 2, n // 2 * P:(n // 2 + 1) * P], ps[:, 6, 0:P]).then_inc(at_copied, 1)

            softmax_head(0)
            for p in range(16):
                scale_probs(p)
                conv_sides(p)
                if p + 1 < 16:
                    softmax_head(p + 1)
                if p % 2 == 1:
                    copy_attn(p // 2)
            conv_sides(16)
            conv_sides(17)

            TT = nc.vector.tensor_tensor

            def butterflies(base, full, even, bank0, B, done):
                for i in range(4):
                    j, s = i // 2, i % 2
                    dve.wait_ge(even, base + i + 1)
                    odd = ps[:, bank0 + i, CH:2 * CH]
                    e_ = EV(B)[s][:, j, :]
                    if s == 0:
                        link(nc.vector.tensor_tensor(B[0][:, j, :], e_, odd, ALU.add))
                        nc.vector.tensor_tensor(B[2][:, j, :], e_, odd, ALU.subtract).then_inc(done, 1)
                    else:
                        link(nc.vector.tensor_tensor(B[3][:, j, :], odd, e_, ALU.subtract))
                        nc.vector.tensor_tensor(B[1][:, j, :], e_, odd, ALU.add).then_inc(done, 1)

            def products(u):
                Zp, Z1, Zq, Z2 = ZP
                Kp, K1, Kq, K2 = Kb[u % 2]
                dve.wait_ge(z_ready, 4 * (u + 1))
                dve.wait_ge(k_ready, 4 * (u + 1))
                if u >= 1:
                    dve.wait_ge(y_full, 2 * u)
                TT(t1, Zp, K1, ALU.mult)
                TT(t2, Zq, K2, ALU.mult)
                link(TT(t3, Z1, Kp, ALU.mult))
                link(TT(t1, t1, t3, ALU.add))
                link(TT(t3, Z2, Kq, ALU.mult))
                link(TT(t2, t2, t3, ALU.add))
                TT(t3, t1, t2, ALU.subtract)
                link(TT(t1, t1, t2, ALU.add))
                TT(t2[0:1, 0, :], Z1[0:1, 0, :], K2[0:1, 0, :], ALU.mult)
                link(TT(t2[0:1, 1, :], Z2[0:1, 0, :], K1[0:1, 0, :], ALU.mult))
                TT(t3[0:1, 0, :], t2[0:1, 0, :], t2[0:1, 1, :], ALU.add)
                TT(Zp, Zp, Kp, ALU.mult)
                TT(Zq, Zq, Kq, ALU.mult)
                TT(Z1, Z1, K1, ALU.mult)
                link(TT(Z2, Z2, K2, ALU.mult))
                TT(K1, Z1, Z2, ALU.add)
                link(TT(K2, Z1, Z2, ALU.subtract))
                nc.vector.tensor_copy(t1[0:1, 0, :], K2[0:1, 0, :])
                nc.vector.memset(K1[0:1, 0, :], 0.0)
                TT(Kp, Zp, Zq, ALU.add)
                link(TT(Kq, Zp, Zq, ALU.subtract))
                nc.vector.memset(K2[0:1, 0, :], 0.0)
                link(TT(Kp, Kp, K1, ALU.subtract))
                TT(Kq, Kq, K2, ALU.subtract).then_inc(prod, 1)

            def gate(u):
                o, th = u // NU, u % NU
                for s in range(2):
                    m = 2 * th + s
                    dve.wait_ge(y_full, 2 * u + s + 1)
                    link(nc.vector.scalar_tensor_tensor(out=uT[:, m, :], in0=uT[:, m, :],
                                                        scalar=vcol[:, V_SKIP + o * HC + m:V_SKIP + o * HC + m + 1],
                                                        in1=ps[:, s, :], op0=ALU.mult, op1=ALU.add))
                    TT(uT[:, m, :], uT[:, m, :], uT[:, (o + 1) * HC + m, :], ALU.mult).then_inc(z_new, 1)

            butterflies(0, k_full, k_even, 4, Kb[0], k_ready)
            for u in range(2 * NU):
                butterflies(4 * u, z_full, z_even, 0, ZP, z_ready)
                products(u)
                if u + 1 < 2 * NU:
                    butterflies(4 * (u + 1), k_full, k_even, 4, Kb[(u + 1) % 2], k_ready)
                gate(u)

            norm_vector(dve, link, "mem", mems, mhn, MT, 1)
            for m in range(KD):
                b = 4 + 2 * (m % 2)
                dve.wait_ge(mix_full, m + 1)
                if m == 0:
                    dve.wait_ge(gate_done, 2 * KD)
                nc.vector.tensor_tensor(mt[:, 0, :], gates[:, m, :], ps[:, b, :], ALU.mult)
                link(nc.vector.tensor_tensor(mt[:, 1, :], gates[:, KD + m, :], ps[:, b + 1, :], ALU.mult))
                nc.vector.tensor_tensor(mixT[:, m, :], mt[:, 0, :], mt[:, 1, :], ALU.add).then_inc(mix_done, 1)
                dve.wait_ge(mix_done, m + 1)
            norm_evac(dve, "mem", mnT, MT, 0, V_MEM, 1)
            for i in range(16):
                j, a = i // 4, i % 4
                dve.wait_ge(out_full, i + 1)
                dst = xs[:, a, j * CW:(j + 1) * CW]
                nc.vector.tensor_tensor(dst, dst, ps[:, 4 + a, 0:CW], ALU.add).then_inc(out_added, 1)
            dve.wait_ge(out_added, 16)
            dve.wait_ge(out_full, 16)
            norm_vector(dve, link, "xa", xs, hn, NT, 4)
            norm_evac(dve, "xa", hT, NT, 0, V_X, 1)
            def x_max(h):
                for a in range(NT):
                    c = 40 + (h % 2) * 4 + a
                    dve.wait_ge(sx_full, 4 * h + 2 * (a // 2) + 2)
                    link(nc.vector.tensor_reduce(st[:, 56 + a:57 + a],
                                                 ps[:, 2 * (h % 2) + a // 2, (a % 2) * MEM:(a % 2 + 1) * MEM], AX.X, ALU.max))
                    nc.vector.tensor_scalar(st[:, c:c + 1], st[:, 56 + a:57 + a], -float(P) ** -0.5, None,
                                            ALU.mult).then_inc(sx_negmax, 1)

            def x_norm(h):
                for a in range(NT):
                    c = 40 + (h % 2) * 4 + a
                    dve.wait_ge(sx_exp, 4 * h + a + 1)
                    link(nc.vector.reciprocal(st[:, 60 + a:61 + a], st[:, c + 8:c + 9]))
                    nc.vector.tensor_scalar(Px[:, h % 2, a, :], Px[:, h % 2, a, :], st[:, 60 + a:61 + a], None,
                                            ALU.mult).then_inc(sx_norm, 1)

            for h in range(XH):
                x_max(h)
                x_norm(h)
            def add_projection(a):
                for j in range(2):
                    i = 2 * a + j
                    dve.wait_ge(xo_full, i + 1)
                    dst = xs[:, a, j * 512:(j + 1) * 512]
                    nc.vector.tensor_tensor(dst, dst, ps[:, i % 4, :], ALU.add).then_inc(xo_added, 1)

            for a in range(NT):
                add_projection(a)
                tile_vector(dve, link, "moe", xs, hn, a)
                if a == 2:
                    pair_evac(dve, "moe", hT, 0, (4, 4), V_MOE, 1)
            pair_evac(dve, "moe", hT, 1, (4, 4), V_MOE, 1)
            dve.wait_ge(rp_full, 2)
            nc.vector.tensor_copy(lgT[:, 2 * P:4 * P], ps[:, 1, 0:2 * P]).then_inc(rp_copied[1], 1)
            dve.wait_ge(r_full, NT)
            logits = ps[:, 4, 0:NT * NE].rearrange("p (a e) -> p a e", a=NT)
            per_token = lambda c: st[:, c:c + NT].unsqueeze(2).to_broadcast([P, NT, NE])
            link(nc.vector.tensor_reduce(st[:, 40:44], logits, AX.X, ALU.max))
            TT(lg, logits, per_token(40), ALU.subtract).then_inc(r_shifted, 1)
            dve.wait_ge(r_exp, 1)
            link(nc.vector.tensor_reduce(st[:, 44:48], lg, AX.X, ALU.add))
            link(nc.vector.reciprocal(st[:, 60:64], st[:, 44:48]))
            TT(aff, lg, per_token(60), ALU.mult).then_inc(r_aff, 1)
            dve.wait_ge(r_turned, 1)
            link(nc.vector.tensor_copy(affT.rearrange("e (m a) -> e a m", a=NT),
                                       ps[0:NE, 0, :].rearrange("e (a m) -> e a m", a=NT)))
            for r in range(CAP // 8):
                link(nc.vector.max(top8, affT))
                link(nc.vector.match_replace(affT, top8, affT, -1.0))
            nc.vector.tensor_scalar(chosenT.rearrange("e (a m) -> e m a", a=NT), affT.rearrange("e (m a) -> e m a", a=NT),
                                    0.0, None, ALU.is_lt).then_inc(top_done, 1)
            dve.wait_ge(sel_turned, 1)
            nc.vector.tensor_copy(chosen, ps[:, 1, 0:NT * NE].rearrange("p (a e) -> p a e", a=NT)).then_inc(sel_copied, 1)
            dve.wait_ge(sel_counted, 1)
            dve.wait_ge(ld_moe, 32)
            link(TT(place_of, ps[:, 2, 0:NT * NE].rearrange("p (a e) -> p a e", a=NT), chosen, ALU.mult))

            def gather_table(q):
                for x in range(2):
                    nc.vector.tensor_tensor(Pg[:, :, x * CAP:(x + 1) * CAP],
                                            place_of[:, :, bass.ds(2 * q + x, 1)].to_broadcast([P, NT, CAP]),
                                            slot_no.unsqueeze(1).to_broadcast([P, NT, CAP]), ALU.is_equal).then_inc(pg_ready, 1)

            def scatter_table(q):
                dve.wait_ge(pg_ready, 2 * q + 2)
                for x in range(2):
                    TT(Pw[:, :, x * CAP:(x + 1) * CAP], Pg[:, :, x * CAP:(x + 1) * CAP],
                       aff[:, :, bass.ds(2 * q + x, 1)].to_broadcast([P, NT, CAP]), ALU.mult).then_inc(pw_ready, 1)
                dve.wait_ge(pw_ready, 2 * q + 2)

            def gathered(n):
                for b in range(2):
                    dve.wait_ge(xe_full, 2 * (n - 1) + (b + 1))
                    TT(xeT[:, 4 * b:4 * b + 4, :], ps[:, b, :].rearrange("p (k s) -> p k s", k=4),
                       vcol[:, V_MOE + 4 * b:V_MOE + 4 * b + 4].unsqueeze(2).to_broadcast([P, 4, P]),
                       ALU.mult).then_inc(xe_ready, 1)

            def expert_pair(q, last):
                scatter_table(q)
                if not last:
                    gather_table(q + 1)
                for x in range(2):
                    e = 2 * q + x
                    for j in range(FB):
                        dve.wait_ge(silu_done, e * FB + (j + 1))
                        TT(hh[:, j % 2, :], sil[:, j % 2, :], ps[CAP:2 * CAP, j % 2, :], ALU.mult).then_inc(hh_ready, 1)
                        dve.wait_ge(hh_turned, e * FB + (j + 1))
                        nc.vector.tensor_copy(hhT[:, j % 2, :, :], ps[:, 2, (j % 2) * 2 * P:(j % 2 + 1) * 2 * P].rearrange(
                            "p (i s) -> p i s", i=4)).then_inc(hhT_ready, 1)
                    dve.wait_ge(y_step, e * (2 * FB) + 2 * FB)
                    for row in range(2):
                        r = slice(CAP * row, CAP * row + CAP)
                        nc.vector.tensor_copy(Y[r, row ^ x, :], ps[r, 3, :]).then_inc(ye_ready, 1)
                if not last:
                    gathered(q + 2)
                for a in range(NT):
                    for half in range(2):
                        dve.wait_ge(sc_full, q * 8 + (2 * a + half + 1))
                        dst = xs[:, a, half * 512:(half + 1) * 512]
                        TT(dst, dst, ps[:, 4 + 2 * (a % 2) + half, :], ALU.add).then_inc(sc_added, 1)
                    if last and a >= 1:
                        tile_root(dve, link, "fin", a - 1)
                dve.wait_ge(sc_added, q * 8 + 8)

            def final_gain(a):
                dve.wait_ge(norms["fin"]["evA"], a + 1)
                if a == 0:
                    dve.wait_ge(ld_gf, 16)
                TT(hT_out(a), hn[:, a, :], gf, ALU.mult).then_inc(norms["fin"]["scaled"], 1)

            gather_table(0)
            gathered(1)
            with dve.Fori(0, NE // 2 - 1) as q:
                expert_pair(q, False)
            expert_pair(NE // 2 - 1, True)
            final_gain(0)
            tile_root(dve, link, "fin", NT - 1)
            for a in range(1, NT):
                final_gain(a)


_INS = ["x", "mem", "w_in", "filt_w1", "filt_w2", "filt_w3", "w_up_hy", "w_up_attn", "w_gate", "w_out", "w_q_x",
        "w_kv_mem", "w_o_x", "w_router", "w_e_gate", "w_e_up", "w_e_down", "ln_f_g"]
_VECTORS = ["ln_mix_g", "ln_x_g", "ln_mem_g", "ln_moe_g", "b_gate", "hy_conv_b", "hy_skip"]
_FILT_VECTORS = ["filt_b1", "filt_freq1", "filt_b2", "filt_freq2"]


def _constants():
    import math

    import numpy as np
    f = np.float32
    m, a = np.arange(P)[:, None], np.arange(NT)[None, :]
    t = 4 * m + a
    flat = t.T.reshape(-1)
    c = {"ident": np.eye(P, dtype=f)}
    tl = np.linspace(0.0, 1.0, SEQ, dtype=f)
    grid = (f(2.0 * math.pi) * np.arange(SEQ, dtype=f) / f(SEQ)).astype(f)
    bands = np.linspace(1e-4, 15, 16, dtype=f)
    arg = (bands[None, :] * grid[:, None]).astype(f)
    emb = np.concatenate([tl[:, None], np.cos(arg), -np.sin(arg)], axis=1).astype(f)
    c["embT"] = emb[flat].T
    deltas = np.linspace(math.log(1e-2) / 1.5, math.log(1e-2) / 0.3, HW, dtype=f)
    c["decay"] = np.exp(-tl[:, None] * np.abs(deltas)[None, :]).astype(f)[t]
    N, H = 2 * SEQ, SEQ // 2
    fr = np.arange(H)
    ang = 2 * np.pi * ((t[:, :, None] * fr) % N) / N
    quarter = 2 * np.pi * ((t * H) % N) / N
    even = (t % 2 == 0)
    co, si = np.cos(ang), np.sin(ang)
    sk = si[:, [0, 2], :P].copy()
    sk[:, :, 0] = 0.0
    si[:, :, 0] = np.where(even, np.cos(quarter), np.sin(quarter))
    c["dftc"], c["dfts"], c["dftsk"] = co, si, sk
    ia = 2 * np.pi * ((fr[:, None] * flat) % N) / N
    ic, isn = np.cos(ia) * 2 / N, np.sin(ia) * 2 / N
    ic[0] = 1.0 / N
    q = 2 * np.pi * ((flat * H) % N) / N
    isn[0] = np.where(flat % 2 == 0, -0.5 * np.cos(q), 0.5 * np.sin(q)) * 2 / N
    c["idftc"] = ic.reshape(2, P, SEQ).transpose(1, 0, 2)
    c["idfts"] = isn.reshape(2, P, SEQ).transpose(1, 0, 2)
    inv = (f(10000.0) ** (-np.arange(0, 64, 2, dtype=f) / f(64))).astype(f)
    ra = (t.astype(f)[:, :, None] * inv).astype(f)
    c["rcos"] = np.concatenate([np.cos(ra), np.cos(ra)], axis=2)
    c["rsin"] = np.concatenate([-np.sin(ra), np.sin(ra)], axis=2)
    ok0 = np.abs(t[:, :, None] - flat) <= 64
    rel = np.abs(np.arange(P)[:, None] - np.arange(P)[None, :])
    ok1 = np.repeat((rel <= 64)[:, None, :], NT, 1)
    ok2 = np.repeat((rel % 4 == 0)[:, None, :], NT, 1)
    c["mask"] = np.where(np.concatenate([ok0, ok1, ok2], axis=2), 0.0, -1e30)
    c["slot_no"] = np.repeat(np.arange(1, CAP + 1)[None, :], P, 0)
    c["count"] = np.concatenate([np.triu(np.ones((P, P))), np.ones((P, P))], axis=1)
    c["sum4"] = np.concatenate([np.eye(NE), np.zeros((32 - NE, NE))] * 4)
    return {k: np.ascontiguousarray(v.astype(f)) for k, v in c.items()}


_CONSTS = ["ident", "embT", "decay", "dftc", "dfts", "dftsk", "idftc", "idfts", "rcos", "rsin", "mask", "slot_no",
           "count", "sum4"]


def kernel(**inputs):
    import numpy as _np
    import concourse.bacc as _bacc
    from concourse import mybir as _mybir
    from concourse.bass_utils import run_bass_kernel_spmd as _run

    nc = _bacc.Bacc("TRN2", target_bir_lowering=False, num_devices=1)
    arrays, args = {}, []
    for name in _INS:
        arrays[f"in_{name}_dram"] = _np.ascontiguousarray(inputs[name])
    arrays["in_vectors_dram"] = _np.concatenate([inputs[n].reshape(-1, P) for n in _VECTORS])
    arrays["in_taps_dram"] = _np.ascontiguousarray(inputs["hy_conv_w"].reshape(-1, P))
    arrays["in_filt_vectors_dram"] = _np.stack([inputs[n] for n in _FILT_VECTORS], axis=1)
    consts = _constants()
    for name in _CONSTS:
        arrays[f"c_{name}_dram"] = consts[name]
    for name, a in arrays.items():
        args.append(nc.dram_tensor(name, a.shape, _mybir.dt.from_np(a.dtype), kind="ExternalInput").ap())
    args.append(nc.dram_tensor("out_0_dram", (1, SEQ, D), F32, kind="ExternalOutput").ap())
    encoder_block(nc, *args)
    r = _run(nc, [arrays], core_ids=[0])
    return r.results[0]["out_0_dram"]
```
